# Optimizing a Trainium2 kernel written in Bass

```python
import jax
import jax.numpy as jnp
from jax import lax
import numpy as np

D_MODEL = 1024
BATCH = 1
SEQ = 512
DEPTH = 2

GRID_W = 64
CTX_LEN = 256
N_EVEN = (DEPTH + 1) // 2
N_ODD = DEPTH // 2
EPS = 1e-6
ROPE_BASE = 10000.0

RET_HEADS = 4
RET_DK = 128
RET_DV = 128
RET_CHUNK = 128
RET_QK = RET_HEADS * RET_DK
RET_VW = RET_HEADS * RET_DV
LRU_WIDTH = 512
LRU_BLOCKS = 8
LRU_BLOCK = LRU_WIDTH // LRU_BLOCKS
LRU_CONV = 4
LRU_C = 8.0
AB_SPLITS = (RET_QK, 2 * RET_QK, 2 * RET_QK + RET_VW, 2 * RET_QK + 2 * RET_VW,
             2 * RET_QK + 2 * RET_VW + LRU_WIDTH)
AB_IN = 2 * RET_QK + 2 * RET_VW + 2 * LRU_WIDTH
AB_MIX = RET_VW + LRU_WIDTH
MLA_HEADS = 16
MLA_NOPE = 64
MLA_ROPE = 32
MLA_V = 64
MLA_Q_RANK = 384
MLA_KV_RANK = 256
MLA_IN = MLA_Q_RANK + MLA_KV_RANK + MLA_ROPE
MLA_Q_BLOCK = 128
MLA_SCALE = (MLA_NOPE + MLA_ROPE) ** -0.5
MOE_GROUPS = 4
MOE_PER_GROUP = 8
MOE_EXPERTS = MOE_GROUPS * MOE_PER_GROUP
MOE_TOPK = 2
MOE_HIDDEN = 512
MOE_BLOCK = 128

kernel_name = 'hybrid_retention_rglru_mla_hmoe_dit'

def rmsnorm(x, g):
    xf = x.astype(jnp.float32)
    y = xf * lax.rsqrt(jnp.mean(xf * xf, axis=-1, keepdims=True) + EPS)
    return (y * g.astype(jnp.float32)).astype(x.dtype)

def modulate(h, shift, scale):
    return h * (1.0 + scale) + shift

def rotate(x, cos, sin):
    x1, x2 = jnp.split(x, 2, axis=-1)
    return jnp.concatenate([x1 * cos - x2 * sin, x1 * sin + x2 * cos], axis=-1).astype(x.dtype)

def to_heads(t, d):
    b, n, _ = t.shape
    return t.reshape(b, n, RET_HEADS, d).transpose(0, 2, 1, 3)

def from_heads(t):
    b, h, n, d = t.shape
    return t.transpose(0, 2, 1, 3).reshape(b, n, h * d)

def head_rms(y):
    return y * lax.rsqrt(jnp.mean(y * y, axis=-1, keepdims=True) + EPS)

def retention_dir(q, k, v, log_gamma, state0, want_out):
    b, h, n, dk = q.shape
    dv = v.shape[-1]
    nc = n // RET_CHUNK
    qc = q.reshape(b, h, nc, RET_CHUNK, dk)
    kc = k.reshape(b, h, nc, RET_CHUNK, dk)
    vc = v.reshape(b, h, nc, RET_CHUNK, dv)
    j = jnp.arange(RET_CHUNK, dtype=jnp.float32)
    lg = log_gamma[:, None]
    zeta = jnp.exp(lg * (RET_CHUNK - 1.0 - j))
    u = jnp.einsum('bhncd,bhnce->bhnde', kc, vc * zeta[None, :, None, :, None])
    chunk_decay = jnp.exp(log_gamma * RET_CHUNK)[None, :, None, None]

    def step(s, u_n):
        return chunk_decay * s + u_n, (s if want_out else None)

    s_final, s_in = lax.scan(step, state0, jnp.moveaxis(u, 2, 0))
    if not want_out:
        return None, s_final
    s_in = jnp.moveaxis(s_in, 0, 2)
    xi = jnp.exp(lg * (j + 1.0))
    inter = jnp.einsum('bhncd,bhnde->bhnce', qc, s_in) * xi[None, :, None, :, None]
    diff = j[:, None] - j[None, :]
    dmat = jnp.where(diff >= 0, jnp.exp(log_gamma[:, None, None] * jnp.maximum(diff, 0.0)), 0.0)
    scores = jnp.einsum('bhncd,bhnmd->bhncm', qc, kc) * dmat[None, :, None]
    intra = jnp.einsum('bhncm,bhnme->bhnce', scores, vc)
    return (intra + inter).reshape(b, h, n, dv), s_final

def retention_bidir(q_c, k_c, v_c, q_l, k_l, v_l, decay_logit, want_ctx):
    b, h, _, dk = q_l.shape
    zero = jnp.zeros((b, h, dk, v_l.shape[-1]), jnp.float32)
    out_c, out_l = None, None
    for d in range(2):
        lg = jax.nn.log_sigmoid(decay_logit[d].astype(jnp.float32))
        f = (lambda t: jnp.flip(t, axis=2)) if d == 1 else (lambda t: t)
        oc, s_ctx = retention_dir(f(q_c), f(k_c), f(v_c), lg, zero, want_ctx)
        ol, _ = retention_dir(f(q_l), f(k_l), f(v_l), lg, s_ctx, True)
        out_l = f(ol) if out_l is None else out_l + f(ol)
        if want_ctx:
            out_c = f(oc) if out_c is None else out_c + f(oc)
    return out_c, out_l

def centred_dwconv(x, w, bias):
    kw = w.shape[0]
    n = x.shape[1]
    xp = jnp.pad(x, ((0, 0), (kw // 2, (kw - 1) // 2), (0, 0)))
    y = xp[:, 0:n] * w[0]
    for t in range(1, kw):
        y = y + xp[:, t:t + n] * w[t]
    return y + bias

def rglru_coeffs(x, gate_w, gate_b, lam):
    b, n, w = x.shape
    xb = x.reshape(b, n, LRU_BLOCKS, LRU_BLOCK)
    gates = jnp.einsum('bnki,gkij->gbnkj', xb, gate_w).reshape(2, b, n, w) + gate_b[:, None, None, :]
    r = jax.nn.sigmoid(gates[0])
    i = jax.nn.sigmoid(gates[1])
    log_a = -LRU_C * r * jax.nn.softplus(-lam.astype(jnp.float32))
    a = jnp.exp(log_a)
    bterm = jnp.sqrt(-jnp.expm1(2.0 * log_a)) * (i * x)
    return a, bterm

def linear_scan(a, bterm, h0):
    def comb(left, right):
        return left[0] * right[0], right[0] * left[1] + right[1]
    a_cum, h = lax.associative_scan(comb, (a, bterm), axis=1)
    return h + a_cum * h0[:, None, :]

def rglru_bidir(xc, xl, gate_w, gate_b, lam, want_ctx):
    b, _, w = xl.shape
    zero = jnp.zeros((b, w), jnp.float32)
    out_c, out_l = None, None
    for d in range(2):
        f = (lambda t: jnp.flip(t, axis=1)) if d == 1 else (lambda t: t)
        a, bt = rglru_coeffs(f(xc), gate_w[d], gate_b[d], lam[d])
        h_ctx = linear_scan(a, bt, zero)
        a, bt = rglru_coeffs(f(xl), gate_w[d], gate_b[d], lam[d])
        h_lat = f(linear_scan(a, bt, h_ctx[:, -1]))
        out_l = h_lat if out_l is None else out_l + h_lat
        if want_ctx:
            out_c = f(h_ctx) if out_c is None else out_c + f(h_ctx)
    return out_c, out_l

def ab_mixer(hc, hl, w_in, w_out, decay_logit, conv_w, conv_b, gate_w, gate_b, lam, ret_cs, want_ctx):
    cos, sin = ret_cs
    pc = jnp.split((hc @ w_in).astype(jnp.float32), AB_SPLITS, axis=-1)
    pl = jnp.split((hl @ w_in).astype(jnp.float32), AB_SPLITS, axis=-1)
    k_scale = RET_DK ** -0.5
    q_c = to_heads(pc[0], RET_DK)
    k_c = to_heads(pc[1], RET_DK) * k_scale
    v_c = to_heads(pc[2], RET_DV)
    q_l = rotate(to_heads(pl[0], RET_DK), cos, sin)
    k_l = rotate(to_heads(pl[1], RET_DK), cos, sin) * k_scale
    v_l = to_heads(pl[2], RET_DV)
    rc, rl = retention_bidir(q_c, k_c, v_c, q_l, k_l, v_l, decay_logit, want_ctx)
    uc = centred_dwconv(pc[4], conv_w, conv_b)
    ul = centred_dwconv(pl[4], conv_w, conv_b)
    lc, ll = rglru_bidir(uc, ul, gate_w, gate_b, lam, want_ctx)

    def merge(r, g, hrec, y, dtype):
        ret = from_heads(head_rms(r)) * jax.nn.silu(g)
        rec = hrec * jax.nn.gelu(y)
        return (jnp.concatenate([ret, rec], axis=-1) @ w_out).astype(dtype)

    ol = merge(rl, pl[3], ll, pl[5], hl.dtype)
    oc = merge(rc, pc[3], lc, pc[5], hc.dtype) if want_ctx else None
    return oc, ol

def mla_project(h, w_in, q_g, kv_g, w_uq, w_ukv, cs):
    b, n, _ = h.shape
    p = h @ w_in
    cq, ckv, kr = jnp.split(p, [MLA_Q_RANK, MLA_Q_RANK + MLA_KV_RANK], axis=-1)
    q = (rmsnorm(cq, q_g) @ w_uq).reshape(b, n, MLA_HEADS, MLA_NOPE + MLA_ROPE)
    kv = (rmsnorm(ckv, kv_g) @ w_ukv).reshape(b, n, MLA_HEADS, MLA_NOPE + MLA_V)
    q_nope, q_rope = jnp.split(q, [MLA_NOPE], axis=-1)
    k_nope, v = jnp.split(kv, [MLA_NOPE], axis=-1)
    if cs is not None:
        cos, sin = cs
        q_rope = rotate(q_rope, cos[:, None, :], sin[:, None, :])
        kr = rotate(kr, cos, sin)
    k = jnp.concatenate([k_nope, jnp.broadcast_to(kr[:, :, None, :], (b, n, MLA_HEADS, MLA_ROPE))], axis=-1)
    q = jnp.concatenate([q_nope, q_rope], axis=-1)
    return q.astype(jnp.float32), k.astype(jnp.float32), v.astype(jnp.float32)

def attend(q, k, v):
    s = jnp.einsum('bqhd,bkhd->bhqk', q, k) * MLA_SCALE
    p = jax.nn.softmax(s, axis=-1)
    return jnp.einsum('bhqk,bkhd->bqhd', p, v)

def mla_mixer(hc, hl, w_in, q_g, kv_g, w_uq, w_ukv, w_out, mla_cs, want_ctx):
    qc, kc, vc = mla_project(hc, w_in, q_g, kv_g, w_uq, w_ukv, None)
    ql, kl, vl = mla_project(hl, w_in, q_g, kv_g, w_uq, w_ukv, mla_cs)
    b, n = hl.shape[:2]
    k_all = jnp.concatenate([kc, kl], axis=1)
    v_all = jnp.concatenate([vc, vl], axis=1)
    nqb = n // MLA_Q_BLOCK
    qb = ql.reshape(b, nqb, MLA_Q_BLOCK, MLA_HEADS, MLA_NOPE + MLA_ROPE).transpose(1, 0, 2, 3, 4)
    ob = lax.map(lambda qq: attend(qq, k_all, v_all), qb)
    ol = (ob.transpose(1, 0, 2, 3, 4).reshape(b, n, MLA_HEADS * MLA_V) @ w_out).astype(hl.dtype)
    if not want_ctx:
        return None, ol
    oc = (attend(qc, kc, vc).reshape(b, hc.shape[1], MLA_HEADS * MLA_V) @ w_out).astype(hc.dtype)
    return oc, ol

def hier_moe(h, group_w, group_b, expert_w, expert_b, w_gate, w_up, w_down):
    t_count, d = h.shape
    hf = h.astype(jnp.float32)
    group_p = jax.nn.softmax(hf @ group_w + group_b, axis=-1)
    g_top, g_sel = lax.top_k(group_p, 1)
    e_logits = (hf @ expert_w + expert_b).reshape(t_count, MOE_GROUPS, MOE_PER_GROUP)
    within = jnp.take_along_axis(e_logits, g_sel[:, :, None], axis=1)[:, 0]
    e_p = jax.nn.softmax(within, axis=-1)
    top_p, top_i = lax.top_k(e_p, MOE_TOPK)
    top_p = top_p / jnp.sum(top_p, axis=-1, keepdims=True)
    weights = (g_top * top_p).reshape(-1)
    e_flat = (g_sel * MOE_PER_GROUP + top_i).reshape(-1)
    tok = jnp.repeat(jnp.arange(t_count, dtype=jnp.int32), MOE_TOPK)
    n_assign = t_count * MOE_TOPK
    order = jnp.argsort(e_flat)
    e_sorted = e_flat[order]
    counts = jnp.zeros((MOE_EXPERTS,), jnp.int32).at[e_flat].add(1)
    padded = (counts + MOE_BLOCK - 1) // MOE_BLOCK * MOE_BLOCK
    start = jnp.cumsum(counts) - counts
    pend = jnp.cumsum(padded)
    pstart = pend - padded
    dest = pstart[e_sorted] + (jnp.arange(n_assign, dtype=jnp.int32) - start[e_sorted])
    n_rows = (n_assign + MOE_EXPERTS * (MOE_BLOCK - 1) + MOE_BLOCK - 1) // MOE_BLOCK * MOE_BLOCK
    n_blocks = n_rows // MOE_BLOCK
    row_tok = jnp.zeros((n_rows,), jnp.int32).at[dest].set(tok[order])
    row_w = jnp.zeros((n_rows,), jnp.float32).at[dest].set(weights[order])
    block_e = jnp.minimum(jnp.searchsorted(pend, jnp.arange(n_blocks, dtype=jnp.int32) * MOE_BLOCK,
                                           side='right'), MOE_EXPERTS - 1)
    xin = h[row_tok].reshape(n_blocks, MOE_BLOCK, d)

    def expert_block(args):
        xb, e = args
        return (jax.nn.silu(xb @ w_gate[e]) * (xb @ w_up[e])) @ w_down[e]

    yb = lax.map(expert_block, (xin, block_e)).reshape(n_rows, d)
    y = jnp.zeros((t_count, d), jnp.float32).at[row_tok].add(yb * row_w[:, None])
    return y.astype(h.dtype)

def setup_inputs(seed: int = 0) -> dict:
    key = jax.random.key(seed)
    keys = iter(jax.random.split(key, 40))

    def nrm(shape, scale):
        return jax.random.normal(next(keys), shape, jnp.float32) * scale

    dm = D_MODEL
    decay_base = jnp.asarray(np.log(2.0 ** (5 + np.arange(RET_HEADS)) - 1.0), jnp.float32)
    a_init = jax.random.uniform(next(keys), (N_EVEN, 2, LRU_WIDTH), jnp.float32, 0.9, 0.999) ** (1.0 / LRU_C)
    return {
        'x': nrm((BATCH, SEQ, dm), 1.0),
        'c': nrm((BATCH, dm), 1.0),
        'ctx': nrm((BATCH, CTX_LEN, dm), 1.0),
        'c_ctx': nrm((dm,), 1.0),
        'ada_w': nrm((DEPTH, dm, 6 * dm), 0.5 * dm ** -0.5),
        'ada_b': nrm((DEPTH, 6 * dm), 0.01),
        'norm_g': 1.0 + nrm((DEPTH, 2, dm), 0.02),
        'ab_w_in': nrm((N_EVEN, dm, AB_IN), dm ** -0.5),
        'ab_w_out': nrm((N_EVEN, AB_MIX, dm), AB_MIX ** -0.5),
        'ret_decay_logit': decay_base + nrm((N_EVEN, 2, RET_HEADS), 0.1),
        'lru_conv_w': nrm((N_EVEN, LRU_CONV, LRU_WIDTH), LRU_CONV ** -0.5),
        'lru_conv_b': nrm((N_EVEN, LRU_WIDTH), 0.01),
        'lru_gate_w': nrm((N_EVEN, 2, 2, LRU_BLOCKS, LRU_BLOCK, LRU_BLOCK), LRU_BLOCK ** -0.5),
        'lru_gate_b': nrm((N_EVEN, 2, 2, LRU_WIDTH), 0.01),
        'lru_lambda': jnp.log(a_init) - jnp.log1p(-a_init),
        'mla_w_in': nrm((N_ODD, dm, MLA_IN), dm ** -0.5),
        'mla_q_norm_g': 1.0 + nrm((N_ODD, MLA_Q_RANK), 0.02),
        'mla_kv_norm_g': 1.0 + nrm((N_ODD, MLA_KV_RANK), 0.02),
        'mla_w_uq': nrm((N_ODD, MLA_Q_RANK, MLA_HEADS * (MLA_NOPE + MLA_ROPE)), MLA_Q_RANK ** -0.5),
        'mla_w_ukv': nrm((N_ODD, MLA_KV_RANK, MLA_HEADS * (MLA_NOPE + MLA_V)), MLA_KV_RANK ** -0.5),
        'mla_w_out': nrm((N_ODD, MLA_HEADS * MLA_V, dm), (MLA_HEADS * MLA_V) ** -0.5),
        'moe_group_w': nrm((DEPTH, dm, MOE_GROUPS), dm ** -0.5),
        'moe_group_b': nrm((DEPTH, MOE_GROUPS), 0.01),
        'moe_expert_w': nrm((DEPTH, dm, MOE_EXPERTS), dm ** -0.5),
        'moe_expert_b': nrm((DEPTH, MOE_EXPERTS), 0.01),
        'moe_w_gate': nrm((DEPTH, MOE_EXPERTS, dm, MOE_HIDDEN), dm ** -0.5),
        'moe_w_up': nrm((DEPTH, MOE_EXPERTS, dm, MOE_HIDDEN), dm ** -0.5),
        'moe_w_down': nrm((DEPTH, MOE_EXPERTS, MOE_HIDDEN, dm), MOE_HIDDEN ** -0.5),
        'final_norm_g': 1.0 + nrm((dm,), 0.02),
    }

def reference(x, c, ctx, c_ctx, ada_w, ada_b, norm_g, ab_w_in, ab_w_out, ret_decay_logit,
              lru_conv_w, lru_conv_b, lru_gate_w, lru_gate_b, lru_lambda, mla_w_in, mla_q_norm_g,
              mla_kv_norm_g, mla_w_uq, mla_w_ukv, mla_w_out, moe_group_w, moe_group_b, moe_expert_w,
              moe_expert_b, moe_w_gate, moe_w_up, moe_w_down, final_norm_g):
    b, n, _ = x.shape
    ctx_len = ctx.shape[1]
    rows = n // GRID_W
    t = jnp.arange(n, dtype=jnp.float32)
    inv1 = ROPE_BASE ** (-jnp.arange(0, RET_DK, 2, dtype=jnp.float32) / RET_DK)
    ang1 = t[:, None] * inv1[None, :]
    ret_cs = (jnp.cos(ang1), jnp.sin(ang1))
    r_pos = jnp.repeat(jnp.arange(rows, dtype=jnp.float32), GRID_W)
    c_pos = jnp.tile(jnp.arange(GRID_W, dtype=jnp.float32), rows)
    ax_dim = MLA_ROPE // 2
    inv2 = ROPE_BASE ** (-jnp.arange(0, ax_dim, 2, dtype=jnp.float32) / ax_dim)
    ang2 = jnp.concatenate([r_pos[:, None] * inv2[None, :], c_pos[:, None] * inv2[None, :]], axis=-1)
    mla_cs = (jnp.cos(ang2), jnp.sin(ang2))

    xl, xc = x, ctx
    s_lat = jax.nn.silu(c)
    s_ctx = jax.nn.silu(c_ctx)
    for layer in range(DEPTH):
        want_ctx = layer != DEPTH - 1
        mod_l = jnp.split((s_lat @ ada_w[layer] + ada_b[layer])[:, None, :], 6, axis=-1)
        mod_c = jnp.split((s_ctx @ ada_w[layer] + ada_b[layer])[None, None, :], 6, axis=-1)
        hl = modulate(rmsnorm(xl, norm_g[layer, 0]), mod_l[0], mod_l[1])
        hc = modulate(rmsnorm(xc, norm_g[layer, 0]), mod_c[0], mod_c[1])
        i = layer // 2
        if layer % 2 == 0:
            oc, ol = ab_mixer(hc, hl, ab_w_in[i], ab_w_out[i], ret_decay_logit[i], lru_conv_w[i],
                              lru_conv_b[i], lru_gate_w[i], lru_gate_b[i], lru_lambda[i], ret_cs, want_ctx)
        else:
            oc, ol = mla_mixer(hc, hl, mla_w_in[i], mla_q_norm_g[i], mla_kv_norm_g[i], mla_w_uq[i],
                               mla_w_ukv[i], mla_w_out[i], mla_cs, want_ctx)
        xl = xl + mod_l[2] * ol
        hl = modulate(rmsnorm(xl, norm_g[layer, 1]), mod_l[3], mod_l[4])
        moe_params = (moe_group_w[layer], moe_group_b[layer], moe_expert_w[layer], moe_expert_b[layer],
                      moe_w_gate[layer], moe_w_up[layer], moe_w_down[layer])
        if want_ctx:
            xc = xc + mod_c[2] * oc
            hc = modulate(rmsnorm(xc, norm_g[layer, 1]), mod_c[3], mod_c[4])
            tokens = jnp.concatenate([hc.reshape(b * ctx_len, -1), hl.reshape(b * n, -1)], axis=0)
            y = hier_moe(tokens, *moe_params)
            xc = xc + mod_c[5] * y[:b * ctx_len].reshape(b, ctx_len, -1)
            xl = xl + mod_l[5] * y[b * ctx_len:].reshape(b, n, -1)
        else:
            y = hier_moe(hl.reshape(b * n, -1), *moe_params)
            xl = xl + mod_l[5] * y.reshape(b, n, -1)
    return rmsnorm(xl, final_norm_g)


_drawn_inputs = setup_inputs


def setup_inputs(seed=0):
    import zlib

    import numpy as np

    out = dict(_drawn_inputs(seed))
    spreads = {}
    factors = {'norm_g': 2.804,
     'lru_conv_b': 2.976,
     'lru_gate_b': 8.0,
     'mla_q_norm_g': 8.0,
     'mla_kv_norm_g': 8.0,
     'moe_group_b': 7.323,
     'moe_expert_b': 6.611,
     'final_norm_g': 2.734}
    for name, (base, spread) in spreads.items():
        noise = np.random.default_rng([zlib.crc32(name.encode()), seed]).standard_normal(out[name].shape)
        drawn = base * np.exp(spread * noise) if base else spread * noise
        out[name] = jnp.asarray(drawn.astype(out[name].dtype))
    for name, factor in factors.items():
        out[name] = (out[name] * factor).astype(out[name].dtype)
    return out
```

```python
import math
from contextlib import ExitStack

import numpy as np

import concourse.bass as bass
from concourse import mybir

F32 = mybir.dt.float32
I32 = mybir.dt.int32
ALU = mybir.AluOpType
ACT = mybir.ActivationFunctionType
AX = mybir.AxisListType.X

P = 128
DM = 1024
SEQ = 512
CTX = 256
TOK = CTX + SEQ
DEPTH = 2
KD = DM // P
CT = CTX // P
NT = TOK // P
EPS = 1e-6
ROPE_BASE = 10000.0
GRID_W = 64

RH, RD = 4, 128
LW = 512
LT = LW // P
LB = 64
CONV = 4
LRU_C = 8.0
QK = RH * RD

AH, NOPE, ROPE, VD = 16, 64, 32, 64
QR, KVR = 384, 256
MLA_SCALE = (NOPE + ROPE) ** -0.5

G, EPG = 4, 8
E = G * EPG
HID = 512
HT_N = HID // P
CAP = P
ROUTES = G + E


class Chain:

    def __init__(self, eng, sem, base=0):
        self.eng, self.sem, self.n = eng, sem, base

    def __call__(self, ins):
        self.n += 1
        ins.then_inc(self.sem, 1)
        self.eng.wait_ge(self.sem, self.n)


class Scope:

    def __init__(self, nc, tag):
        self.nc, self.tag, self.stack, self.sems = nc, tag, ExitStack(), []

    def __enter__(self):
        self.stack.__enter__()
        return self

    def __exit__(self, *a):
        self.stack.__exit__(*a)
        if self.sems and a[0] is None:
            self.nc.clear_and_free_semaphores(self.sems)
            self.nc.all_engine_barrier()

    def sb(self, name, shape, dt=F32):
        return self.stack.enter_context(self.nc.sbuf_tensor(f"{self.tag}_{name}", shape, dt))

    def ps(self, name, shape, dt=F32):
        return self.stack.enter_context(self.nc.psum_tensor(f"{self.tag}_{name}", shape, dt))

    def sem(self, name):
        self.sems.append(self.nc.alloc_semaphore(f"{self.tag}_{name}"))
        return self.sems[-1]

    def block(self):
        return self.stack.enter_context(self.nc.Block())


def refined_rsqrt(nc, link, rstd, root, ms, tmp):
    V = nc.vector
    link(V.reciprocal(rstd, root))
    link(V.tensor_scalar(ms, ms, 1.0 / DM, EPS, ALU.mult, ALU.add))
    link(V.tensor_tensor(tmp, rstd, rstd, ALU.mult))
    link(V.tensor_tensor(tmp, tmp, ms, ALU.mult))
    link(V.tensor_scalar(tmp, tmp, -0.5, 1.5, ALU.mult, ALU.add))
    link(V.tensor_tensor(rstd, rstd, tmp, ALU.mult))


def constants(nc, c):
    with Scope(nc, "const") as s:
        zeroed, made = s.sem("zeroed"), s.sem("made")
        block = s.block()

        @block.gpsimd
        def _(pool):
            nc.gpsimd.memset(c.ident[:], 0.0).then_inc(zeroed, 1)
            nc.gpsimd.memset(c.ones[:], 1.0).then_inc(zeroed, 1)
            pool.wait_ge(zeroed, 2)
            nc.gpsimd.affine_select(out=c.ident[:], in_=c.ident[:], compare_op=ALU.not_equal, fill=1.0,
                                    base=0, pattern=[[-1, P]], channel_multiplier=1).then_inc(made, 1)
            nc.gpsimd.affine_select(out=c.before[:], in_=c.ones[:], compare_op=ALU.is_gt, fill=0.0,
                                    base=0, pattern=[[1, P]], channel_multiplier=-1).then_inc(made, 1)
            pool.wait_ge(made, 2)


def clear_further_rows(nc, c):
    with Scope(nc, "clear") as s:
        zeroed = s.sem("zeroed")
        block = s.block()

        @block.gpsimd
        def _(pool):
            nc.gpsimd.memset(c.zero_row[:], 0.0).then_inc(zeroed, 1)

        @block.sync
        def _(sp):
            sp.wait_ge(zeroed, 1)
            for b in range(2 * NT - 1):
                sp.dma_start(c.ys[(E + b) * P:(E + b + 1) * P, :], c.zero_row[:]).then_inc(c.rows_clear, 16)
            sp.wait_ge(c.rows_clear, 16 * (2 * NT - 1))


def adaln(nc, c, a):
    NB = 6 * DM // 512
    R = NB // 4
    LOADS = DEPTH * R
    with Scope(nc, "ada") as s:
        w = [s.sb(f"w{i}", [P, KD, 4 * 512]) for i in range(2)]
        craw = s.sb("craw", [P, 2, KD])
        sT = s.sb("sT", [P, KD, 32])
        bias = s.sb("bias", [P, LOADS, 512])
        mod = s.sb("mod", [P, LOADS, 512])
        ps = [s.ps(f"ps{i}", [P, 512]) for i in range(2)]
        w_ready = [s.sem(f"w_ready{i}") for i in range(2)]
        c_ready, b_ready, zeroed, silu_done = (s.sem(n) for n in ("c_ready", "b_ready", "zeroed", "silu_done"))
        mm_done, mod_done, stored = (s.sem(n) for n in ("mm_done", "mod_done", "stored"))
        block = s.block()

        @block.sync
        def _(sp):
            for n in range(LOADS):
                l, r = divmod(n, R)
                if n >= 2:
                    sp.wait_ge(mm_done, n - 1)
                sp.dma_start(w[n % 2][:], a["ada_w"][l, :, r * 2048:(r + 1) * 2048]
                             .rearrange("(p k) n -> p k n", k=KD)).then_inc(w_ready[n % 2], 16)
            sp.wait_ge(mod_done, LOADS)
            for st in range(2):
                for l in range(DEPTH):
                    sp.dma_start(c.mods[st, l].rearrange("(r j n) -> j r n", j=4, n=512),
                                 mod[st:P:32, l * R:(l + 1) * R, :]).then_inc(stored, 16)
            sp.wait_ge(stored, 16 * 2 * DEPTH)

        @block.gpsimd
        def _(pool):
            nc.gpsimd.memset(bias[:], 0.0).then_inc(zeroed, 1)
            nc.gpsimd.memset(sT[:], 0.0).then_inc(zeroed, 1)
            pool.wait_ge(c.x_ready, 16 * NT)

        @block.scalar
        def _(act):
            act.dma_start(craw[:, 0, :], a["c"][0].rearrange("(p k) -> p k", k=KD)).then_inc(c_ready, 16)
            act.dma_start(craw[:, 1, :], a["c_ctx"].rearrange("(p k) -> p k", k=KD)).then_inc(c_ready, 16)
            for t in range(CT):
                act.dma_start(c.X[:, t, :], a["ctx"][0, t * P:(t + 1) * P, :]).then_inc(c.x_ready, 16)
            for t in range(CT, NT):
                act.dma_start(c.X[:, t, :], a["x"][0, (t - CT) * P:(t - CT + 1) * P, :]).then_inc(c.x_ready, 16)
            act.wait_ge(zeroed, 2)
            for st in range(2):
                for l in range(DEPTH):
                    act.dma_start(bias[st:P:32, l * R:(l + 1) * R, :],
                                  a["ada_b"][l].rearrange("(r j n) -> j r n", j=4, n=512)).then_inc(b_ready, 16)
            act.wait_ge(c_ready, 32)
            nc.scalar.activation(sT[:, :, 0:2], craw[:].rearrange("p s k -> p k s"), ACT.Silu).then_inc(silu_done, 1)

        @block.tensor
        def _(pe):
            pe.wait_ge(silu_done, 1)
            for n in range(LOADS):
                pe.wait_ge(w_ready[n % 2], 16 * (n // 2 + 1))
                if n >= 2:
                    pe.wait_ge(mod_done, n - 1)
                for k in range(KD):
                    for j in range(4):
                        last = nc.tensor.matmul(ps[n % 2][32 * j:32 * j + 32, :], sT[:, k, :],
                                                w[n % 2][:, k, j * 512:(j + 1) * 512],
                                                start=(k == 0), stop=(k == KD - 1))
                last.then_inc(mm_done, 1)

        @block.vector
        def _(dve):
            dve.wait_ge(b_ready, 16 * 2 * DEPTH)
            for n in range(LOADS):
                dve.wait_ge(mm_done, n + 1)
                nc.vector.tensor_add(mod[:, n, :], ps[n % 2][:], bias[:, n, :]).then_inc(mod_done, 1)


def norm_modulate(nc, c, a, layer, sub, t0, hT, mb, h_out):
    T = NT - t0
    with Scope(nc, f"norm{layer}{sub}") as s:
        g = s.sb("g", [P, DM])
        junk = s.sb("junk", [P, DM])
        h = s.sb("h", [P, T, DM])
        ms = s.sb("ms", [P, T])
        rstd, root, tmp = (s.sb(n, [P, T]) for n in ("rstd", "root", "tmp"))
        eps = s.sb("eps", [P, 1])
        tp = [s.ps(f"tp{i}", [P, 4, P]) for i in range(4)]
        g_ready, m_ready, eps_ready, sq_done, sqrt_done, chain = (
            s.sem(n) for n in ("g_ready", "m_ready", "eps_ready", "sq_done", "sqrt_done", "chain"))
        scaled, h_done, tr_done, ev_act, ev_dve, h_stored = (
            s.sem(n) for n in ("scaled", "h_done", "tr_done", "ev_act", "ev_dve", "h_stored"))
        block = s.block()
        streams = range(1 if t0 else 2)

        @block.sync
        def _(sp):
            sp.dma_start(g[:], a["norm_g"][layer, sub:sub + 1, :].to_broadcast([P, DM])).then_inc(g_ready, 16)
            for st in streams:
                sp.dma_start(mb[:, st].rearrange("p r n -> p (r n)"),
                             c.mods[st, layer:layer + 1, sub * 3 * DM:(sub + 1) * 3 * DM]
                             .to_broadcast([P, 3 * DM])).then_inc(m_ready, 16)
            if h_out is not None:
                for t in range(T):
                    sp.wait_ge(h_done, t + 1)
                    sp.dma_start(h_out[(t0 + t) * P:(t0 + t + 1) * P, :], h[:, t, :]).then_inc(h_stored, 16)
                sp.wait_ge(h_stored, 16 * T)

        @block.scalar
        def _(act):
            for t in range(T):
                nc.scalar.activation(junk[:], c.X[:, t0 + t, :], ACT.Square,
                                     accum_out=ms[:, t:t + 1]).then_inc(sq_done, 1)
                act.wait_ge(sq_done, t + 1)
            act.wait_ge(eps_ready, 1)
            nc.scalar.activation(root[:], ms[:], ACT.Sqrt, scale=1.0 / DM, bias=eps[:]).then_inc(sqrt_done, 1)
            for t in range(T):
                act.wait_ge(tr_done, 2 * t + 1)
                nc.scalar.copy(hT[:, 0:4, t * P:(t + 1) * P], tp[2 * (t % 2)][:]).then_inc(ev_act, 1)

        @block.vector
        def _(dve):
            link = Chain(dve, chain)
            nc.vector.memset(eps[:], EPS).then_inc(eps_ready, 1)
            dve.wait_ge(g_ready, 16)
            dve.wait_ge(m_ready, 16 * len(streams))
            for st in streams:
                link(nc.vector.scalar_tensor_tensor(out=mb[:, st, 1, :], in0=mb[:, st, 1, :], scalar=1.0,
                                                    in1=g[:], op0=ALU.add, op1=ALU.mult))
            dve.wait_ge(sqrt_done, 1)
            refined_rsqrt(nc, link, rstd[:], root[:], ms[:], tmp[:])
            for t in range(T):
                st = 1 if t0 + t < CT else 0
                nc.vector.scalar_tensor_tensor(out=h[:, t, :], in0=c.X[:, t0 + t, :], scalar=rstd[:, t:t + 1],
                                               in1=mb[:, st, 1, :], op0=ALU.mult, op1=ALU.mult).then_inc(scaled, 1)
            for t in range(T):
                dve.wait_ge(tr_done, 2 * t + 2)
                nc.vector.tensor_copy(hT[:, 4:8, t * P:(t + 1) * P], tp[2 * (t % 2) + 1][:]).then_inc(ev_dve, 1)

        @block.gpsimd
        def _(pool):
            for t in range(T):
                st = 1 if t0 + t < CT else 0
                pool.wait_ge(scaled, t + 1)
                nc.gpsimd.tensor_add(h[:, t, :], h[:, t, :], mb[:, st, 0, :]).then_inc(h_done, 1)

        @block.tensor
        def _(pe):
            for t in range(T):
                pe.wait_ge(h_done, t + 1)
                for half in range(2):
                    if t >= 2:
                        pe.wait_ge(ev_dve if half else ev_act, t - 1)
                    for j in range(4):
                        k = 4 * half + j
                        last = nc.tensor.transpose(tp[2 * (t % 2) + half][:, j, :], h[:, t, k * P:(k + 1) * P],
                                                   c.ident[:])
                    last.then_inc(tr_done, 1)


def rms_rows(V, link, rstd, root, ms, tmp, width):
    link(V.reciprocal(rstd, root))
    link(V.tensor_scalar(ms, ms, 1.0 / width, EPS, ALU.mult, ALU.add))
    link(V.tensor_tensor(tmp, rstd, rstd, ALU.mult))
    link(V.tensor_tensor(tmp, tmp, ms, ALU.mult))
    link(V.tensor_scalar(tmp, tmp, -0.5, 1.5, ALU.mult, ALU.add))
    link(V.tensor_tensor(rstd, rstd, tmp, ALU.mult))


PADL, PADR = CONV // 2, (CONV - 1) // 2
U_CTX = PADL
U_LAT = PADL + CTX + PADR + PADL
U_LEN = U_LAT + SEQ + PADR


def ab_project(nc, c, a, hT, rows, u, yT):
    with Scope(nc, "abp") as s:
        S = 3
        w = [s.sb(f"w{i}", [P, KD, 512]) for i in range(S)]
        ps = [s.ps(f"ps{i}", [P, 512]) for i in range(8)]
        w_ready = [s.sem(f"w_ready{i}") for i in range(S)]
        w_free, mm, ev, cleared = (s.sem(n) for n in ("w_free", "mm", "ev", "cleared"))
        block = s.block()
        groups = [(b, t) for b in range(4) for t in range(NT)]
        groups += [(b, (ct, o, n)) for b in (4, 5) for ct in range(LT) for o, n in ((0, CTX), (CTX, SEQ))]

        @block.sync
        def _(sp):
            for b in range(6):
                if b >= S:
                    sp.wait_ge(w_free, b - S + 1)
                sp.dma_start(w[b % S][:], a["ab_w_in"][0, :, b * 512:(b + 1) * 512]
                             .rearrange("(k p) n -> p k n", p=P)).then_inc(w_ready[b % S], 16)

        @block.gpsimd
        def _(pool):
            nc.gpsimd.memset(u[:], 0.0).then_inc(cleared, 1)

        @block.tensor
        def _(pe):
            for i, (b, what) in enumerate(groups):
                if i == 0 or groups[i - 1][0] != b:
                    pe.wait_ge(w_ready[b % S], 16 * (b // S + 1))
                if i >= 8:
                    pe.wait_ge(ev, i - 7)
                for k in range(KD):
                    if b < 4:
                        last = nc.tensor.matmul(ps[i % 8][:], hT[:, k, what * P:(what + 1) * P], w[b % S][:, k, :],
                                                start=(k == 0), stop=(k == KD - 1))
                    else:
                        ct, o, n = what
                        last = nc.tensor.matmul(ps[i % 8][:, 0:n], w[b % S][:, k, ct * P:(ct + 1) * P],
                                                hT[:, k, o:o + n], start=(k == 0), stop=(k == KD - 1))
                last.then_inc(mm, 1)
                if i + 1 == len(groups) or groups[i + 1][0] != b:
                    pe.wait_ge(mm, i + 1)
                    pe.sem_inc(w_free, 1)

        @block.vector
        def _(dve):
            dve.wait_ge(cleared, 1)
            for i, (b, what) in enumerate(groups):
                dve.wait_ge(mm, i + 1)
                if b == 1:
                    nc.vector.tensor_scalar(rows[:, b, what, :], ps[i % 8][:], RD ** -0.5, None, ALU.mult).then_inc(ev, 1)
                elif b < 4:
                    nc.vector.tensor_copy(rows[:, b, what, :], ps[i % 8][:]).then_inc(ev, 1)
                else:
                    ct, o, n = what
                    at = (U_LAT if o else U_CTX) if b == 4 else o
                    nc.vector.tensor_copy((u if b == 4 else yT)[:, ct, at:at + n], ps[i % 8][:, 0:n]).then_inc(ev, 1)


def small_tables(nc, c, a, k):
    NZ = 2 * RH + 2 * LT
    with Scope(nc, "tab") as s:
        z, az, e, q, x2, acc = (s.sb(n, [P, NZ]) for n in ("z", "az", "e", "q", "x2", "acc"))
        col = s.sb("col", [P, 2, RH])
        jrow = s.sb("jrow", [P, 2, RD])
        dist = s.sb("dist", [P, 2, P])
        dm = s.sb("dm", [P, 2, RH, P])
        ready, io, e_in, e_out, chain, lg_ready, xi_done, dm_done, dcols = (
            s.sem(n) for n in ("ready", "io", "e_in", "e_out", "chain", "lg_ready", "xi_done", "dm_done", "dcols"))
        masked = s.sem("masked")
        block = s.block()

        @block.sync
        def _(sp):
            sp.dma_start(z[:, 0:2 * RH], a["ret_decay_logit"].rearrange("o d h -> o (d h)")
                         .to_broadcast([P, 2 * RH])).then_inc(ready, 16)
            for d in range(2):
                sp.dma_start(z[:, 2 * RH + d * LT:2 * RH + (d + 1) * LT],
                             a["lru_lambda"][0, d].rearrange("(c p) -> p c", p=P),
                             allow_slow_non_contiguous=True).then_inc(ready, 16)

        @block.gpsimd
        def _(pool):
            def idx(out, pattern, base, mult):
                nc.gpsimd.iota(out, pattern=pattern, base=base, channel_multiplier=mult,
                               allow_small_or_imprecise_dtypes=True).then_inc(io, 1)

            idx(col[:, 0, :], [[0, RH]], P - 1, -1)
            idx(col[:, 1, :], [[0, RH]], 0, 1)
            idx(jrow[:, 0, :], [[1, RD]], 1, 0)
            idx(jrow[:, 1, :], [[-1, RD]], P, 0)
            idx(dist[:, 0, :], [[1, P]], 0, -1)
            idx(dist[:, 1, :], [[-1, P]], 0, 1)
            pool.wait_ge(dm_done, 2 * RH)
            for d in range(2):
                sign = 1 if d == 0 else -1
                nc.gpsimd.affine_select(out=dm[:, d], in_=dm[:, d], compare_op=ALU.is_ge, fill=0.0, base=0,
                                        pattern=[[0, RH], [sign, P]], channel_multiplier=-sign).then_inc(masked, 1)

        @block.vector
        def _(dve):
            link = Chain(dve, chain)
            V = nc.vector
            dve.wait_ge(ready, 48)
            dve.wait_ge(io, 6)
            link(V.tensor_scalar(z[:], z[:], -1.0, None, ALU.mult))
            link(V.tensor_scalar(az[:], z[:], -1.0, None, ALU.mult))
            link(V.tensor_tensor(az[:], az[:], z[:], ALU.min))
            V.tensor_scalar(z[:], z[:], 0.0, None, ALU.max).then_inc(e_in, 1)
            dve.wait_ge(e_in, 1)
            dve.wait_ge(e_out, 1)
            link(V.tensor_scalar(q[:], e[:], 2.0, None, ALU.add))
            link(V.reciprocal(q[:], q[:]))
            link(V.tensor_tensor(q[:], q[:], e[:], ALU.mult))
            link(V.tensor_tensor(x2[:], q[:], q[:], ALU.mult))
            link(V.tensor_scalar(acc[:], x2[:], 1.0 / 17, 1.0 / 15, ALU.mult, ALU.add))
            for n in (13, 11, 9, 7, 5, 3, 1):
                link(V.tensor_tensor(acc[:], acc[:], x2[:], ALU.mult))
                link(V.tensor_scalar(acc[:], acc[:], 1.0 / n, None, ALU.add))
            link(V.tensor_tensor(acc[:], acc[:], q[:], ALU.mult))
            link(V.scalar_tensor_tensor(out=k.sp[:], in0=acc[:], scalar=2.0, in1=z[:], op0=ALU.mult, op1=ALU.add))
            V.tensor_scalar(k.lg[:], k.sp[:, 0:2 * RH], -1.0, None, ALU.mult).then_inc(lg_ready, 1)
            dve.wait_ge(lg_ready, 1)
            link(V.tensor_scalar(dist[:], dist[:], 0.0, None, ALU.max))
            lg3 = k.lg[:].rearrange("p (d h) -> p d h", d=2)
            link(V.tensor_tensor(k.zeta[:], col[:], lg3, ALU.mult))
            V.tensor_scalar(k.dec[:], lg3, float(P), None, ALU.mult).then_inc(dcols, 1)
            dve.wait_ge(masked, 2)
            link(V.tensor_tensor(k.DT[:], dm[:, 0], dm[:, 1], ALU.add))

        @block.scalar
        def _(act):
            act.wait_ge(e_in, 1)
            nc.scalar.activation(e[:], az[:], ACT.Exp).then_inc(e_out, 1)
            act.wait_ge(dcols, 1)
            nc.scalar.activation(k.zeta[:], k.zeta[:], ACT.Exp).then_inc(xi_done, 1)
            nc.scalar.activation(k.dec[:], k.dec[:], ACT.Exp).then_inc(xi_done, 1)
            for d in range(2):
                for h in range(RH):
                    lg = k.lg[:, d * RH + h:d * RH + h + 1]
                    nc.scalar.activation(k.XI[:, d, h, :], jrow[:, d, :], ACT.Exp, scale=lg).then_inc(xi_done, 1)
                    nc.scalar.activation(dm[:, d, h, :], dist[:, d, :], ACT.Exp, scale=lg).then_inc(dm_done, 1)


def retention(nc, c, a, k, rows, qT, kT):
    ORDER = (list(range(NT)), list(range(CT))[::-1] + list(range(CT, NT))[::-1])
    with Scope(nc, "ret") as s:
        cs = s.sb("cs", [P, 2, NT - CT, RD // 2])
        vz = [s.sb(f"vz{d}", [P, RH, RD]) for d in range(2)]
        st = s.sb("st", [P, 2, NT, RH, RD])
        sT = [s.sb(f"sT{i}", [P, RH, P]) for i in range(2)]
        qx = [[s.sb(f"qx{i}{d}", [P, RH, P]) for d in range(2)] for i in range(2)]
        tq, tk = s.ps("tq", [P, RH, P]), s.ps("tk", [P, RH, P])
        up = [s.ps(f"up{d}", [P, RH, RD]) for d in range(2)]
        sp_ = [s.ps(f"sp{i}", [P, RH, P]) for i in range(2)]
        op = [s.ps(f"op{i}", [P, RH, RD]) for i in range(2)]
        (cs_ready, qrot, krot, trq, trk, evq, evk, vz_done, u_done, st_done, sc, sc_ev, o_done, o_ev, qx_done,
         chain, pchain) = (s.sem(n) for n in (
             "cs_ready", "qrot", "krot", "trq", "trk", "evq", "evk", "vz_done", "u_done", "st_done", "sc",
             "sc_ev", "o_done", "o_ev", "qx_done", "chain", "pchain"))
        block = s.block()
        L = NT - CT
        q_t, k_t, v_t = rows[:, 0], rows[:, 1], rows[:, 2]

        def rotate(eng, link, b, done):
            x = rows[:, b, CT:, :].rearrange("p t (h two n) -> p t h two n", h=RH, two=2)
            x1, x2 = x[:, :, :, 0, :], x[:, :, :, 1, :]
            co, si = (cs[:, i, :, None, :].to_broadcast([P, L, RH, RD // 2]) for i in range(2))
            t1, t2 = (st[:, b, 2 * i:2 * i + 2].rearrange("p t h (two n) -> p (t h two) n", two=2)
                      .rearrange("p (t h) n -> p t h n", h=RH) for i in range(2))
            link(eng.tensor_tensor(t1, x1, si, ALU.mult))
            link(eng.tensor_tensor(t2, x2, si, ALU.mult))
            link(eng.tensor_tensor(x1, x1, co, ALU.mult))
            link(eng.tensor_tensor(x2, x2, co, ALU.mult))
            link(eng.tensor_tensor(x1, x1, t2, ALU.subtract))
            eng.tensor_tensor(x2, x2, t1, ALU.add).then_inc(done, 1)

        @block.sync
        def _(sp):
            sp.dma_start(cs[:], a["ret_cs"]).then_inc(cs_ready, 16)

        @block.gpsimd
        def _(pool):
            pool.wait_ge(cs_ready, 16)
            rotate(nc.gpsimd, Chain(pool, pchain), 1, krot)
            for n in range(NT - 1):
                for d in range(2):
                    t = ORDER[d][n]
                    if n >= 1:
                        pool.wait_ge(u_done, 2 * (n - 1) + d + 1)
                    nc.gpsimd.tensor_tensor(vz[d][:], v_t[:, t].rearrange("p (h e) -> p h e", h=RH),
                                            k.zeta[:, d, :, None].to_broadcast([P, RH, RD]), ALU.mult).then_inc(vz_done, 1)

        @block.tensor
        def _(pe):
            def transposes(t):
                for x, ps, rot, ev, tr in ((q_t, tq, qrot, evq, trq), (k_t, tk, krot, evk, trk)):
                    if t >= CT:
                        pe.wait_ge(rot, 1)
                    if t >= 1:
                        pe.wait_ge(ev, t)
                    for h in range(RH):
                        last = nc.tensor.transpose(ps[:, h, :], x[:, t, h * RD:(h + 1) * RD], c.ident[:])
                    last.then_inc(tr, 1)

            for t in range(NT):
                transposes(t)
            for n in range(NT - 1):
                for d in range(2):
                    t = ORDER[d][n]
                    pe.wait_ge(vz_done, 2 * n + d + 1)
                    if n >= 1:
                        pe.wait_ge(st_done, 2 * (n - 1) + d + 1)
                    for h in range(RH):
                        last = nc.tensor.matmul(up[d][:, h, :], k_t[:, t, h * RD:(h + 1) * RD], vz[d][:, h, :],
                                                start=True, stop=True)
                    last.then_inc(u_done, 1)
            pe.wait_ge(evq, NT)
            pe.wait_ge(evk, NT)
            pe.wait_ge(st_done, 2 * (NT - 1))
            for t in range(NT):
                if t >= 2:
                    pe.wait_ge(sc_ev, t - 1)
                for h in range(RH):
                    last = nc.tensor.matmul(sp_[t % 2][:, h, :], kT[:, h, t * P:(t + 1) * P],
                                            qT[:, h, t * P:(t + 1) * P], start=True, stop=True)
                last.then_inc(sc, 1)
                pe.wait_ge(sc_ev, t + 1)
                pe.wait_ge(qx_done, 2 * t + 2)
                if t >= 2:
                    pe.wait_ge(o_ev, t - 1)
                for h in range(RH):
                    parts = [(sT[t % 2][:, h, :], v_t[:, t, h * RD:(h + 1) * RD])]
                    parts += [(qx[t % 2][d][:, h, :], st[:, d, t, h, :]) for d in range(2) if t != ORDER[d][0]]
                    for n, (lhs, rhs) in enumerate(parts):
                        last = nc.tensor.matmul(op[t % 2][:, h, :], lhs, rhs, start=(n == 0), stop=(n == len(parts) - 1))
                last.then_inc(o_done, 1)

        @block.scalar
        def _(act):
            for t in range(NT):
                act.wait_ge(trq, t + 1)
                nc.scalar.copy(qT[:, :, t * P:(t + 1) * P], tq[:]).then_inc(evq, 1)
                act.wait_ge(trk, t + 1)
                nc.scalar.copy(kT[:, :, t * P:(t + 1) * P], tk[:]).then_inc(evk, 1)
            for t in range(NT):
                act.wait_ge(o_done, t + 1)
                nc.scalar.copy(rows[:, 0, t, :].rearrange("p (h e) -> p h e", h=RH), op[t % 2][:]).then_inc(o_ev, 1)

        @block.vector
        def _(dve):
            link = Chain(dve, chain)
            V = nc.vector
            dve.wait_ge(cs_ready, 16)
            rotate(V, link, 0, qrot)
            dve.wait_ge(krot, 1)
            dve.wait_ge(qrot, 1)
            for n in range(NT - 1):
                for d in range(2):
                    t, nxt = ORDER[d][n], ORDER[d][n + 1]
                    dve.wait_ge(u_done, 2 * n + d + 1)
                    if n == 0:
                        V.tensor_copy(st[:, d, nxt], up[d][:]).then_inc(st_done, 1)
                    else:
                        dve.wait_ge(st_done, 2 * n)
                        link(V.tensor_tensor(st[:, d, nxt], st[:, d, t],
                                             k.dec[:, d, :, None].to_broadcast([P, RH, RD]), ALU.mult))
                        V.tensor_tensor(st[:, d, nxt], st[:, d, nxt], up[d][:], ALU.add).then_inc(st_done, 1)
            dve.wait_ge(evq, NT)
            for t in range(NT):
                if t >= 2:
                    dve.wait_ge(o_done, t - 1)
                for d in range(2):
                    V.tensor_tensor(qx[t % 2][d][:], qT[:, :, t * P:(t + 1) * P], k.XI[:, d], ALU.mult).then_inc(qx_done, 1)
                dve.wait_ge(sc, t + 1)
                V.tensor_tensor(sT[t % 2][:], sp_[t % 2][:], k.DT[:], ALU.mult).then_inc(sc_ev, 1)


def rglru(nc, c, a, k, u, yT):
    W = U_LEN - PADL
    with Scope(nc, "lru") as s:
        cw = s.sb("cw", [P, CONV + 1, LT])
        gb = s.sb("gb", [P, 4, LT])
        gw = s.sb("gw", [P, 4, LT, P])
        xc = s.sb("xc", [P, LT, W])
        x = s.sb("x", [P, LT, TOK])
        r_, i_ = s.sb("r", [P, LT, TOK]), s.sb("i", [P, LT, TOK])
        hs = s.sb("hs", [P, LT, TOK])
        n8 = s.sb("n8", [P, 2 * LT])
        ps = [s.ps(f"ps{i}", [P, 512]) for i in range(8)]
        (p_ready, w_zero, w_ready, conv_done, x_ready, mm, sig, th_in, th_out, q_in, q_out, scan_done, chain,
         y_in, y_out, gx) = (s.sem(n) for n in (
             "p_ready", "w_zero", "w_ready", "conv_done", "x_ready", "mm", "sig", "th_in", "th_out", "q_in",
             "q_out", "scan_done", "chain", "y_in", "y_out", "gx"))
        block = s.block()
        PARTS = ((0, CTX), (CTX, SEQ))

        @block.sync
        def _(sp):
            for t in range(CONV):
                sp.dma_start(cw[:, t, :], a["lru_conv_w"][0, t].rearrange("(c p) -> p c", p=P),
                             allow_slow_non_contiguous=True).then_inc(p_ready, 16)
            sp.dma_start(cw[:, CONV, :], a["lru_conv_b"][0].rearrange("(c p) -> p c", p=P),
                         allow_slow_non_contiguous=True).then_inc(p_ready, 16)
            for dg in range(4):
                sp.dma_start(gb[:, dg, :], a["lru_gate_b"][0, dg // 2, dg % 2].rearrange("(c p) -> p c", p=P),
                             allow_slow_non_contiguous=True).then_inc(p_ready, 16)
            sp.wait_ge(w_zero, 1)
            for dg in range(4):
                for half in range(2):
                    src = a["lru_gate_w"][0, dg // 2, dg % 2].rearrange("(c b) i j -> b i c j", b=2)
                    sp.dma_start(gw[half * LB:(half + 1) * LB, dg, :, half * LB:(half + 1) * LB],
                                 src[half]).then_inc(w_ready, 16)

        @block.gpsimd
        def _(pool):
            nc.gpsimd.memset(gw[:], 0.0).then_inc(w_zero, 1)

        @block.tensor
        def _(pe):
            pe.wait_ge(w_ready, 16 * 8)
            pe.wait_ge(x_ready, 2)
            n = 0
            for d in range(2):
                for ct in range(LT):
                    for g in range(2):
                        for o, m in PARTS:
                            if n >= 8:
                                pe.wait_ge(sig, n - 7)
                            nc.tensor.matmul(ps[n % 8][:, 0:m], gw[:, 2 * d + g, ct, :], x[:, ct, o:o + m],
                                             start=True, stop=True).then_inc(mm, 1)
                            n += 1

        @block.scalar
        def _(act):
            act.wait_ge(p_ready, 16 * (CONV + 5))
            n = 0
            for d in range(2):
                if d == 1:
                    act.wait_ge(scan_done, 1)
                for ct in range(LT):
                    for g in range(2):
                        for o, m in PARTS:
                            act.wait_ge(mm, n + 1)
                            nc.scalar.activation((r_, i_)[g][:, ct, o:o + m], ps[n % 8][:, 0:m], ACT.Sigmoid,
                                                 bias=gb[:, 2 * d + g, ct:ct + 1]).then_inc(sig, 1)
                            n += 1
                act.wait_ge(th_in, d + 1)
                nc.scalar.activation(r_[:], r_[:], ACT.Tanh, scale=0.5).then_inc(th_out, 1)
                act.wait_ge(q_in, d + 1)
                nc.scalar.activation(xc[:, :, 0:TOK], xc[:, :, 0:TOK], ACT.Sqrt).then_inc(q_out, 1)
            act.wait_ge(y_in, 1)
            nc.scalar.activation(r_[:], r_[:], ACT.Tanh, scale=math.sqrt(2.0 / math.pi)).then_inc(y_out, 1)

        @block.vector
        def _(dve):
            link = Chain(dve, chain)
            V = nc.vector
            dve.wait_ge(p_ready, 16 * (CONV + 5))
            for ct in range(LT):
                link(V.tensor_scalar(xc[:, ct, :W - PADR], u[:, ct, 0:W - PADR], cw[:, 0, ct:ct + 1],
                                     cw[:, CONV, ct:ct + 1], ALU.mult, ALU.add))
                for t in range(1, CONV):
                    link(V.scalar_tensor_tensor(out=xc[:, ct, :W - PADR], in0=u[:, ct, t:t + W - PADR],
                                                scalar=cw[:, t, ct:ct + 1], in1=xc[:, ct, :W - PADR],
                                                op0=ALU.mult, op1=ALU.add))
            V.tensor_copy(x[:, :, 0:CTX], xc[:, :, 0:CTX]).then_inc(x_ready, 1)
            V.tensor_copy(x[:, :, CTX:], xc[:, :, U_LAT - PADL:U_LAT - PADL + SEQ]).then_inc(x_ready, 1)
            dve.wait_ge(x_ready, 2)
            link(V.tensor_scalar(n8[:], k.sp[:, 2 * RH:], LRU_C, None, ALU.mult))
            for d in range(2):
                dve.wait_ge(sig, 16 * (d + 1))
                for ct in range(LT):
                    link(V.tensor_scalar(r_[:, ct, :], r_[:, ct, :], n8[:, d * LT + ct:d * LT + ct + 1], None, ALU.mult))
                dve.sem_inc(th_in, 1)
                link(V.tensor_tensor(i_[:], i_[:], x[:], ALU.mult))
                dve.wait_ge(th_out, d + 1)
                q = xc[:, :, 0:TOK]
                link(V.tensor_scalar(q, r_[:], 1.0, None, ALU.add))
                link(V.reciprocal(q, q))
                link(V.scalar_tensor_tensor(out=r_[:], in0=r_[:], scalar=2.0, in1=q, op0=ALU.mult, op1=ALU.mult))
                link(V.tensor_scalar(q, r_[:], -1.0, 2.0, ALU.mult, ALU.add))
                link(V.tensor_tensor(q, q, r_[:], ALU.mult))
                dve.sem_inc(q_in, 1)
                link(V.tensor_scalar(r_[:], r_[:], -1.0, 1.0, ALU.mult, ALU.add))
                dve.wait_ge(q_out, d + 1)
                link(V.tensor_tensor(i_[:], i_[:], q, ALU.mult))
                for ct in range(LT):
                    if d == 0:
                        link(V.tensor_tensor_scan(hs[:, ct, :], r_[:, ct, :], i_[:, ct, :], 0.0, ALU.mult, ALU.add))
                    else:
                        link(V.tensor_tensor_scan(q[:, ct, CTX - 1::-1], r_[:, ct, CTX - 1::-1],
                                                  i_[:, ct, CTX - 1::-1], 0.0, ALU.mult, ALU.add))
                        link(V.tensor_tensor_scan(q[:, ct, TOK - 1:CTX - 1:-1], r_[:, ct, TOK - 1:CTX - 1:-1],
                                                  i_[:, ct, TOK - 1:CTX - 1:-1], q[:, ct, 0:1], ALU.mult, ALU.add))
                dve.sem_inc(scan_done, 1)
            link(V.tensor_tensor(hs[:], hs[:], xc[:, :, 0:TOK], ALU.add))
            link(V.tensor_tensor(r_[:], yT[:], yT[:], ALU.mult))
            link(V.tensor_scalar(r_[:], r_[:], 0.044715, 1.0, ALU.mult, ALU.add))
            link(V.tensor_tensor(r_[:], r_[:], yT[:], ALU.mult))
            dve.sem_inc(y_in, 1)
            link(V.tensor_tensor(yT[:], yT[:], hs[:], ALU.mult))
            dve.wait_ge(y_out, 1)
            link(V.tensor_scalar(r_[:], r_[:], 0.5, 0.5, ALU.mult, ALU.add))
            link(V.tensor_tensor(yT[:], yT[:], r_[:], ALU.mult))


def ab_output(nc, c, a, mb, rows, yT):
    with Scope(nc, "abo") as s:
        w = s.sb("w", [P, KD, DM])
        rT = s.sb("rT", [P, RH, TOK])
        sg = s.sb("sg", [P, NT, QK])
        sq = s.sb("sq", [P, NT, QK])
        tmp = [s.sb(f"tmp{i}", [P, 512]) for i in range(2)]
        ms, root, rstd, tm = (s.sb(n, [P, NT * RH]) for n in ("ms", "root", "rstd", "tm"))
        eps = s.sb("eps", [P, 1])
        tp = [s.ps(f"tp{i}", [P, RH, P]) for i in range(2)]
        ps = [s.ps(f"ps{i}", [P, 512]) for i in range(4)]
        w_ready, chain, ms_done, root_done, sg_done, r_done, tr, tr_ev, mm, x_done = (
            s.sem(n) for n in ("w_ready", "chain", "ms_done", "root_done", "sg_done", "r_done", "tr", "tr_ev",
                               "mm", "x_done"))
        block = s.block()
        ret = rows[:, 0]

        @block.sync
        def _(sp):
            sp.dma_start(w[:], a["ab_w_out"][0].rearrange("(k p) n -> p k n", p=P)).then_inc(w_ready, 16)

        @block.scalar
        def _(act):
            nc.scalar.activation(sg[:], rows[:, 3], ACT.Silu).then_inc(sg_done, 1)
            act.wait_ge(ms_done, 1)
            nc.scalar.activation(root[:], ms[:], ACT.Sqrt, scale=1.0 / RD, bias=eps[:]).then_inc(root_done, 1)
            for t in range(NT):
                act.wait_ge(tr, t + 1)
                nc.scalar.copy(rT[:, :, t * P:(t + 1) * P], tp[t % 2][:]).then_inc(tr_ev, 1)

        @block.vector
        def _(dve):
            link = Chain(dve, chain)
            V = nc.vector
            link(V.memset(eps[:], EPS))
            link(V.tensor_tensor(sq[:], ret, ret, ALU.mult))
            V.tensor_reduce(ms[:], sq[:].rearrange("p t (h e) -> p (t h) e", e=RD), AX, ALU.add).then_inc(ms_done, 1)
            dve.wait_ge(ms_done, 1)
            dve.wait_ge(root_done, 1)
            rms_rows(V, link, rstd[:], root[:], ms[:], tm[:], RD)
            dve.wait_ge(sg_done, 1)
            for t in range(NT):
                link(V.tensor_tensor(ret[:, t].rearrange("p (h e) -> p h e", e=RD),
                                     ret[:, t].rearrange("p (h e) -> p h e", e=RD),
                                     rstd[:, t * RH:(t + 1) * RH, None].to_broadcast([P, RH, RD]), ALU.mult))
                V.tensor_tensor(ret[:, t], ret[:, t], sg[:, t], ALU.mult).then_inc(r_done, 1)
            add_gated(nc, dve, link, c, mb[:, :, 2], NT, 0, ps, tmp, mm, x_done)

        @block.tensor
        def _(pe):
            for t in range(NT):
                pe.wait_ge(r_done, t + 1)
                if t >= 2:
                    pe.wait_ge(tr_ev, t - 1)
                for h in range(RH):
                    last = nc.tensor.transpose(tp[t % 2][:, h, :], ret[:, t, h * RD:(h + 1) * RD], c.ident[:])
                last.then_inc(tr, 1)
            pe.wait_ge(w_ready, 16)
            for t in range(NT):
                pe.wait_ge(tr_ev, t + 1)
                for half in range(2):
                    n = 2 * t + half
                    if n >= 4:
                        pe.wait_ge(x_done, n - 3)
                    for j in range(KD):
                        lhs = rT[:, j, t * P:(t + 1) * P] if j < RH else yT[:, j - RH, t * P:(t + 1) * P]
                        last = nc.tensor.matmul(ps[n % 4][:], lhs, w[:, j, half * 512:(half + 1) * 512],
                                                start=(j == 0), stop=(j == KD - 1))
                    last.then_inc(mm, 1)


def add_gated(nc, dve, link, c, gate, T, t0, ps, tmp, mm, x_done):
    for n in range(2 * T):
        t, half = divmod(n, 2)
        st = 1 if t0 + t < CT else 0
        cols = slice(half * 512, (half + 1) * 512)
        dve.wait_ge(mm, n + 1)
        link(nc.vector.tensor_tensor(tmp[n % 2][:], ps[n % len(ps)][:], gate[:, st, cols], ALU.mult))
        nc.vector.tensor_tensor(c.X[:, t0 + t, cols], c.X[:, t0 + t, cols], tmp[n % 2][:], ALU.add).then_inc(x_done, 1)


def ab_layer(nc, c, a):
    with Scope(nc, "ab") as s:
        mb = s.sb("mb", [P, 2, 3, DM])
        rows = s.sb("rows", [P, 4, NT, QK])
        u = s.sb("u", [P, LT, U_LEN])
        yT = s.sb("yT", [P, LT, TOK])
        k = Box()
        k.sp = s.sb("sp", [P, 2 * RH + 2 * LT])
        k.lg = s.sb("lg", [P, 2 * RH])
        k.zeta, k.dec = s.sb("zeta", [P, 2, RH]), s.sb("dec", [P, 2, RH])
        k.XI = s.sb("XI", [P, 2, RH, P])
        k.DT = s.sb("DT", [P, RH, P])
        with Scope(nc, "abh") as s2:
            hT = s2.sb("hT", [P, KD, TOK])
            norm_modulate(nc, c, a, 0, 0, 0, hT, mb, None)
            ab_project(nc, c, a, hT, rows, u, yT)
        small_tables(nc, c, a, k)
        with Scope(nc, "abr") as s3:
            qT, kT = s3.sb("qT", [P, RH, TOK]), s3.sb("kT", [P, RH, TOK])
            retention(nc, c, a, k, rows, qT, kT)
        rglru(nc, c, a, k, u, yT)
        ab_output(nc, c, a, mb, rows, yT)


def mla_latents(nc, c, a, hT, k):
    IN = QR + KVR + ROPE
    L = NT - CT
    with Scope(nc, "mlat") as s:
        w = s.sb("w", [P, KD, IN])
        p = s.sb("p", [P, NT, IN])
        junk = s.sb("junk", [P, QR])
        g = s.sb("g", [P, (QR + KVR) // P])
        ms = s.sb("ms", [P, 2, NT])
        root, rstd, tmp, width = (s.sb(n, [P, 2, NT]) for n in ("root", "rstd", "tmp", "width"))
        eps = s.sb("eps", [P, 1])
        cs = s.sb("cs", [P, 2, L, ROPE // 2])
        ta, tb = s.sb("ta", [P, L, ROPE // 2]), s.sb("tb", [P, L, ROPE // 2])
        ps = [s.ps(f"ps{i}", [P, 2, 512]) for i in range(2)]
        tq, tk, tr_ = (s.ps(n, [P, 4, P]) for n in ("tq", "tk", "tr"))
        ready, g_ready, mm, ev, sq, root_done, chain, rows_done, qtr, ktr, rtr, q_ev, k_ev, r_ev, set_ = (
            s.sem(n) for n in ("ready", "g_ready", "mm", "ev", "sq", "root_done", "chain", "rows_done", "qtr",
                               "ktr", "rtr", "q_ev", "k_ev", "r_ev", "set"))
        block = s.block()

        @block.sync
        def _(sp):
            sp.dma_start(w[:], a["mla_w_in"][0].rearrange("(k p) n -> p k n", p=P)).then_inc(ready, 16)
            sp.dma_start(g[:, 0:QR // P], a["mla_q_norm_g"][0].rearrange("(c p) -> p c", p=P),
                         allow_slow_non_contiguous=True).then_inc(g_ready, 16)
            sp.dma_start(g[:, QR // P:], a["mla_kv_norm_g"][0].rearrange("(c p) -> p c", p=P),
                         allow_slow_non_contiguous=True).then_inc(g_ready, 16)
            sp.dma_start(cs[:], a["mla_cs"]).then_inc(g_ready, 16)

        @block.tensor
        def _(pe):
            pe.wait_ge(ready, 16)
            for t in range(NT):
                if t >= 2:
                    pe.wait_ge(ev, t - 1)
                for k_ in range(KD):
                    if t >= CT:
                        nc.tensor.matmul(ps[t % 2][:, 0, 0:QR], hT[:, k_, t * P:(t + 1) * P], w[:, k_, 0:QR],
                                         start=(k_ == 0), stop=(k_ == KD - 1))
                for k_ in range(KD):
                    last = nc.tensor.matmul(ps[t % 2][:, 1, 0:KVR + ROPE], hT[:, k_, t * P:(t + 1) * P], w[:, k_, QR:],
                                            start=(k_ == 0), stop=(k_ == KD - 1))
                last.then_inc(mm, 1)
            for t in range(NT):
                pe.wait_ge(rows_done, t + 1)
                if t > CT:
                    pe.wait_ge(q_ev, t - CT)
                if t >= CT:
                    for j in range(QR // P):
                        last = nc.tensor.transpose(tq[:, j, :], p[:, t, j * P:(j + 1) * P], c.ident[:])
                    last.then_inc(qtr, 1)
                if t >= 1:
                    pe.wait_ge(k_ev, t)
                for j in range(KVR // P):
                    last = nc.tensor.transpose(tk[:, j, :], p[:, t, QR + j * P:QR + (j + 1) * P], c.ident[:])
                last.then_inc(ktr, 1)
                if t >= 1:
                    pe.wait_ge(r_ev, t)
                nc.tensor.transpose(tr_[0:ROPE, 0, :], p[:, t, QR + KVR:], c.ident[:]).then_inc(rtr, 1)

        @block.scalar
        def _(act):
            act.wait_ge(set_, 1)
            n = 0
            for t in range(NT):
                act.wait_ge(ev, t + 1)
                for i, (o, m) in enumerate(((0, QR), (QR, KVR))):
                    if i == 0 and t < CT:
                        continue
                    n += 1
                    nc.scalar.activation(junk[:, 0:m], p[:, t, o:o + m], ACT.Square, accum_out=ms[:, i, t:t + 1]).then_inc(sq, 1)
                    act.wait_ge(sq, n)
            nc.scalar.activation(root[:, 0], ms[:, 0], ACT.Sqrt, scale=1.0 / QR, bias=eps[:]).then_inc(root_done, 1)
            nc.scalar.activation(root[:, 1], ms[:, 1], ACT.Sqrt, scale=1.0 / KVR, bias=eps[:]).then_inc(root_done, 1)

        @block.gpsimd
        def _(pool):
            for t in range(NT):
                pool.wait_ge(r_ev, t + 1)
            for h in range(AH):
                nc.gpsimd.tensor_copy(k.KT[NOPE:NOPE + ROPE, h, :], k.krT[NOPE:NOPE + ROPE, :]).then_inc(k.kr_done, 1)
            pool.wait_ge(k.kr_done, AH)

        @block.vector
        def _(dve):
            link = Chain(dve, chain)
            V = nc.vector
            link(V.memset(eps[:], EPS))
            link(V.memset(width[:, 0], 1.0 / QR))
            link(V.memset(width[:, 1], 1.0 / KVR))
            V.memset(ms[:], 1.0).then_inc(set_, 1)
            for t in range(NT):
                dve.wait_ge(mm, t + 1)
                if t >= CT:
                    link(V.tensor_copy(p[:, t, 0:QR], ps[t % 2][:, 0, 0:QR]))
                V.tensor_copy(p[:, t, QR:], ps[t % 2][:, 1, 0:KVR + ROPE]).then_inc(ev, 1)
            dve.wait_ge(g_ready, 48)
            x1, x2 = (p[:, CT:, QR + KVR + i * (ROPE // 2):QR + KVR + (i + 1) * (ROPE // 2)] for i in range(2))
            dve.wait_ge(ev, NT)
            link(V.tensor_tensor(ta[:], x1, cs[:, 1], ALU.mult))
            link(V.tensor_tensor(tb[:], x2, cs[:, 1], ALU.mult))
            link(V.tensor_tensor(x1, x1, cs[:, 0], ALU.mult))
            link(V.tensor_tensor(x2, x2, cs[:, 0], ALU.mult))
            link(V.tensor_tensor(x1, x1, tb[:], ALU.subtract))
            link(V.tensor_tensor(x2, x2, ta[:], ALU.add))
            dve.wait_ge(root_done, 2)
            link(V.reciprocal(rstd[:], root[:]))
            link(V.tensor_tensor(ms[:], ms[:], width[:], ALU.mult))
            link(V.tensor_scalar(ms[:], ms[:], EPS, None, ALU.add))
            link(V.tensor_tensor(tmp[:], rstd[:], rstd[:], ALU.mult))
            link(V.tensor_tensor(tmp[:], tmp[:], ms[:], ALU.mult))
            link(V.tensor_scalar(tmp[:], tmp[:], -0.5, 1.5, ALU.mult, ALU.add))
            link(V.tensor_tensor(rstd[:], rstd[:], tmp[:], ALU.mult))
            for t in range(NT):
                if t >= CT:
                    link(V.tensor_scalar(p[:, t, 0:QR], p[:, t, 0:QR], rstd[:, 0, t:t + 1], None, ALU.mult))
                V.tensor_scalar(p[:, t, QR:QR + KVR], p[:, t, QR:QR + KVR], rstd[:, 1, t:t + 1], None,
                                ALU.mult).then_inc(rows_done, 1)
            for t in range(NT):
                if t >= CT:
                    dve.wait_ge(qtr, t - CT + 1)
                    V.tensor_tensor(k.cqT[:, :, (t - CT) * P:(t - CT + 1) * P], tq[:, 0:QR // P, :],
                                    g[:, 0:QR // P, None].to_broadcast([P, QR // P, P]), ALU.mult).then_inc(q_ev, 1)
                dve.wait_ge(ktr, t + 1)
                V.tensor_tensor(k.ckT[:, :, t * P:(t + 1) * P], tk[:, 0:KVR // P, :],
                                g[:, QR // P:, None].to_broadcast([P, KVR // P, P]), ALU.mult).then_inc(k_ev, 1)
                dve.wait_ge(rtr, t + 1)
                V.tensor_copy(k.krT[NOPE:NOPE + ROPE, t * P:(t + 1) * P], tr_[0:ROPE, 0, :]).then_inc(r_ev, 1)


def mla_heads(nc, c, a, k):
    L = NT - CT
    QD = NOPE + ROPE
    HALF = TOK // 2
    with Scope(nc, "mhead") as s:
        wq = s.sb("wq", [P, QR // P, AH * QD])
        wkv = s.sb("wkv", [P, KVR // P, AH * (NOPE + VD)])
        q = k.q
        cs = s.sb("cs", [P, 2, L, ROPE // 2])
        ta, tb = (s.sb(n, [P, AH, ROPE // 2]) for n in ("ta", "tb"))
        ps = [s.ps(f"ps{i}", [P, 512]) for i in range(8)]
        ready, mm, chain, rot = (s.sem(n) for n in ("ready", "mm", "chain", "rot"))
        evs = [s.sem("ev_act"), s.sem("ev_dve")]
        block = s.block()
        groups = [("v", t, b) for t in range(NT) for b in range(2)]
        groups += [("q", t, b) for t in range(L) for b in range(3)]
        groups += [("k", h, b) for h in range(0, AH, 2) for b in range(2)]
        groups += [("t", h, 0) for h in range(AH)]
        Q_END = NT * 2 + L * 3

        def copy_out(eng_copy, eng_scale, i, kind, x, b):
            bank = ps[i % 8]
            if kind == "v":
                return [eng_copy(k.V[:, x, b * 512:(b + 1) * 512], bank[:])]
            if kind == "q":
                return [eng_copy(q[:, x, b * 512:(b + 1) * 512], bank[:])]
            if kind == "k":
                return [eng_copy(k.KT[0:NOPE, x + j, b * HALF:(b + 1) * HALF], bank[64 * j:64 * j + NOPE, 0:HALF])
                        for j in range(2)]
            return [eng_scale(k.QT[0:QD, x, :], bank[0:QD, :])]

        @block.sync
        def _(sp):
            sp.dma_start(wkv[:], a["mla_w_ukv"][0].rearrange("(k p) n -> p k n", p=P)).then_inc(ready, 16)
            sp.dma_start(wq[:], a["mla_w_uq"][0].rearrange("(k p) n -> p k n", p=P)).then_inc(ready, 16)
            sp.dma_start(cs[:], a["mla_cs"]).then_inc(ready, 16)

        @block.tensor
        def _(pe):
            pe.wait_ge(ready, 48)
            wv = wkv[:].rearrange("p k (h two n) -> p k h two n", two=2, n=VD)
            for i, (kind, x, b) in enumerate(groups):
                bank = ps[i % 8]
                if i >= 8:
                    pe.wait_ge(evs[i % 2], (i - 8) // 2 + 1)
                if kind == "v":
                    for j in range(KVR // P):
                        last = nc.tensor.matmul(bank[:], k.ckT[:, j, x * P:(x + 1) * P], wv[:, j, b * 8:(b + 1) * 8, 1, :],
                                                start=(j == 0), stop=(j == KVR // P - 1))
                elif kind == "q":
                    for j in range(QR // P):
                        last = nc.tensor.matmul(bank[:], k.cqT[:, j, x * P:(x + 1) * P], wq[:, j, b * 512:(b + 1) * 512],
                                                start=(j == 0), stop=(j == QR // P - 1))
                elif kind == "k":
                    for j in range(KVR // P):
                        for e in range(2):
                            last = nc.tensor.matmul(bank[64 * e:64 * e + NOPE, 0:HALF], wv[:, j, x + e, 0, :],
                                                    k.ckT[:, j, b * HALF:(b + 1) * HALF],
                                                    start=(j == 0), stop=(j == KVR // P - 1))
                else:
                    pe.wait_ge(rot, L)
                    for t in range(L):
                        last = nc.tensor.transpose(bank[0:QD, t * P:(t + 1) * P], q[:, t, x * QD:(x + 1) * QD], c.ident[:])
                last.then_inc(mm, 1)

        @block.scalar
        def _(act):
            for i in range(0, len(groups), 2):
                act.wait_ge(mm, i + 1)
                copies = copy_out(nc.scalar.copy, lambda o, x: nc.scalar.mul(o, x, MLA_SCALE), i, *groups[i])
                copies[-1].then_inc(evs[0], 1)

        @block.vector
        def _(dve):
            link = Chain(dve, chain)
            V = nc.vector
            dve.wait_ge(ready, 48)
            for i in range(1, len(groups), 2):
                dve.wait_ge(mm, i + 1)
                copies = copy_out(V.tensor_copy, lambda o, x: V.tensor_scalar(o, x, MLA_SCALE, None, ALU.mult),
                                  i, *groups[i])
                copies[-1].then_inc(evs[1], 1)
                if i + 1 == Q_END:
                    dve.wait_ge(evs[0], Q_END // 2)
                    dve.wait_ge(evs[1], Q_END // 2)
                    for t in range(L):
                        x = q[:, t, :].rearrange("p (h n) -> p h n", n=QD)
                        x1, x2 = x[:, :, NOPE:NOPE + ROPE // 2], x[:, :, NOPE + ROPE // 2:]
                        co, si = (cs[:, j, t, None, :].to_broadcast([P, AH, ROPE // 2]) for j in range(2))
                        link(V.tensor_tensor(ta[:], x1, si, ALU.mult))
                        link(V.tensor_tensor(tb[:], x2, si, ALU.mult))
                        link(V.tensor_tensor(x1, x1, co, ALU.mult))
                        link(V.tensor_tensor(x2, x2, co, ALU.mult))
                        link(V.tensor_tensor(x1, x1, tb[:], ALU.subtract))
                        V.tensor_tensor(x2, x2, ta[:], ALU.add).then_inc(rot, 1)
                        dve.wait_ge(rot, t + 1)


def attention(nc, c, k):
    L = NT - CT
    QD = NOPE + ROPE
    UNITS = [(h, t) for h in range(AH) for t in range(L)]
    N = len(UNITS)
    with Scope(nc, "att") as s:
        pr = [s.sb(f"pr{i}", [P, TOK]) for i in range(2)]
        pT = [s.sb(f"pT{i}", [P, NT, P]) for i in range(2)]
        nmax = s.sb("nmax", [P, 2])
        tot = s.sb("tot", [P, 2])
        inv = s.sb("inv", [P, 2])
        sc = [s.ps(f"sc{i}", [P, 2, 512]) for i in range(2)]
        tp = [s.ps(f"tp{i}", [P, 3, P]) for i in range(2)]
        pv = [s.ps(f"pv{i}", [P, 512]) for i in range(2)]
        sc_done, mx, ex, tr, ev_a, ev_d, pv_done, inv_done, o_done = (
            s.sem(n) for n in ("sc_done", "mx", "ex", "tr", "ev_a", "ev_d", "pv_done", "inv_done", "o_done"))
        block = s.block()
        HALF = TOK // 2

        @block.tensor
        def _(pe):
            def scores(n):
                h, t = UNITS[n]
                if n >= 2:
                    pe.wait_ge(ex, n - 1)
                for b in range(2):
                    last = nc.tensor.matmul(sc[n % 2][:, b, 0:HALF], k.QT[0:QD, h, t * P:(t + 1) * P],
                                            k.KT[0:QD, h, b * HALF:(b + 1) * HALF], start=True, stop=True)
                last.then_inc(sc_done, 1)

            scores(0)
            for n, (h, t) in enumerate(UNITS):
                if n + 1 < N:
                    scores(n + 1)
                pe.wait_ge(ex, n + 1)
                for b, ev in ((0, ev_a), (1, ev_d)):
                    if n >= 1:
                        pe.wait_ge(ev, n)
                    for j in range(3):
                        kt = 3 * b + j
                        last = nc.tensor.transpose(tp[b][:, j, :], pr[n % 2][:, kt * P:(kt + 1) * P], c.ident[:])
                    last.then_inc(tr, 1)
                if n >= 2:
                    pe.wait_ge(o_done, n - 1)
                for kt in range(NT):
                    if kt % 3 == 0:
                        pe.wait_ge((ev_a, ev_d)[kt // 3], n + 1)
                    last = nc.tensor.matmul(pv[n % 2][:, 0:VD], pT[n % 2][:, kt, :], k.V[:, kt, h * VD:(h + 1) * VD],
                                            start=(kt == 0), stop=(kt == NT - 1))
                last.then_inc(pv_done, 1)

        @block.scalar
        def _(act):
            for n in range(N):
                act.wait_ge(mx, n + 1)
                if n >= 2:
                    act.wait_ge(inv_done, n - 1)
                nc.scalar.activation(pr[n % 2][:].rearrange("p (b m) -> p b m", b=2), sc[n % 2][:, :, 0:HALF], ACT.Exp,
                                     bias=nmax[:, n % 2:n % 2 + 1], accum_out=tot[:, n % 2:n % 2 + 1]).then_inc(ex, 1)
                if n >= 2:
                    act.wait_ge(pv_done, n - 1)
                act.wait_ge(tr, 2 * n + 1)
                nc.scalar.copy(pT[n % 2][:, 0:3, :], tp[0][:]).then_inc(ev_a, 1)

        @block.vector
        def _(dve):
            def maximum(n):
                dve.wait_ge(sc_done, n + 1)
                if n >= 2:
                    dve.wait_ge(ex, n - 1)
                nc.vector.tensor_reduce(nmax[:, n % 2:n % 2 + 1], sc[n % 2][:, :, 0:HALF], mybir.AxisListType.XY,
                                        ALU.max, negate=True).then_inc(mx, 1)

            maximum(0)
            for n, (h, t) in enumerate(UNITS):
                if n + 1 < N:
                    maximum(n + 1)
                dve.wait_ge(ex, n + 1)
                if n >= 2:
                    dve.wait_ge(o_done, n - 1)
                nc.vector.reciprocal(inv[:, n % 2:n % 2 + 1], tot[:, n % 2:n % 2 + 1]).then_inc(inv_done, 1)
                dve.wait_ge(tr, 2 * n + 2)
                nc.vector.tensor_copy(pT[n % 2][:, 3:6, :], tp[1][:]).then_inc(ev_d, 1)
                dve.wait_ge(inv_done, n + 1)
                dve.wait_ge(pv_done, n + 1)
                nc.vector.tensor_scalar(k.O[:, t, h * VD:(h + 1) * VD], pv[n % 2][:, 0:VD], inv[:, n % 2:n % 2 + 1],
                                        None, ALU.mult).then_inc(o_done, 1)


def mla_output(nc, c, a, gate, O):
    L = NT - CT
    with Scope(nc, "mlao") as s:
        w = s.sb("w", [P, KD, DM])
        oT = s.sb("oT", [P, KD, L * P])
        tmp = [s.sb(f"tmp{i}", [P, 512]) for i in range(2)]
        tp = [s.ps(f"tp{i}", [P, 4, P]) for i in range(2)]
        ps = [s.ps(f"ps{i}", [P, 512]) for i in range(4)]
        w_ready, tr, ev, mm, x_done, chain = (s.sem(n) for n in ("w_ready", "tr", "ev", "mm", "x_done", "chain"))
        block = s.block()

        @block.sync
        def _(sp):
            sp.dma_start(w[:], a["mla_w_out"][0].rearrange("(k p) n -> p k n", p=P)).then_inc(w_ready, 16)

        @block.tensor
        def _(pe):
            for n in range(2 * L):
                t, half = divmod(n, 2)
                if n >= 2:
                    pe.wait_ge(ev, n - 1)
                for j in range(4):
                    m = 4 * half + j
                    last = nc.tensor.transpose(tp[n % 2][:, j, :], O[:, t, m * P:(m + 1) * P], c.ident[:])
                last.then_inc(tr, 1)
            pe.wait_ge(w_ready, 16)
            for n in range(2 * L):
                t, half = divmod(n, 2)
                pe.wait_ge(ev, 2 * t + 2)
                if n >= 4:
                    pe.wait_ge(x_done, n - 3)
                for j in range(KD):
                    last = nc.tensor.matmul(ps[n % 4][:], oT[:, j, t * P:(t + 1) * P], w[:, j, half * 512:(half + 1) * 512],
                                            start=(j == 0), stop=(j == KD - 1))
                last.then_inc(mm, 1)

        @block.scalar
        def _(act):
            for n in range(2 * L):
                t, half = divmod(n, 2)
                act.wait_ge(tr, n + 1)
                nc.scalar.copy(oT[:, 4 * half:4 * half + 4, t * P:(t + 1) * P], tp[n % 2][:]).then_inc(ev, 1)

        @block.vector
        def _(dve):
            add_gated(nc, dve, Chain(dve, chain), c, gate[:, :, 0], L, CT, ps, tmp, mm, x_done)


def keep_gate(nc, gate, mb):
    with Scope(nc, "gate") as s:
        done = s.sem("done")
        block = s.block()

        @block.vector
        def _(dve):
            nc.vector.tensor_copy(gate[:, 0, 0, :], mb[:, 0, 2, :]).then_inc(done, 1)
            dve.wait_ge(done, 1)


def mla_layer(nc, c, a):
    L = NT - CT
    with Scope(nc, "mla") as s:
        gate = s.sb("gate", [P, 1, 1, DM])
        k = Box()
        k.q = s.sb("q", [P, L, AH * (NOPE + ROPE)])
        k.O = k.q[:, :, 0:AH * VD]
        with Scope(nc, "mlak") as s1:
            k.KT = s1.sb("KT", [P, AH, TOK])
            k.kr_done = s1.sem("kr_done")
            k.cqT = s1.sb("cqT", [P, QR // P, L * P])
            k.ckT = s1.sb("ckT", [P, KVR // P, TOK])
            with Scope(nc, "mlah") as s2:
                k.krT = s2.sb("krT", [P, TOK])
                hT = s2.sb("hT", [P, KD, TOK])
                with Scope(nc, "mlam") as s3:
                    mb = s3.sb("mb", [P, 2, 3, DM])
                    norm_modulate(nc, c, a, 1, 0, 0, hT, mb, None)
                    keep_gate(nc, gate, mb)
                mla_latents(nc, c, a, hT, k)
            k.V = s1.sb("V", [P, NT, AH * VD])
            k.QT = s1.sb("QT", [P, AH, L * P])
            mla_heads(nc, c, a, k)
            attention(nc, c, k)
        mla_output(nc, c, a, gate, k.O)


def routing(nc, c, a, layer, t0, hT, r):
    T = NT - t0
    OVB = T * 2 - 1
    STEPS = T - 1
    with Scope(nc, f"route{layer}") as s:
        rw = s.sb("rw", [P, KD, ROUTES])
        rb = s.sb("rb", [P, ROUTES])
        lg = s.sb("lg", [P, T, ROUTES])
        g4 = [s.sb(f"g4_{i}", [P, T, G]) for i in range(3)]
        t1 = [s.sb(f"t1_{i}", [P, T, 1]) for i in range(6)]
        e8 = [s.sb(f"e8_{i}", [P, T, EPG]) for i in range(5)]
        sel = s.sb("sel", [P, T, G, EPG])
        pick = [s.sb(f"pick{i}", [P, T, E]) for i in range(2)]
        both = s.sb("both", [P, T, E])
        pos = s.sb("pos", [P, T, E])
        nb = s.sb("nb", [P, T, E])
        hot = s.sb("hot", [P, T, E])
        slot = s.sb("slot", [P, T, E])
        cnt = s.sb("cnt", [P, E])
        blocks = s.sb("blocks", [P, E])
        ends = s.sb("ends", [P, E])
        starts = s.sb("starts", [P, E])
        oute = s.sb("oute", [P, OVB, E])
        ove = s.sb("ove", [P, OVB + 1])
        iog = s.sb("iog", [P, G])
        ioe = s.sb("ioe", [P, EPG])
        ioE = s.sb("ioE", [P, E])
        iob = s.sb("iob", [P, OVB])
        tokid = s.sb("tokid", [P, T], I32)
        place = s.sb("place", [P, 2 * T], I32)
        zero = s.sb("zero", [P, E + OVB], I32)
        onesE = s.sb("onesE", [P, E])
        lps = s.ps("lps", [P, T, ROUTES])
        pps = s.ps("pps", [P, T, E])
        cps = s.ps("cps", [P, E])
        w_ready, io_ready, lg_done, m_done, pos_done, chain, zero_done, list0, slots_done, scat, back = (
            s.sem(n) for n in ("w_ready", "io_ready", "lg_done", "m_done", "pos_done", "chain", "zero_done",
                               "list0", "slots_done", "scat", "back"))
        block = s.block()

        @block.sync
        def _(sp):
            sp.dma_start(rw[:, :, 0:G], a["moe_group_w"][layer].rearrange("(k p) n -> p k n", p=P)).then_inc(w_ready, 16)
            sp.dma_start(rw[:, :, G:], a["moe_expert_w"][layer].rearrange("(k p) n -> p k n", p=P)).then_inc(w_ready, 16)
            sp.dma_start(rb[:, 0:G], a["moe_group_b"][layer:layer + 1, :].to_broadcast([P, G])).then_inc(w_ready, 16)
            sp.dma_start(rb[:, G:], a["moe_expert_b"][layer:layer + 1, :].to_broadcast([P, E])).then_inc(w_ready, 16)
            sp.wait_ge(zero_done, 1)
            sp.dma_start(c.slot_tok[0:(E + OVB) * P, :].rearrange("(p c) o -> p (c o)", p=P), zero[:]).then_inc(list0, 16)
            sp.wait_ge(scat, 16 * 2 * T)
            sp.dma_start(r.tok[:, 0:E + OVB], c.slot_tok[0:(E + OVB) * P, :]
                         .rearrange("(p c) o -> p (c o)", p=P)).then_inc(back, 16)
            sp.wait_ge(back, 16)

        @block.gpsimd
        def _(pool):
            nc.gpsimd.iota(iog[:], pattern=[[-1, G]], base=G, channel_multiplier=0,
                           allow_small_or_imprecise_dtypes=True).then_inc(io_ready, 1)
            nc.gpsimd.iota(ioe[:], pattern=[[-1, EPG]], base=EPG, channel_multiplier=0,
                           allow_small_or_imprecise_dtypes=True).then_inc(io_ready, 1)
            nc.gpsimd.iota(ioE[:], pattern=[[1, E]], base=0, channel_multiplier=0,
                           allow_small_or_imprecise_dtypes=True).then_inc(io_ready, 1)
            nc.gpsimd.iota(iob[:], pattern=[[1, OVB]], base=0, channel_multiplier=0,
                           allow_small_or_imprecise_dtypes=True).then_inc(io_ready, 1)
            nc.gpsimd.iota(tokid[:], pattern=[[P, T]], base=t0 * P, channel_multiplier=1).then_inc(io_ready, 1)
            nc.gpsimd.memset(onesE[:], 1.0).then_inc(io_ready, 1)
            nc.gpsimd.iota(zero[:], pattern=[[0, E + OVB]], base=t0 * P, channel_multiplier=0).then_inc(zero_done, 1)
            pool.wait_ge(io_ready, 5)
            pool.wait_ge(list0, 16)
            pool.wait_ge(slots_done, 4)
            for t in range(T):
                for k in range(2):
                    nc.gpsimd.indirect_dma_start(
                        c.slot_tok[:, :], bass.IndirectOffsetOnAxis(place[:, k * T + t:k * T + t + 1], 0),
                        tokid[:, t:t + 1], None).then_inc(scat, 16)
            pool.wait_ge(scat, 16 * 2 * T)

        @block.tensor
        def _(pe):
            pe.wait_ge(w_ready, 64)
            for t in range(T):
                for k in range(KD):
                    last = nc.tensor.matmul(lps[:, t, :], hT[:, k, t * P:(t + 1) * P], rw[:, k, :],
                                            start=(k == 0), stop=(k == KD - 1))
            last.then_inc(lg_done, 1)
            pe.wait_ge(m_done, 1)
            for t in range(T):
                for q in range(t + 1):
                    nc.tensor.matmul(pps[:, t, :], c.before[:] if q == t else c.ones[:], both[:, q, :],
                                     start=(q == 0), stop=(q == t))
            for q in range(T):
                last = nc.tensor.matmul(cps[:], c.ones[:], both[:, q, :], start=(q == 0), stop=(q == T - 1))
            last.then_inc(pos_done, 1)

        @block.vector
        def _(dve):
            link = Chain(dve, chain)
            V = nc.vector
            dve.wait_ge(io_ready, 6)
            dve.wait_ge(lg_done, 1)
            link(V.tensor_tensor(lg[:], lps[:], rb[:, None, :].to_broadcast([P, T, ROUTES]), ALU.add))
            gl, el = lg[:, :, 0:G], lg[:, :, G:]

            def first_hot(out, vals, top, order, tmp, best, n):
                link(V.tensor_reduce(top[:, :, 0], vals, AX, ALU.max))
                link(V.tensor_tensor(tmp, vals, top[:].to_broadcast([P, T, n]), ALU.is_equal))
                link(V.tensor_tensor(tmp, tmp, order[:, None, :].to_broadcast([P, T, n]), ALU.mult))
                link(V.tensor_reduce(best[:, :, 0], tmp, AX, ALU.max))
                link(V.tensor_tensor(out, tmp, best[:].to_broadcast([P, T, n]), ALU.is_equal))

            gtop, best, e1, e2, gsum, wt = t1
            first_hot(g4[0][:], gl, gtop, iog, g4[1][:], best, G)
            link(V.tensor_tensor(g4[1][:], gl, gtop[:].to_broadcast([P, T, G]), ALU.subtract))
            link(V.tensor_tensor(sel[:], el.rearrange("p t (g e) -> p t g e", g=G),
                                 g4[0][:, :, :, None].to_broadcast([P, T, G, EPG]), ALU.mult))
            link(V.tensor_reduce(e8[0][:], sel[:].rearrange("p t g e -> p t e g"), AX, ALU.add))
            first_hot(e8[1][:], e8[0][:], e1, ioe, e8[2][:], best, EPG)
            link(V.scalar_tensor_tensor(out=e8[3][:], in0=e8[1][:], scalar=-1e30, in1=e8[0][:],
                                        op0=ALU.mult, op1=ALU.add))
            first_hot(e8[4][:], e8[3][:], e2, ioe, e8[2][:], best, EPG)
            link(V.tensor_tensor(wt[:], e2[:], e1[:], ALU.subtract))
            for k, hot8 in ((0, e8[1]), (1, e8[4])):
                link(V.tensor_tensor(pick[k][:].rearrange("p t (g e) -> p t g e", g=G),
                                     g4[0][:, :, :, None].to_broadcast([P, T, G, EPG]),
                                     hot8[:, :, None, :].to_broadcast([P, T, G, EPG]), ALU.mult))
            V.tensor_tensor(both[:], pick[0][:], pick[1][:], ALU.add).then_inc(m_done, 1)
            dve.wait_ge(pos_done, 1)
            link(V.tensor_copy(pos[:], pps[:]))
            link(V.tensor_copy(cnt[:], cps[:]))
            link(V.tensor_scalar(blocks[:], cnt[:], float(CAP), None, ALU.is_gt))
            for j in range(2, STEPS + 1):
                link(V.scalar_tensor_tensor(out=blocks[:], in0=cnt[:], scalar=float(CAP * j), in1=blocks[:],
                                            op0=ALU.is_gt, op1=ALU.add))
            link(V.tensor_tensor_scan(ends[:], onesE[:], blocks[:], 0.0, ALU.mult, ALU.add))
            link(V.tensor_tensor(starts[:], ends[:], blocks[:], ALU.subtract))
            link(V.tensor_scalar(nb[:], pos[:], float(CAP), None, ALU.is_ge))
            for j in range(2, STEPS + 1):
                link(V.scalar_tensor_tensor(out=nb[:], in0=pos[:], scalar=float(CAP * j), in1=nb[:],
                                            op0=ALU.is_ge, op1=ALU.add))
            link(V.tensor_scalar(hot[:], nb[:], 0.0, None, ALU.is_gt))
            link(V.tensor_scalar(starts[:], starts[:], float(E - 1), None, ALU.add))
            link(V.tensor_tensor(starts[:], starts[:], ioE[:], ALU.subtract))
            link(V.tensor_tensor(slot[:], hot[:], starts[:, None, :].to_broadcast([P, T, E]), ALU.mult))
            link(V.tensor_tensor(slot[:], slot[:], ioE[:, None, :].to_broadcast([P, T, E]), ALU.add))
            link(V.tensor_tensor(slot[:], slot[:], nb[:], ALU.add))
            link(V.scalar_tensor_tensor(out=pos[:], in0=nb[:], scalar=-float(CAP), in1=pos[:],
                                        op0=ALU.mult, op1=ALU.add))
            link(V.scalar_tensor_tensor(out=nb[:], in0=pos[:], scalar=float(E + OVB), in1=slot[:],
                                        op0=ALU.mult, op1=ALU.add))
            link(V.scalar_tensor_tensor(out=slot[:], in0=slot[:], scalar=float(CAP), in1=pos[:],
                                        op0=ALU.mult, op1=ALU.add))
            for k in range(2):
                for n, (of, into) in enumerate(((slot, r.slot), (nb, place))):
                    link(V.tensor_tensor(hot[:], pick[k][:], of[:], ALU.mult))
                    link(V.tensor_reduce(best[:, :, 0], hot[:], AX, ALU.add))
                    V.tensor_copy(into[:, k * T:(k + 1) * T], best[:, :, 0]).then_inc(slots_done, 1)
                    dve.wait_ge(slots_done, 2 * k + n + 1)
            link(V.tensor_tensor(oute[:], ends[:, None, :].to_broadcast([P, OVB, E]),
                                 iob[:, :, None].to_broadcast([P, OVB, E]), ALU.is_le))
            link(V.tensor_reduce(ove[:, 0:OVB], oute[:], AX, ALU.add))
            link(V.tensor_scalar(ove[:, 0:OVB], ove[:, 0:OVB], float(E - 1), None, ALU.min))
            link(V.tensor_copy(ove[:, OVB:OVB + 1], ends[:, E - 1:E]))
            link(V.tensor_copy(r.more[:, 0:OVB + 1], ove[:]))
            link(V.tensor_copy(r.gshift[:, 0:T, :], g4[1][:]))
            link(V.tensor_copy(r.eshift[:, 0:T], wt[:, :, 0]))


def route_weights(nc, c, layer, t0, r):
    T = NT - t0
    with Scope(nc, f"rw{layer}") as s:
        gs = s.sb("gs", [P, T])
        ex = s.sb("ex", [P, T])
        exp_done, chain = s.sem("exp_done"), s.sem("chain")
        block = s.block()

        @block.scalar
        def _(act):
            nc.scalar.activation(r.gshift[:, 0:T, :], r.gshift[:, 0:T, :], ACT.Exp).then_inc(exp_done, 1)
            nc.scalar.activation(ex[:], r.eshift[:, 0:T], ACT.Exp).then_inc(exp_done, 1)

        @block.vector
        def _(dve):
            link = Chain(dve, chain)
            V = nc.vector
            dve.wait_ge(exp_done, 2)
            link(V.tensor_reduce(gs[:], r.gshift[:, 0:T, :], AX, ALU.add))
            link(V.scalar_tensor_tensor(out=gs[:], in0=ex[:], scalar=1.0, in1=gs[:], op0=ALU.add, op1=ALU.mult))
            link(V.reciprocal(r.w[:, 0, 0:T], gs[:]))
            link(V.tensor_tensor(r.w[:, 1, 0:T], r.w[:, 0, 0:T], ex[:], ALU.mult))


def experts(nc, c, a, layer, t0, r):
    with Scope(nc, f"exp{layer}") as s:
        S = 2
        wg = [s.sb(f"wg{i}", [P, KD, HID]) for i in range(S)]
        wu = [s.sb(f"wu{i}", [P, KD, HID]) for i in range(S)]
        wd = [s.sb(f"wd{i}", [P, HT_N, DM]) for i in range(S)]
        idx = s.sb("idx", [P, S], I32)
        spare = s.sb("spare", [1, 1])
        xg = [s.sb(f"xg{i}", [P, DM]) for i in range(S)]
        xT = [s.sb(f"xT{i}", [P, KD, P]) for i in range(S)]
        sg = s.sb("sg", [P, HID])
        h = s.sb("h", [P, HID])
        hT = s.sb("hT", [P, HT_N, P])
        y = [s.sb(f"y{i}", [P, DM]) for i in range(S)]
        xps = [s.ps(f"xps{i}", [P, 4, P]) for i in range(2)]
        gps, ups = s.ps("gps", [P, HID]), s.ps("ups", [P, HID])
        hps = s.ps("hps", [P, HT_N, P])
        yps = [s.ps(f"yps{i}", [P, 512]) for i in range(2)]
        gu_ready = [s.sem(f"gu_ready{i}") for i in range(S)]
        wd_ready = [s.sem(f"wd_ready{i}") for i in range(S)]
        x_ready = [s.sem(f"x_ready{i}") for i in range(S)]
        y_free = [s.sem(f"y_free{i}") for i in range(S)]
        (gu_free, wd_free, idx_done, xg_free, xt_act, xt_dve, xtr, gu_done, sg_done, h_done, htr, ht_done,
         down, y_act, y_dve) = (s.sem(n) for n in (
             "gu_free", "wd_free", "idx_done", "xg_free", "xt_act", "xt_dve", "xtr", "gu_done", "sg_done",
             "h_done", "htr", "ht_done", "down", "y_act", "y_dve"))
        block = s.block()
        LOOPS = E // S
        wg_e = a["moe_w_gate"][layer].rearrange("e (k p) n -> e p k n", p=P)
        wu_e = a["moe_w_up"][layer].rearrange("e (k p) n -> e p k n", p=P)
        wd_e = a["moe_w_down"][layer].rearrange("e (k p) n -> e p k n", p=P)
        ys = c.ys.rearrange("(b p) n -> b p n", p=P)

        @block.sync
        def _(sp):
            with sp.Fori(0, LOOPS) as i:
                for q in range(S):
                    sp.wait_ge(gu_free, i * S + q + 1)
                    sp.dma_start(wg[q][:], wg_e[bass.ds(i * S + q, 1)].rearrange("o p k n -> (o p) k n")).then_inc(gu_ready[q], 16)
                    sp.dma_start(wu[q][:], wu_e[bass.ds(i * S + q, 1)].rearrange("o p k n -> (o p) k n")).then_inc(gu_ready[q], 16)
                    sp.wait_ge(wd_free, i * S + q + 1)
                    sp.dma_start(wd[q][:], wd_e[bass.ds(i * S + q, 1)].rearrange("o p k n -> (o p) k n")).then_inc(wd_ready[q], 16)

        @block.gpsimd
        def _(pool):
            nc.gpsimd.memset(spare[:], 0.0)
            with pool.Fori(0, LOOPS) as i:
                for q in range(S):
                    pool.wait_ge(xg_free, i * S + q + 1)
                    nc.gpsimd.tensor_copy(idx[:, q:q + 1], r.tok[:, bass.ds(i * S + q, 1)]).then_inc(idx_done, 1)
                    pool.wait_ge(idx_done, i * S + q + 1)
                    nc.gpsimd.tensor_tensor(spare[:], spare[:], spare[:], ALU.add)
                    nc.gpsimd.indirect_dma_start(xg[q][:], None, c.h_rows[:, :],
                                                 bass.IndirectOffsetOnAxis(idx[:, q:q + 1], 0)).then_inc(x_ready[q], 16)

        @block.tensor
        def _(pe):
            pe.sem_inc(gu_free, S)
            pe.sem_inc(wd_free, S)
            pe.sem_inc(xg_free, S)
            with pe.Fori(0, LOOPS) as i:
                for q in range(S):
                    n = i * S + q
                    pe.wait_ge(x_ready[q], i * 16 + 16)
                    pe.wait_ge(xt_act, n + 1)
                    for k in range(4):
                        nc.tensor.transpose(xps[0][:, k, :], xg[q][:, k * P:(k + 1) * P], c.ident[:])
                    pe.wait_ge(xt_dve, n + 1)
                    for k in range(4, 8):
                        last = nc.tensor.transpose(xps[1][:, k - 4, :], xg[q][:, k * P:(k + 1) * P], c.ident[:])
                    last.then_inc(xtr, 1)
                    pe.wait_ge(gu_ready[q], i * 32 + 32)
                    pe.wait_ge(xt_act, n + 2)
                    pe.wait_ge(xt_dve, n + 2)
                    pe.wait_ge(sg_done, n + 1)
                    for k in range(KD):
                        last = nc.tensor.matmul(gps[:], xT[q][:, k, :], wg[q][:, k, :], start=(k == 0), stop=(k == KD - 1))
                    last.then_inc(gu_done, 1)
                    pe.wait_ge(h_done, n + 1)
                    for k in range(KD):
                        last = nc.tensor.matmul(ups[:], xT[q][:, k, :], wu[q][:, k, :], start=(k == 0), stop=(k == KD - 1))
                    last.then_inc(gu_free, 1)
                    pe.wait_ge(h_done, n + 2)
                    pe.wait_ge(ht_done, n + 1)
                    for k in range(HT_N):
                        last = nc.tensor.transpose(hps[:, k, :], h[:, k * P:(k + 1) * P], c.ident[:])
                    last.then_inc(htr, 1)
                    pe.wait_ge(wd_ready[q], i * 16 + 16)
                    pe.wait_ge(ht_done, n + 2)
                    pe.wait_ge(y_act, n + 1)
                    for k in range(HT_N):
                        last = nc.tensor.matmul(yps[0][:], hT[:, k, :], wd[q][:, k, 0:512], start=(k == 0), stop=(k == HT_N - 1))
                    last.then_inc(down, 1)
                    pe.wait_ge(y_dve, n + 1)
                    for k in range(HT_N):
                        last = nc.tensor.matmul(yps[1][:], hT[:, k, :], wd[q][:, k, 512:1024], start=(k == 0), stop=(k == HT_N - 1))
                    last.then_inc(wd_free, 1)

        @block.scalar
        def _(act):
            act.sem_inc(xt_act, 1)
            act.sem_inc(sg_done, 1)
            act.sem_inc(y_act, 1)
            for q in range(S):
                act.sem_inc(y_free[q], 16)
            with act.Fori(0, LOOPS) as i:
                for q in range(S):
                    n = i * S + q
                    act.wait_ge(xtr, n + 1)
                    nc.scalar.copy(xT[q][:, 0:4, :], xps[0][:]).then_inc(xt_act, 1)
                    act.wait_ge(gu_done, n + 1)
                    act.wait_ge(h_done, n + 1)
                    nc.scalar.activation(sg[:], gps[:], ACT.Silu).then_inc(sg_done, 1)
                    act.wait_ge(down, n + 1)
                    act.wait_ge(y_free[q], i * 16 + 16)
                    nc.scalar.copy(y[q][:, 0:512], yps[0][:]).then_inc(y_act, 1)
                    act.wait_ge(y_act, n + 2)
                    act.wait_ge(y_dve, n + 2)
                    act.dma_start(ys[bass.ds(n, 1)].rearrange("o p n -> (o p) n"), y[q][:]).then_inc(y_free[q], 16)
            for q in range(S):
                act.wait_ge(y_free[q], 16 * (LOOPS + 1))

        @block.vector
        def _(dve):
            dve.sem_inc(xt_dve, 1)
            dve.sem_inc(h_done, 1)
            dve.sem_inc(ht_done, 1)
            dve.sem_inc(y_dve, 1)
            with dve.Fori(0, LOOPS) as i:
                for q in range(S):
                    n = i * S + q
                    dve.wait_ge(xtr, n + 1)
                    dve.sem_inc(xg_free, 1)
                    nc.vector.tensor_copy(xT[q][:, 4:8, :], xps[1][:]).then_inc(xt_dve, 1)
                    dve.wait_ge(sg_done, n + 2)
                    dve.wait_ge(gu_free, n + S + 1)
                    nc.vector.tensor_tensor(h[:], sg[:], ups[:], ALU.mult).then_inc(h_done, 1)
                    dve.wait_ge(htr, n + 1)
                    nc.vector.tensor_copy(hT[:], hps[:]).then_inc(ht_done, 1)
                    dve.wait_ge(wd_free, n + S + 1)
                    dve.wait_ge(y_free[q], i * 16 + 16)
                    nc.vector.tensor_copy(y[q][:, 512:1024], yps[1][:]).then_inc(y_dve, 1)


def further_blocks(nc, c, a, layer, t0, r):
    T = NT - t0
    OVB = T * 2 - 1
    with Scope(nc, f"more{layer}") as s:
        wg, wu = s.sb("wg", [P, KD, HID]), s.sb("wu", [P, KD, HID])
        wd = s.sb("wd", [P, HT_N, DM])
        idx = s.sb("idx", [P, 1], I32)
        spare = s.sb("spare", [1, 1])
        xg = s.sb("xg", [P, DM])
        xT = s.sb("xT", [P, KD, P])
        sg, h = s.sb("sg", [P, HID]), s.sb("h", [P, HID])
        hT = s.sb("hT", [P, HT_N, P])
        y = s.sb("y", [P, DM])
        xps = s.ps("xps", [P, KD, P])
        gps, ups = s.ps("gps", [P, HID]), s.ps("ups", [P, HID])
        hps = s.ps("hps", [P, HT_N, P])
        yps = s.ps("yps", [P, DM])
        w_ready, idx_done, x_ready, xtr, xt, gu, sg_done, h_done, htr, ht, down, y_done, stored = (
            s.sem(n) for n in ("w_ready", "idx_done", "x_ready", "xtr", "xt", "gu", "sg_done", "h_done",
                               "htr", "ht", "down", "y_done", "stored"))
        block = s.block()
        wg_e = a["moe_w_gate"][layer].rearrange("e (k p) n -> e p k n", p=P)
        wu_e = a["moe_w_up"][layer].rearrange("e (k p) n -> e p k n", p=P)
        wd_e = a["moe_w_down"][layer].rearrange("e (k p) n -> e p k n", p=P)
        ys = c.ys.rearrange("(b p) n -> b p n", p=P)

        def asked(eng):
            return eng.value_load(r.more[0:1, OVB:OVB + 1], min_val=0, max_val=OVB)

        @block.sync
        def _(sp):
            num = asked(sp)
            with sp.Fori(0, OVB) as b:
                with sp.If(b < num):
                    e = sp.value_load(r.more[0:1, bass.ds(b, 1)], min_val=0, max_val=E - 1)
                    sp.dma_start(wg[:], wg_e[bass.ds(e, 1)].rearrange("o p k n -> (o p) k n")).then_inc(w_ready, 16)
                    sp.dma_start(wu[:], wu_e[bass.ds(e, 1)].rearrange("o p k n -> (o p) k n")).then_inc(w_ready, 16)
                    sp.dma_start(wd[:], wd_e[bass.ds(e, 1)].rearrange("o p k n -> (o p) k n")).then_inc(w_ready, 16)
                    sp.wait_ge(y_done, b + 1)
                    sp.dma_start(ys[bass.ds(b + E, 1)].rearrange("o p n -> (o p) n"), y[:]).then_inc(stored, 16)

        @block.gpsimd
        def _(pool):
            num = asked(pool)
            nc.gpsimd.memset(spare[:], 0.0)
            with pool.Fori(0, OVB) as b:
                with pool.If(b < num):
                    nc.gpsimd.tensor_copy(idx[:], r.tok[:, bass.ds(b + E, 1)]).then_inc(idx_done, 1)
                    pool.wait_ge(idx_done, b + 1)
                    nc.gpsimd.tensor_tensor(spare[:], spare[:], spare[:], ALU.add)
                    nc.gpsimd.indirect_dma_start(xg[:], None, c.h_rows[:, :],
                                                 bass.IndirectOffsetOnAxis(idx[:], 0)).then_inc(x_ready, 16)
                    pool.wait_ge(stored, b * 16 + 16)

        @block.tensor
        def _(pe):
            num = asked(pe)
            with pe.Fori(0, OVB) as b:
                with pe.If(b < num):
                    pe.wait_ge(x_ready, b * 16 + 16)
                    for k in range(KD):
                        last = nc.tensor.transpose(xps[:, k, :], xg[:, k * P:(k + 1) * P], c.ident[:])
                    last.then_inc(xtr, 1)
                    pe.wait_ge(w_ready, b * 48 + 48)
                    pe.wait_ge(xt, b + 1)
                    for k in range(KD):
                        nc.tensor.matmul(gps[:], xT[:, k, :], wg[:, k, :], start=(k == 0), stop=(k == KD - 1))
                    for k in range(KD):
                        last = nc.tensor.matmul(ups[:], xT[:, k, :], wu[:, k, :], start=(k == 0), stop=(k == KD - 1))
                    last.then_inc(gu, 1)
                    pe.wait_ge(h_done, b + 1)
                    for k in range(HT_N):
                        last = nc.tensor.transpose(hps[:, k, :], h[:, k * P:(k + 1) * P], c.ident[:])
                    last.then_inc(htr, 1)
                    pe.wait_ge(ht, b + 1)
                    for half in range(2):
                        for k in range(HT_N):
                            last = nc.tensor.matmul(yps[:, half * 512:(half + 1) * 512], hT[:, k, :],
                                                    wd[:, k, half * 512:(half + 1) * 512],
                                                    start=(k == 0), stop=(k == HT_N - 1))
                    last.then_inc(down, 1)

        @block.scalar
        def _(act):
            num = asked(act)
            with act.Fori(0, OVB) as b:
                with act.If(b < num):
                    act.wait_ge(gu, b + 1)
                    nc.scalar.activation(sg[:], gps[:], ACT.Silu).then_inc(sg_done, 1)

        @block.vector
        def _(dve):
            num = asked(dve)
            with dve.Fori(0, OVB) as b:
                with dve.If(b < num):
                    dve.wait_ge(xtr, b + 1)
                    nc.vector.tensor_copy(xT[:], xps[:]).then_inc(xt, 1)
                    dve.wait_ge(sg_done, b + 1)
                    nc.vector.tensor_tensor(h[:], sg[:], ups[:], ALU.mult).then_inc(h_done, 1)
                    dve.wait_ge(htr, b + 1)
                    nc.vector.tensor_copy(hT[:], hps[:]).then_inc(ht, 1)
                    dve.wait_ge(down, b + 1)
                    nc.vector.tensor_copy(y[:], yps[:]).then_inc(y_done, 1)


def combine(nc, c, layer, t0, mb, r):
    T = NT - t0
    with Scope(nc, f"comb{layer}") as s:
        y = [[s.sb(f"y{b}{k}", [P, DM]) for k in range(2)] for b in range(2)]
        got = [s.sem(f"got{b}") for b in range(2)]
        used, chain = s.sem("used"), s.sem("chain")
        block = s.block()

        @block.gpsimd
        def _(pool):
            for t in range(T):
                if t >= 2:
                    pool.wait_ge(used, t - 1)
                for k in range(2):
                    nc.gpsimd.indirect_dma_start(y[t % 2][k][:], None, c.ys[:, :],
                                                 bass.IndirectOffsetOnAxis(r.slot[:, k * T + t:k * T + t + 1], 0)
                                                 ).then_inc(got[t % 2], 16)

        @block.vector
        def _(dve):
            link = Chain(dve, chain)
            V = nc.vector
            for t in range(T):
                st = 1 if t0 + t < CT else 0
                y0, y1 = y[t % 2]
                dve.wait_ge(got[t % 2], 32 * (t // 2 + 1))
                link(V.tensor_scalar(y0[:], y0[:], r.w[:, 0, t:t + 1], None, ALU.mult))
                link(V.scalar_tensor_tensor(out=y0[:], in0=y1[:], scalar=r.w[:, 1, t:t + 1], in1=y0[:],
                                            op0=ALU.mult, op1=ALU.add))
                link(V.tensor_tensor(y0[:], y0[:], mb[:, st, 2, :], ALU.mult))
                V.tensor_tensor(c.X[:, t0 + t, :], c.X[:, t0 + t, :], y0[:], ALU.add).then_inc(used, 1)
            dve.wait_ge(used, T)


def moe(nc, c, a, layer, t0):
    with Scope(nc, f"moe{layer}") as s:
        mb = s.sb("mb", [P, 2, 3, DM])
        r = Box()
        r.slot = s.sb("slot", [P, 2 * NT], I32)
        r.tok = s.sb("tok", [P, E + 2 * NT], I32)
        r.more = s.sb("more", [P, 2 * NT], I32)
        r.gshift = s.sb("gshift", [P, NT, G])
        r.eshift = s.sb("eshift", [P, NT])
        r.w = s.sb("w", [P, 2, NT])
        with Scope(nc, f"moeh{layer}") as s2:
            hT = s2.sb("hT", [P, KD, TOK])
            norm_modulate(nc, c, a, layer, 1, t0, hT, mb, c.h_rows)
            routing(nc, c, a, layer, t0, hT, r)
        route_weights(nc, c, layer, t0, r)
        experts(nc, c, a, layer, t0, r)
        further_blocks(nc, c, a, layer, t0, r)
        combine(nc, c, layer, t0, mb, r)


class Box:
    pass


def final_norm(nc, c, a, out):
    with Scope(nc, "final") as s:
        T = NT - CT
        g = s.sb("g", [P, DM])
        junk = s.sb("junk", [P, DM])
        o = s.sb("o", [P, T, DM])
        ms, eps = s.sb("ms", [P, T]), s.sb("eps", [P, 1])
        rstd, root, tmp = (s.sb(n, [P, T]) for n in ("rstd", "root", "tmp"))
        g_ready, sq_done, sqrt_done, eps_ready, chain, o_done, stored = (
            s.sem(n) for n in ("g_ready", "sq_done", "sqrt_done", "eps_ready", "chain", "o_done", "stored"))
        block = s.block()

        @block.sync
        def _(sp):
            sp.dma_start(g[:], a["final_norm_g"].rearrange("(o n) -> o n", o=1).to_broadcast([P, DM])).then_inc(g_ready, 16)
            for t in range(T):
                sp.wait_ge(o_done, t + 1)
                sp.dma_start(out[0, t * P:(t + 1) * P, :], o[:, t, :]).then_inc(stored, 16)
            sp.wait_ge(stored, 16 * T)

        @block.scalar
        def _(act):
            act.wait_ge(eps_ready, 1)
            for t in range(T):
                nc.scalar.activation(junk[:], c.X[:, CT + t, :], ACT.Square, accum_out=ms[:, t:t + 1]).then_inc(sq_done, 1)
                act.wait_ge(sq_done, t + 1)
            nc.scalar.activation(root[:], ms[:], ACT.Sqrt, scale=1.0 / DM, bias=eps[:]).then_inc(sqrt_done, 1)

        @block.vector
        def _(dve):
            link = Chain(dve, chain)
            nc.vector.memset(eps[:], EPS).then_inc(eps_ready, 1)
            dve.wait_ge(g_ready, 16)
            dve.wait_ge(sqrt_done, 1)
            refined_rsqrt(nc, link, rstd[:], root[:], ms[:], tmp[:])
            for t in range(T):
                nc.vector.scalar_tensor_tensor(out=o[:, t, :], in0=c.X[:, CT + t, :], scalar=rstd[:, t:t + 1],
                                               in1=g[:], op0=ALU.mult, op1=ALU.mult).then_inc(o_done, 1)


def backbone(nc, a, out, only=None):
    c = Box()
    c.mods = nc.dram_tensor("mods", (2, DEPTH, 6 * DM), F32, kind="Internal").ap()
    c.h_rows = nc.dram_tensor("h_rows", (TOK, DM), F32, kind="Internal").ap()
    slots = (E + 2 * NT - 1) * P
    c.slot_tok = nc.dram_tensor("slot_tok", (slots, 1), I32, kind="Internal").ap()
    c.ys = nc.dram_tensor("ys", (slots, DM), F32, kind="Internal").ap()
    with Scope(nc, "all") as s:
        c.X = s.sb("X", [P, NT, DM])
        c.ident, c.ones, c.before = (s.sb(n, [P, P]) for n in ("ident", "ones", "before"))
        c.x_ready = s.sem("x_ready")
        constants(nc, c)
        with Scope(nc, "rows") as z:
            c.zero_row = z.sb("zero_row", [P, DM])
            c.rows_clear = z.sem("rows_clear")
            clear_further_rows(nc, c)
        adaln(nc, c, a)
        if only is None or "ab" in only:
            ab_layer(nc, c, a)
        if only is None or "moe0" in only:
            moe(nc, c, a, 0, 0)
        if only is None or "mla" in only:
            mla_layer(nc, c, a)
        if only is None or "moe1" in only:
            moe(nc, c, a, 1, CT)
        final_norm(nc, c, a, out)


_INS = ['x', 'c', 'ctx', 'c_ctx', 'ada_w', 'ada_b', 'norm_g', 'ab_w_in', 'ab_w_out', 'ret_decay_logit',
        'lru_conv_w', 'lru_conv_b', 'lru_gate_w', 'lru_gate_b', 'lru_lambda', 'mla_w_in', 'mla_q_norm_g',
        'mla_kv_norm_g', 'mla_w_uq', 'mla_w_ukv', 'mla_w_out', 'moe_group_w', 'moe_group_b', 'moe_expert_w',
        'moe_expert_b', 'moe_w_gate', 'moe_w_up', 'moe_w_down', 'final_norm_g']


def rope_tables():
    t = np.arange(SEQ, dtype=np.float32)
    inv1 = np.float32(ROPE_BASE) ** (-np.arange(0, RD, 2, dtype=np.float32) / np.float32(RD))
    ang1 = t[:, None] * inv1[None, :]
    ax = ROPE // 2
    inv2 = np.float32(ROPE_BASE) ** (-np.arange(0, ax, 2, dtype=np.float32) / np.float32(ax))
    r_pos = np.repeat(np.arange(SEQ // GRID_W, dtype=np.float32), GRID_W)
    c_pos = np.tile(np.arange(GRID_W, dtype=np.float32), SEQ // GRID_W)
    ang2 = np.concatenate([r_pos[:, None] * inv2[None, :], c_pos[:, None] * inv2[None, :]], axis=-1)

    def laid(ang):
        both = np.stack([np.cos(ang), np.sin(ang)]).astype(np.float32)
        return np.ascontiguousarray(both.reshape(2, SEQ // P, P, -1).transpose(2, 0, 1, 3))

    return {"ret_cs": laid(ang1), "mla_cs": laid(ang2)}


def kernel(**inputs):
    import concourse.bacc as bacc
    from concourse.bass_utils import run_bass_kernel_spmd as run

    nc = bacc.Bacc("TRN2", target_bir_lowering=False, num_devices=1)
    arrays, args = {}, {}
    for name in _INS:
        v = np.ascontiguousarray(inputs[name])
        arrays[f"in_{name}"] = v
        args[name] = nc.dram_tensor(f"in_{name}", v.shape, mybir.dt.from_np(v.dtype), kind="ExternalInput").ap()
    for name, v in rope_tables().items():
        arrays[f"in_{name}"] = v
        args[name] = nc.dram_tensor(f"in_{name}", v.shape, F32, kind="ExternalInput").ap()
    out = nc.dram_tensor("out", (1, SEQ, DM), F32, kind="ExternalOutput").ap()
    backbone(nc, args, out)
    return run(nc, [arrays], core_ids=[0]).results[0]["out"]
```

```python
import math
from contextlib import ExitStack

import numpy as np

import concourse.bass as bass
from concourse import mybir

F32 = mybir.dt.float32
I32 = mybir.dt.int32
ALU = mybir.AluOpType
ACT = mybir.ActivationFunctionType
AX = mybir.AxisListType.X

P = 128
DM = 1024
SEQ = 512
CTX = 256
TOK = CTX + SEQ
DEPTH = 2
KD = DM // P
CT = CTX // P
NT = TOK // P
EPS = 1e-6
ROPE_BASE = 10000.0
GRID_W = 64

RH, RD = 4, 128
LW = 512
LT = LW // P
LB = 64
CONV = 4
LRU_C = 8.0
QK = RH * RD

AH, NOPE, ROPE, VD = 16, 64, 32, 64
QR, KVR = 384, 256
MLA_SCALE = (NOPE + ROPE) ** -0.5

G, EPG = 4, 8
E = G * EPG
HID = 512
HT_N = HID // P
CAP = P
ROUTES = G + E
BLOCKS = E + 2 * NT - 1


class Chain:

    def __init__(self, eng, sem, base=0):
        self.eng, self.sem, self.n = eng, sem, base

    def __call__(self, ins):
        self.n += 1
        ins.then_inc(self.sem, 1)
        self.eng.wait_ge(self.sem, self.n)


class Scope:

    def __init__(self, nc, tag):
        self.nc, self.tag, self.stack, self.sems = nc, tag, ExitStack(), []

    def __enter__(self):
        self.stack.__enter__()
        return self

    def __exit__(self, *a):
        self.stack.__exit__(*a)
        if self.sems and a[0] is None:
            self.nc.clear_and_free_semaphores(self.sems)
            self.nc.all_engine_barrier()

    def sb(self, name, shape, dt=F32):
        return self.stack.enter_context(self.nc.sbuf_tensor(f"{self.tag}_{name}", shape, dt))

    def ps(self, name, shape, dt=F32):
        return self.stack.enter_context(self.nc.psum_tensor(f"{self.tag}_{name}", shape, dt))

    def sem(self, name):
        self.sems.append(self.nc.alloc_semaphore(f"{self.tag}_{name}"))
        return self.sems[-1]

    def block(self):
        return self.stack.enter_context(self.nc.Block())


def refined_rsqrt(nc, link, rstd, root, ms, tmp):
    V = nc.vector
    link(V.reciprocal(rstd, root))
    link(V.tensor_scalar(ms, ms, 1.0 / DM, EPS, ALU.mult, ALU.add))
    link(V.tensor_tensor(tmp, rstd, rstd, ALU.mult))
    link(V.tensor_tensor(tmp, tmp, ms, ALU.mult))
    link(V.tensor_scalar(tmp, tmp, -0.5, 1.5, ALU.mult, ALU.add))
    link(V.tensor_tensor(rstd, rstd, tmp, ALU.mult))


def constants(nc, c):
    with Scope(nc, "const") as s:
        zeroed, made = s.sem("zeroed"), s.sem("made")
        block = s.block()

        @block.gpsimd
        def _(pool):
            nc.gpsimd.memset(c.ident[:], 0.0).then_inc(zeroed, 1)
            nc.gpsimd.memset(c.ones[:], 1.0).then_inc(zeroed, 1)
            pool.wait_ge(zeroed, 2)
            nc.gpsimd.affine_select(out=c.ident[:], in_=c.ident[:], compare_op=ALU.not_equal, fill=1.0,
                                    base=0, pattern=[[-1, P]], channel_multiplier=1).then_inc(made, 1)
            nc.gpsimd.affine_select(out=c.before[:], in_=c.ones[:], compare_op=ALU.is_gt, fill=0.0,
                                    base=0, pattern=[[1, P]], channel_multiplier=-1).then_inc(made, 1)
            pool.wait_ge(made, 2)


def adaln(nc, c, a, k):
    NB = 6 * DM // 512
    R = NB // 4
    ROUNDS = DEPTH * R
    FIRST = -(-3 * DM // 2048)
    HK = KD // 2
    WB = 3
    with Scope(nc, "ada") as s:
        w = [s.sb(f"w{i}", [P, HK, 4 * 512]) for i in range(WB)]
        craw = s.sb("craw", [P, 2, KD])
        sT = s.sb("sT", [P, KD, 32])
        bias = s.sb("bias", [P, ROUNDS, 512])
        mod = bias
        ps = [s.ps(f"ps{i}", [P, 512]) for i in range(2)]
        w_ready = [s.sem(f"w_ready{i}") for i in range(WB)]
        c_ready, b_ready, zeroed, silu_done = (s.sem(n) for n in ("c_ready", "b_ready", "zeroed", "silu_done"))
        w_used, mm_done, mod_done, stored, first_stored, chain = (
            s.sem(n) for n in ("w_used", "mm_done", "mod_done", "stored", "first_stored", "norm_chain"))
        tables = small_tables(nc, a, k, s)
        norm = NormModulate(nc, c, a, s, 0, 0, 0, lambda eng, t: eng.wait_ge(c.x_ready, 16 * NT), pairs=2)
        block = s.block()

        def store_mods(eng, l, r0, r1, sem):
            for st in range(2):
                eng.dma_start(c.mods[st, l].rearrange("(r j n) -> j r n", j=4, n=512)[:, r0:r1],
                              mod[st:P:32, l * R + r0:l * R + r1, :]).then_inc(sem, 16)

        @block.sync
        def _(sp):
            tables.sync(sp)
            norm.load_gains(sp)
            for m in range(2 * ROUNDS):
                l, r = divmod(m // 2, R)
                if m >= WB:
                    sp.wait_ge(w_used, m - WB + 1)
                sp.dma_start(w[m % WB][:], a["ada_w"][l, :, r * 2048:(r + 1) * 2048]
                             .rearrange("(p k) n -> p k n", k=KD)[:, (m % 2) * HK:(m % 2 + 1) * HK, :]
                             ).then_inc(w_ready[m % WB], 16)
            sp.wait_ge(mod_done, ROUNDS)
            store_mods(sp, 0, FIRST, R, stored)
            for l in range(1, DEPTH):
                store_mods(sp, l, 0, R, stored)
            sp.wait_ge(stored, 16 * 2 * DEPTH)

        @block.gpsimd
        def _(pool):
            nc.gpsimd.memset(bias[:], 0.0).then_inc(zeroed, 1)
            nc.gpsimd.memset(sT[:], 0.0).then_inc(zeroed, 1)
            tables.gpsimd(pool)
            for t in range(NT):
                norm.shift(pool, t)

        @block.scalar
        def _(act):
            act.dma_start(craw[:, 0, :], a["c"][0].rearrange("(p k) -> p k", k=KD)).then_inc(c_ready, 16)
            act.dma_start(craw[:, 1, :], a["c_ctx"].rearrange("(p k) -> p k", k=KD)).then_inc(c_ready, 16)
            for t in range(CT):
                act.dma_start(c.X[:, t, :], a["ctx"][0, t * P:(t + 1) * P, :]).then_inc(c.x_ready, 16)
            for t in range(CT, NT):
                act.dma_start(c.X[:, t, :], a["x"][0, (t - CT) * P:(t - CT + 1) * P, :]).then_inc(c.x_ready, 16)
            act.wait_ge(zeroed, 2)
            for st in range(2):
                for l in range(DEPTH):
                    act.dma_start(bias[st:P:32, l * R:(l + 1) * R, :],
                                  a["ada_b"][l].rearrange("(r j n) -> j r n", j=4, n=512)).then_inc(b_ready, 16)
            act.wait_ge(c_ready, 32)
            nc.scalar.activation(sT[:, :, 0:2], craw[:].rearrange("p s k -> p k s"), ACT.Silu).then_inc(silu_done, 1)
            tables.scalar(act)
            for t in range(NT):
                norm.square(act, t)
            act.wait_ge(mod_done, FIRST)
            store_mods(act, 0, 0, FIRST, first_stored)
            act.wait_ge(first_stored, 32)
            norm.load_shift_scale(act)
            for t in range(NT):
                norm.first_half(act, t)

        @block.tensor
        def _(pe):
            norm_tiles = {2 * ROUNDS - 4: (0, 1), 2 * ROUNDS - 3: (2, 3), 2 * ROUNDS - 2: (4,), 2 * ROUNDS - 1: (5,)}
            pe.wait_ge(silu_done, 1)
            for n in range(ROUNDS):
                if n >= 2:
                    pe.wait_ge(mod_done, n - 1)
                for m in (2 * n, 2 * n + 1):
                    pe.wait_ge(w_ready[m % WB], 16 * (m // WB + 1))
                    for kk in range(HK):
                        k_ = (m % 2) * HK + kk
                        for j in range(4):
                            last = nc.tensor.matmul(ps[n % 2][32 * j:32 * j + 32, :], sT[:, k_, :],
                                                    w[m % WB][:, kk, j * 512:(j + 1) * 512],
                                                    start=(k_ == 0), stop=(k_ == KD - 1))
                    last.then_inc(w_used, 1)
                    for t in norm_tiles.get(m, ()):
                        norm.transpose(pe, t)
                pe.wait_ge(w_used, 2 * n + 2)
                pe.sem_inc(mm_done, 1)

        @block.vector
        def _(dve):
            link = Chain(dve, chain)
            nc.vector.memset(norm.eps[:], EPS).then_inc(norm.eps_set, 1)
            tables.vector(dve)
            dve.wait_ge(b_ready, 16 * 2 * DEPTH)
            for n in range(ROUNDS):
                dve.wait_ge(mm_done, n + 1)
                nc.vector.tensor_add(mod[:, n, :], ps[n % 2][:], bias[:, n, :]).then_inc(mod_done, 1)
                if n == FIRST + 1:
                    norm.prepare(dve, eps=False)
                    for t in range(NT):
                        norm.scale(dve, link, t)
                        if t >= 1:
                            norm.second_half(dve, t - 1)
                    norm.second_half(dve, NT - 1)


def carve(space):
    used = [0]

    def piece(_name, shape):
        size = math.prod(shape[1:])
        part = space[:, used[0]:used[0] + size]
        used[0] += size
        if len(shape) == 3:
            return part.rearrange("p (a b) -> p a b", a=shape[1])
        if len(shape) == 4:
            return part.rearrange("p (a b c) -> p a b c", a=shape[1], b=shape[2])
        return part

    return piece


class RowNorm:

    def __init__(self, nc, c, a, s, t0, x_ready, sb):
        self.nc, self.c, self.a, self.t0, self.x_ready, self.T = nc, c, a, t0, x_ready, NT - t0
        T = self.T
        self.g = sb("ng", [P, DM])
        self.junk = sb("njunk", [P, DM])
        self.ms, self.root, self.rstd, self.tmp = (s.sb(n, [P, T]) for n in ("nms", "nroot", "nrstd", "ntmp"))
        self.eps = s.sb("neps", [P, 1])
        self.g_ready, self.eps_set, self.sq_done, self.root_done = (
            s.sem(n) for n in ("norm_g_ready", "norm_eps_set", "norm_sq_done", "norm_root_done"))

    def square(self, act, t):
        nc, col = self.nc, slice(t, t + 1)
        if t == 0:
            act.wait_ge(self.eps_set, 1)
        self.x_ready(act, t)
        nc.scalar.activation(self.junk[:], self.c.X[:, self.t0 + t, :], ACT.Square,
                             accum_out=self.ms[:, col]).then_inc(self.sq_done, 1)
        act.wait_ge(self.sq_done, t + 1)
        nc.scalar.activation(self.root[:, col], self.ms[:, col], ACT.Sqrt, scale=1.0 / DM,
                             bias=self.eps[:]).then_inc(self.root_done, 1)

    def inverse(self, dve, link, t):
        col = slice(t, t + 1)
        dve.wait_ge(self.root_done, t + 1)
        refined_rsqrt(self.nc, link, self.rstd[:, col], self.root[:, col], self.ms[:, col], self.tmp[:, col])


class NormModulate(RowNorm):

    def __init__(self, nc, c, a, s, layer, sub, t0, x_ready, h_out=None, sb=None, hT_free=None,
                 pairs=1, logits=None):
        sb = sb or s.sb
        super().__init__(nc, c, a, s, t0, x_ready, sb)
        self.layer, self.sub, self.h_out, self.hT_free = layer, sub, h_out, hT_free
        self.HB = 2
        self.streams = range(1 if t0 else 2)
        self.mb = sb("nmb", [P, len(self.streams), 2, DM])
        self.h = sb("nh", [P, self.HB, DM])
        self.pairs = pairs
        self.tp = [s.ps(f"ntp{i}", [P, 4, P]) for i in range(2 * pairs)]
        if logits is not None:
            self.lps = logits
            self.rw = sb("nrw", [P, KD, ROUTES])
            self.rb = sb("nrb", [P, ROUTES])
            self.rw_ready, self.lg_done, self.lg_out = (s.sem(n) for n in ("rw_ready", "lg_done", "lg_out"))
        self.m_ready, self.m_done, self.scaled, self.h_done, self.tr_done, self.ev_act, self.ev_dve = (
            s.sem(n) for n in ("norm_m_ready", "norm_m_done", "norm_scaled", "norm_h_done", "norm_tr_done", "norm_ev_act", "norm_ev_dve"))
        self.h_stored = [s.sem(f"norm_h_stored{i}") for i in range(self.HB)]

    def load(self, sp):
        self.load_gains(sp)
        self.load_shift_scale(sp)

    def load_gains(self, sp):
        sp.dma_start(self.g[:], self.a["norm_g"][self.layer, self.sub:self.sub + 1, :]
                     .to_broadcast([P, DM])).then_inc(self.g_ready, 16)

    def load_shift_scale(self, sp):
        for st in self.streams:
            sp.dma_start(self.mb[:, st].rearrange("p r n -> p (r n)"),
                         self.c.mods[st, self.layer:self.layer + 1, self.sub * 3 * DM:(self.sub * 3 + 2) * DM]
                         .to_broadcast([P, 2 * DM])).then_inc(self.m_ready, 16)

    def load_router(self, sp):
        a, layer = self.a, self.layer
        sp.dma_start(self.rw[:, :, 0:G], a["moe_group_w"][layer].rearrange("(k p) n -> p k n", p=P)).then_inc(self.rw_ready, 16)
        sp.dma_start(self.rw[:, :, G:], a["moe_expert_w"][layer].rearrange("(k p) n -> p k n", p=P)).then_inc(self.rw_ready, 16)
        sp.dma_start(self.rb[:, 0:G], a["moe_group_b"][layer:layer + 1, :].to_broadcast([P, G])).then_inc(self.rw_ready, 16)
        sp.dma_start(self.rb[:, G:], a["moe_expert_b"][layer:layer + 1, :].to_broadcast([P, E])).then_inc(self.rw_ready, 16)

    def logits(self, pe, t):
        if t == 0:
            pe.wait_ge(self.rw_ready, 64)
        pe.wait_ge(self.ev_act, t + 1)
        pe.wait_ge(self.ev_dve, t + 1)
        for k in range(KD):
            last = self.nc.tensor.matmul(self.lps[:, t, :], self.c.hT[:, k, t * P:(t + 1) * P], self.rw[:, k, :],
                                         start=(k == 0), stop=(k == KD - 1))
        last.then_inc(self.lg_done, 1)

    def logits_out(self, dve):
        dve.wait_ge(self.rw_ready, 64)
        dve.wait_ge(self.lg_done, self.T)
        self.nc.vector.tensor_tensor(self.c.lg[:, 0:self.T, :], self.lps,
                                     self.rb[:, None, :].to_broadcast([P, self.T, ROUTES]), ALU.add).then_inc(self.lg_out, 1)

    def store(self, sp):
        if self.h_out is None:
            return
        for t in range(self.T):
            sp.wait_ge(self.h_done, t + 1)
            sp.dma_start(self.h_out[(self.t0 + t) * P:(self.t0 + t + 1) * P, :],
                         self.h[:, t % self.HB, :]).then_inc(self.h_stored[t % self.HB], 16)
        for i in range(self.HB):
            sp.wait_ge(self.h_stored[i], 16 * (self.T // self.HB))

    def prepare(self, dve, eps=True):
        V = self.nc.vector
        if eps:
            V.memset(self.eps[:], EPS).then_inc(self.eps_set, 1)
        dve.wait_ge(self.g_ready, 16)
        dve.wait_ge(self.m_ready, 16 * len(self.streams))
        for st in self.streams:
            V.scalar_tensor_tensor(out=self.mb[:, st, 1, :], in0=self.mb[:, st, 1, :], scalar=1.0,
                                   in1=self.g[:], op0=ALU.add, op1=ALU.mult).then_inc(self.m_done, 1)
        dve.wait_ge(self.m_done, len(self.streams))

    def scale(self, dve, link, t):
        self.inverse(dve, link, t)
        st = 1 if self.t0 + t < CT else 0
        if t >= self.HB:
            dve.wait_ge(self.tr_done, 2 * (t - self.HB) + 2)
            if self.h_out is not None:
                dve.wait_ge(self.h_stored[t % self.HB], 16 * (t // self.HB))
        self.nc.vector.scalar_tensor_tensor(out=self.h[:, t % self.HB, :], in0=self.c.X[:, self.t0 + t, :],
                                            scalar=self.rstd[:, t:t + 1], in1=self.mb[:, st, 1, :],
                                            op0=ALU.mult, op1=ALU.mult).then_inc(self.scaled, 1)

    def shift(self, pool, t):
        st = 1 if self.t0 + t < CT else 0
        pool.wait_ge(self.scaled, t + 1)
        h = self.h[:, t % self.HB, :]
        self.nc.gpsimd.tensor_add(h, h, self.mb[:, st, 0, :]).then_inc(self.h_done, 1)

    def bank(self, t, half):
        return self.tp[2 * (t % self.pairs) + half]

    def transpose(self, pe, t):
        pe.wait_ge(self.h_done, t + 1)
        for half in range(2):
            if t >= self.pairs:
                pe.wait_ge(self.ev_dve if half else self.ev_act, t - self.pairs + 1)
            for j in range(4):
                k = 4 * half + j
                last = self.nc.tensor.transpose(self.bank(t, half)[:, j, :], self.h[:, t % self.HB, k * P:(k + 1) * P],
                                                self.c.ident[:])
            last.then_inc(self.tr_done, 1)

    def first_half(self, act, t):
        if t == 0 and self.hT_free:
            self.hT_free(act)
        act.wait_ge(self.tr_done, 2 * t + 1)
        self.nc.scalar.copy(self.c.hT[:, 0:4, t * P:(t + 1) * P], self.bank(t, 0)[:]).then_inc(self.ev_act, 1)

    def second_half(self, eng, t, copy=None):
        if t == 0 and self.hT_free:
            self.hT_free(eng)
        eng.wait_ge(self.tr_done, 2 * t + 2)
        (copy or self.nc.vector.tensor_copy)(self.c.hT[:, 4:8, t * P:(t + 1) * P], self.bank(t, 1)[:]).then_inc(self.ev_dve, 1)


def rms_rows(V, link, rstd, root, ms, tmp, width):
    link(V.reciprocal(rstd, root))
    link(V.tensor_scalar(ms, ms, 1.0 / width, EPS, ALU.mult, ALU.add))
    link(V.tensor_tensor(tmp, rstd, rstd, ALU.mult))
    link(V.tensor_tensor(tmp, tmp, ms, ALU.mult))
    link(V.tensor_scalar(tmp, tmp, -0.5, 1.5, ALU.mult, ALU.add))
    link(V.tensor_tensor(rstd, rstd, tmp, ALU.mult))


PADL, PADR = CONV // 2, (CONV - 1) // 2
U_CTX = PADL
U_LAT = PADL + CTX + PADR + PADL
U_LEN = U_LAT + SEQ + PADR


def ab_project(nc, c, a, k, hT, rows, u, yT):
    with Scope(nc, "abp") as s:
        S = 2
        RB = 4
        w = [s.sb(f"w{i}", [P, KD, 512]) for i in range(S)]
        cw = s.sb("cw", [P, CONV + 1, LT])
        gb = s.sb("gb", [P, 4, LT])
        gw = s.sb("gw", [P, 4, LT, P])
        x = s.sb("x", [P, LT, TOK])
        R, I = ([s.sb(f"{n}{i}", [P, TOK]) for i in range(2)] for n in "ri")
        xc = s.sb("xc", [P, U_LEN])
        q = xc[:, 0:TOK]
        gt = s.sb("gt", [P, TOK])
        n4 = s.sb("n4", [P, 2 * LT])
        zero = s.sb("zero", [P, DM // 4])
        cs = s.sb("cs", [P, 2, NT - CT, RD // 2])
        L2 = (NT - CT) // 2
        t1 = s.sb("t1", [P, L2, RH, RD // 2])
        t2 = gt[:, 0:L2 * RH * RD // 2].rearrange("p (t h n) -> p t h n", t=L2, h=RH)
        cs_ready, rotated = s.sem("cs_ready"), s.sem("rotated")
        ps = [s.ps(f"ps{i}", [P, 512]) for i in range(RB)]
        gps = [s.ps(f"gps{i}", [P, 512]) for i in range(4)]
        w_ready = [s.sem(f"w_ready{i}") for i in range(S)]
        (w_free, mm, ev_act, ev_dve, cleared, z_set, z_stored, p_ready, gw_zero, gw_ready, x_ready, gates, sig,
         n4_done, th, q_in, q_out, unit_done, chain, pchain, y_in, y_out, gelu_done, y_ready) = (s.sem(n) for n in (
             "w_free", "mm", "ev_act", "ev_dve", "cleared", "z_set", "z_stored", "p_ready", "gw_zero", "gw_ready",
             "x_ready", "gates", "sig", "n4_done", "th", "q_in", "q_out", "unit_done", "chain", "pchain", "y_in",
             "y_out", "gelu_done", "y_ready"))
        block = s.block()
        PARTS = ((0, CTX), (CTX, SEQ))
        hs = u
        BLOCKS_IN_ORDER = (4, 5, 0, 1, 2, 3)
        channel_groups = [(b, (ct, o, n)) for b in (4, 5) for ct in range(LT) for o, n in PARTS]
        groups = channel_groups + [(b, t) for b in range(4) for t in range(NT)]
        C = len(channel_groups)
        UNITS = [(d, ct) for d in range(2) for ct in range(LT)]
        BEFORE = [3 + j * (len(groups) - C - 4) // len(UNITS) for j in range(len(UNITS))]

        def copied(i):
            if i < C:
                return (ev_dve, i // 2 + 1) if i % 2 else (ev_act, i // 2 + 1)
            return ev_act, C // 2 + i - C + 1

        def channels_out(copy, i):
            b, (ct, o, n) = groups[i]
            at = (U_LAT if o else U_CTX) if b == 4 else o
            return copy((u if b == 4 else yT)[:, ct, at:at + n], ps[i % RB][:, 0:n])

        @block.sync
        def _(sp):
            def block_of(n):
                b = BLOCKS_IN_ORDER[n]
                sp.dma_start(w[n % S][:], a["ab_w_in"][0, :, b * 512:(b + 1) * 512]
                             .rearrange("(k p) n -> p k n", p=P)).then_inc(w_ready[n % S], 16)

            block_of(0)
            for t in range(CONV):
                sp.dma_start(cw[:, t, :], a["lru_conv_w"][0, t].rearrange("(c p) -> p c", p=P),
                             allow_slow_non_contiguous=True).then_inc(p_ready, 16)
            sp.dma_start(cw[:, CONV, :], a["lru_conv_b"][0].rearrange("(c p) -> p c", p=P),
                         allow_slow_non_contiguous=True).then_inc(p_ready, 16)
            block_of(1)
            sp.dma_start(cs[:], a["ret_cs"]).then_inc(cs_ready, 16)
            for dg in range(4):
                sp.dma_start(gb[:, dg, :], a["lru_gate_b"][0, dg // 2, dg % 2].rearrange("(c p) -> p c", p=P),
                             allow_slow_non_contiguous=True).then_inc(p_ready, 16)
            sp.wait_ge(gw_zero, 1)
            for dg in range(4):
                for half in range(2):
                    src = a["lru_gate_w"][0, dg // 2, dg % 2].rearrange("(c b) i j -> b i c j", b=2)
                    sp.dma_start(gw[half * LB:(half + 1) * LB, dg, :, half * LB:(half + 1) * LB],
                                 src[half]).then_inc(gw_ready, 16)
            for n in range(2, 6):
                sp.wait_ge(w_free, n - S + 1)
                block_of(n)
            sp.wait_ge(z_set, 1)
            for b in range(BLOCKS):
                lo = 0 if b >= E else P // 2
                sp.dma_start(c.ys[b * P + lo:(b + 1) * P, :].rearrange("p (a n) -> p a n", a=4),
                             zero[lo:, None, :].to_broadcast([P - lo, 4, DM // 4])).then_inc(z_stored, 16)
            sp.wait_ge(z_stored, 16 * BLOCKS)

        @block.gpsimd
        def _(pool):
            link = Chain(pool, pchain)
            nc.gpsimd.memset(u[:], 0.0).then_inc(cleared, 1)
            nc.gpsimd.memset(gw[:], 0.0).then_inc(gw_zero, 1)
            nc.gpsimd.memset(zero[:], 0.0).then_inc(z_set, 1)
            pool.wait_ge(y_ready, 1)
            for ct in range(LT):
                y = yT[:, ct, :]
                link(nc.gpsimd.tensor_tensor(gt[:], y, y, ALU.mult))
                link(nc.gpsimd.tensor_scalar(gt[:], gt[:], 0.044715, 1.0, ALU.mult, ALU.add))
                nc.gpsimd.tensor_tensor(gt[:], gt[:], y, ALU.mult).then_inc(y_in, 1)
                pool.wait_ge(y_out, ct + 1)
                link(nc.gpsimd.tensor_scalar(gt[:], gt[:], 0.5, 0.5, ALU.mult, ALU.add))
                nc.gpsimd.tensor_tensor(y, y, gt[:], ALU.mult).then_inc(gelu_done, 1)
                pool.wait_ge(gelu_done, ct + 1)
            pool.wait_ge(cs_ready, 16)
            for n, (b, lo) in enumerate((b, lo) for b in range(2) for lo in (0, L2)):
                pool.wait_ge(*copied(C + (b + 1) * NT - 1))
                x = rows[:, b, CT + lo:CT + lo + L2, :].rearrange("p t (h two n) -> p t h two n", h=RH, two=2)
                x1, x2 = x[:, :, :, 0, :], x[:, :, :, 1, :]
                co, si = (cs[:, i, lo:lo + L2, None, :].to_broadcast([P, L2, RH, RD // 2]) for i in range(2))
                link(nc.gpsimd.tensor_tensor(t1[:], x1, si, ALU.mult))
                link(nc.gpsimd.tensor_tensor(t2, x2, si, ALU.mult))
                link(nc.gpsimd.tensor_tensor(x1, x1, co, ALU.mult))
                link(nc.gpsimd.tensor_tensor(x2, x2, co, ALU.mult))
                link(nc.gpsimd.tensor_tensor(x1, x1, t2, ALU.subtract))
                nc.gpsimd.tensor_tensor(x2, x2, t1[:], ALU.add).then_inc(rotated, 1)
                pool.wait_ge(rotated, n + 1)

        @block.tensor
        def _(pe):
            for i, (b, what) in enumerate(groups):
                n = BLOCKS_IN_ORDER.index(b)
                if i == 0 or groups[i - 1][0] != b:
                    pe.wait_ge(w_ready[n % S], 16 * (n // S + 1))
                if i >= RB:
                    pe.wait_ge(*copied(i - RB))
                for kk in range(KD):
                    if i >= C:
                        last = nc.tensor.matmul(ps[i % RB][:], hT[:, kk, what * P:(what + 1) * P], w[n % S][:, kk, :],
                                                start=(kk == 0), stop=(kk == KD - 1))
                    else:
                        ct, o, m = what
                        last = nc.tensor.matmul(ps[i % RB][:, 0:m], w[n % S][:, kk, ct * P:(ct + 1) * P],
                                                hT[:, kk, o:o + m], start=(kk == 0), stop=(kk == KD - 1))
                last.then_inc(mm, 1)
                if i + 1 == len(groups) or groups[i + 1][0] != b:
                    pe.wait_ge(mm, i + 1)
                    pe.sem_inc(w_free, 1)
                if i - C + 1 in BEFORE:
                    j = BEFORE.index(i - C + 1)
                    d, ct = UNITS[j]
                    if j == 0:
                        pe.wait_ge(gw_ready, 16 * 8)
                    pe.wait_ge(x_ready, ct + 1)
                    pe.wait_ge(sig, 4 * j) if j else None
                    for g in range(2):
                        for e, (o, m) in enumerate(PARTS):
                            last = nc.tensor.matmul(gps[2 * g + e][:, 0:m], gw[:, 2 * d + g, ct, :], x[:, ct, o:o + m],
                                                    start=True, stop=True)
                    last.then_inc(gates, 1)

        @block.scalar
        def _(act):
            act.wait_ge(cleared, 1)
            for i in range(0, C, 2):
                act.wait_ge(mm, i + 1)
                channels_out(nc.scalar.copy, i).then_inc(ev_act, 1)
            act.wait_ge(p_ready, 16 * (CONV + 5))
            act.wait_ge(n4_done, 1)

            def row_groups(lo, hi):
                for i in range(C + lo, C + hi):
                    b, t = groups[i]
                    act.wait_ge(mm, i + 1)
                    if b == 1:
                        nc.scalar.mul(rows[:, b, t, :], ps[i % RB][:], RD ** -0.5).then_inc(ev_act, 1)
                    else:
                        nc.scalar.copy(rows[:, b, t, :], ps[i % RB][:]).then_inc(ev_act, 1)

            for j, (d, ct) in enumerate(UNITS):
                row_groups(BEFORE[j - 1] if j else 0, BEFORE[j])
                act.wait_ge(gates, j + 1)
                if j >= 2:
                    act.wait_ge(unit_done, j - 1)
                for g in range(2):
                    for e, (o, m) in enumerate(PARTS):
                        nc.scalar.activation((R, I)[g][j % 2][:, o:o + m], gps[2 * g + e][:, 0:m], ACT.Sigmoid,
                                             bias=gb[:, 2 * d + g, ct:ct + 1]).then_inc(sig, 1)
                act.wait_ge(sig, 4 * j + 2)
                nc.scalar.activation(R[j % 2][:], R[j % 2][:], ACT.Tanh, scale=n4[:, d * LT + ct:d * LT + ct + 1]).then_inc(th, 1)
                if j < LT:
                    act.wait_ge(y_in, j + 1)
                    nc.scalar.activation(gt[:], gt[:], ACT.Tanh, scale=math.sqrt(2.0 / math.pi)).then_inc(y_out, 1)
                act.wait_ge(q_in, j + 1)
                nc.scalar.activation(q, q, ACT.Sqrt).then_inc(q_out, 1)
            row_groups(BEFORE[-1], len(groups) - C)

        @block.vector
        def _(dve):
            link = Chain(dve, chain)
            V = nc.vector
            W = U_LEN - PADL - PADR
            dve.wait_ge(cleared, 1)
            V.tensor_scalar(n4[:], k.sp[:, 2 * RH:], LRU_C / 2, None, ALU.mult).then_inc(n4_done, 1)
            for i in range(1, C, 2):
                dve.wait_ge(mm, i + 1)
                channels_out(V.tensor_copy, i).then_inc(ev_dve, 1)
            dve.wait_ge(ev_act, C // 2)
            dve.wait_ge(ev_dve, C // 2)
            dve.sem_inc(y_ready, 1)
            dve.wait_ge(p_ready, 16 * (CONV + 5))
            for ct in range(LT):
                link(V.tensor_scalar(xc[:, :W], u[:, ct, 0:W], cw[:, 0, ct:ct + 1],
                                     cw[:, CONV, ct:ct + 1], ALU.mult, ALU.add))
                for t in range(1, CONV):
                    link(V.scalar_tensor_tensor(out=xc[:, :W], in0=u[:, ct, t:t + W], scalar=cw[:, t, ct:ct + 1],
                                                in1=xc[:, :W], op0=ALU.mult, op1=ALU.add))
                link(V.tensor_copy(x[:, ct, 0:CTX], xc[:, 0:CTX]))
                V.tensor_copy(x[:, ct, CTX:], xc[:, U_LAT - PADL:U_LAT - PADL + SEQ]).then_inc(x_ready, 1)
                dve.wait_ge(x_ready, ct + 1)
            for j, (d, ct) in enumerate(UNITS):
                r_, i_ = R[j % 2], I[j % 2]
                dve.wait_ge(sig, 4 * j + 4)
                link(V.tensor_tensor(i_[:], i_[:], x[:, ct, :], ALU.mult))
                dve.wait_ge(th, j + 1)
                link(V.tensor_scalar(q, r_[:], 1.0, None, ALU.add))
                link(V.reciprocal(q, q))
                link(V.scalar_tensor_tensor(out=r_[:], in0=r_[:], scalar=2.0, in1=q, op0=ALU.mult, op1=ALU.mult))
                link(V.tensor_scalar(q, r_[:], -1.0, 2.0, ALU.mult, ALU.add))
                V.tensor_tensor(q, q, r_[:], ALU.mult).then_inc(q_in, 1)
                link(V.tensor_scalar(r_[:], r_[:], -1.0, 1.0, ALU.mult, ALU.add))
                dve.wait_ge(q_out, j + 1)
                link(V.tensor_tensor(i_[:], i_[:], q, ALU.mult))
                if d == 0:
                    V.tensor_tensor_scan(hs[:, ct, 0:TOK], r_[:], i_[:], 0.0, ALU.mult, ALU.add).then_inc(unit_done, 1)
                    dve.wait_ge(unit_done, j + 1)
                    continue
                link(V.tensor_tensor_scan(xc[:, CTX - 1::-1], r_[:, CTX - 1::-1], i_[:, CTX - 1::-1], 0.0, ALU.mult, ALU.add))
                V.tensor_tensor_scan(xc[:, TOK - 1:CTX - 1:-1], r_[:, TOK - 1:CTX - 1:-1],
                                     i_[:, TOK - 1:CTX - 1:-1], xc[:, 0:1], ALU.mult, ALU.add).then_inc(unit_done, 1)
                dve.wait_ge(unit_done, j + 1)
                link(V.tensor_tensor(q, q, hs[:, ct, 0:TOK], ALU.add))
                dve.wait_ge(gelu_done, ct + 1)
                link(V.tensor_tensor(yT[:, ct, :], yT[:, ct, :], q, ALU.mult))


class Bodies:

    def __init__(self, sync, gpsimd, vector, scalar):
        self.sync, self.gpsimd, self.vector, self.scalar = sync, gpsimd, vector, scalar


def small_tables(nc, a, k, s):
    NZ = 2 * RH + 2 * LT
    z, az, e, q, x2, acc = (s.sb(n, [P, NZ]) for n in ("z", "az", "e", "q", "x2", "acc"))
    col = s.sb("col", [P, 2, RH])
    jrow = s.sb("jrow", [P, 2, RD])
    dist = s.sb("dist", [P, 2, P])
    dm = s.sb("dm", [P, 2, RH, P])
    ready, io, e_in, e_out, chain, lg_ready, xi_done, dm_done, dcols = (
        s.sem(n) for n in ("ready", "io", "e_in", "e_out", "chain", "lg_ready", "xi_done", "dm_done", "dcols"))
    masked = s.sem("masked")

    def sync(sp):
        sp.dma_start(z[:, 0:2 * RH], a["ret_decay_logit"].rearrange("o d h -> o (d h)")
                     .to_broadcast([P, 2 * RH])).then_inc(ready, 16)
        for d in range(2):
            sp.dma_start(z[:, 2 * RH + d * LT:2 * RH + (d + 1) * LT],
                         a["lru_lambda"][0, d].rearrange("(c p) -> p c", p=P),
                         allow_slow_non_contiguous=True).then_inc(ready, 16)

    def gpsimd(pool):
        def idx(out, pattern, base, mult):
            nc.gpsimd.iota(out, pattern=pattern, base=base, channel_multiplier=mult,
                           allow_small_or_imprecise_dtypes=True).then_inc(io, 1)

        idx(col[:, 0, :], [[0, RH]], P - 1, -1)
        idx(col[:, 1, :], [[0, RH]], 0, 1)
        idx(jrow[:, 0, :], [[1, RD]], 1, 0)
        idx(jrow[:, 1, :], [[-1, RD]], P, 0)
        idx(dist[:, 0, :], [[1, P]], 0, -1)
        idx(dist[:, 1, :], [[-1, P]], 0, 1)
        pool.wait_ge(dm_done, 2 * RH)
        for d in range(2):
            sign = 1 if d == 0 else -1
            nc.gpsimd.affine_select(out=dm[:, d], in_=dm[:, d], compare_op=ALU.is_ge, fill=0.0, base=0,
                                    pattern=[[0, RH], [sign, P]], channel_multiplier=-sign).then_inc(masked, 1)

    def vector(dve):
        link = Chain(dve, chain)
        V = nc.vector
        dve.wait_ge(ready, 48)
        dve.wait_ge(io, 6)
        link(V.tensor_scalar(z[:], z[:], -1.0, None, ALU.mult))
        link(V.tensor_scalar(az[:], z[:], -1.0, None, ALU.mult))
        link(V.tensor_tensor(az[:], az[:], z[:], ALU.min))
        V.tensor_scalar(z[:], z[:], 0.0, None, ALU.max).then_inc(e_in, 1)
        dve.wait_ge(e_in, 1)
        dve.wait_ge(e_out, 1)
        link(V.tensor_scalar(q[:], e[:], 2.0, None, ALU.add))
        link(V.reciprocal(q[:], q[:]))
        link(V.tensor_tensor(q[:], q[:], e[:], ALU.mult))
        link(V.tensor_tensor(x2[:], q[:], q[:], ALU.mult))
        link(V.tensor_scalar(acc[:], x2[:], 1.0 / 17, 1.0 / 15, ALU.mult, ALU.add))
        for n in (13, 11, 9, 7, 5, 3, 1):
            link(V.tensor_tensor(acc[:], acc[:], x2[:], ALU.mult))
            link(V.tensor_scalar(acc[:], acc[:], 1.0 / n, None, ALU.add))
        link(V.tensor_tensor(acc[:], acc[:], q[:], ALU.mult))
        link(V.scalar_tensor_tensor(out=k.sp[:], in0=acc[:], scalar=2.0, in1=z[:], op0=ALU.mult, op1=ALU.add))
        V.tensor_scalar(k.lg[:], k.sp[:, 0:2 * RH], -1.0, None, ALU.mult).then_inc(lg_ready, 1)
        dve.wait_ge(lg_ready, 1)
        link(V.tensor_scalar(dist[:], dist[:], 0.0, None, ALU.max))
        lg3 = k.lg[:].rearrange("p (d h) -> p d h", d=2)
        link(V.tensor_tensor(k.zeta[:], col[:], lg3, ALU.mult))
        V.tensor_scalar(k.dec[:], lg3, float(P), None, ALU.mult).then_inc(dcols, 1)
        dve.wait_ge(masked, 2)
        link(V.tensor_tensor(k.DT[:], dm[:, 0], dm[:, 1], ALU.add))

    def scalar(act):
        act.wait_ge(e_in, 1)
        nc.scalar.activation(e[:], az[:], ACT.Exp).then_inc(e_out, 1)
        act.wait_ge(dcols, 1)
        nc.scalar.activation(k.zeta[:], k.zeta[:], ACT.Exp).then_inc(xi_done, 1)
        nc.scalar.activation(k.dec[:], k.dec[:], ACT.Exp).then_inc(xi_done, 1)
        for d in range(2):
            for h in range(RH):
                lg = k.lg[:, d * RH + h:d * RH + h + 1]
                nc.scalar.activation(k.XI[:, d, h, :], jrow[:, d, :], ACT.Exp, scale=lg).then_inc(xi_done, 1)
                nc.scalar.activation(dm[:, d, h, :], dist[:, d, :], ACT.Exp, scale=lg).then_inc(dm_done, 1)

    return Bodies(sync, gpsimd, vector, scalar)


def retention(nc, c, a, k, rows, qT, kT, w, w_ready, gate, gate_ready, ms):
    ORDER = (list(range(NT)), list(range(CT))[::-1] + list(range(CT, NT))[::-1])
    with Scope(nc, "ret") as s:
        vz = [s.sb(f"vz{d}", [P, RH, RD]) for d in range(2)]
        st = s.sb("st", [P, 2, NT, RH, RD])
        sT = [s.sb(f"sT{i}", [P, RH, P]) for i in range(2)]
        qx = [[s.sb(f"qx{i}{d}", [P, RH, P]) for d in range(2)] for i in range(2)]
        tq, tk = s.ps("tq", [P, RH, P]), s.ps("tk", [P, RH, P])
        up = [s.ps(f"up{d}", [P, RH, RD]) for d in range(2)]
        sp_ = [s.ps(f"sp{i}", [P, RH, P]) for i in range(2)]
        op = [s.ps(f"op{i}", [P, RH, RD]) for i in range(2)]
        (trq, trk, evq, evk, vz_done, u_done, st_done, sc, sc_ev, o_done, o_ev, qx_done,
         chain, squared, tail) = (s.sem(n) for n in (
             "trq", "trk", "evq", "evk", "vz_done", "u_done", "st_done", "sc",
             "sc_ev", "o_done", "o_ev", "qx_done", "chain", "squared", "tail"))
        block = s.block()
        q_t, k_t, v_t = rows[:, 0], rows[:, 1], rows[:, 2]

        @block.sync
        def _(sp):
            sp.dma_start(w[:], a["ab_w_out"][0].rearrange("(k p) n -> p k n", p=P)).then_inc(w_ready, 16)
            load_gates(sp, c, gate, gate_ready, 0, 0, 2)
            sp.wait_ge(gate_ready, 32)

        @block.gpsimd
        def _(pool):
            for n in range(NT - 1):
                for d in range(2):
                    t = ORDER[d][n]
                    if n >= 1:
                        pool.wait_ge(u_done, 2 * (n - 1) + d + 1)
                    nc.gpsimd.tensor_tensor(vz[d][:], v_t[:, t].rearrange("p (h e) -> p h e", h=RH),
                                            k.zeta[:, d, :, None].to_broadcast([P, RH, RD]), ALU.mult).then_inc(vz_done, 1)
            for t in range(NT):
                pool.wait_ge(o_ev, t + 1)
                nc.gpsimd.tensor_tensor(rows[:, 1, t], rows[:, 0, t], rows[:, 0, t], ALU.mult).then_inc(squared, 1)

        @block.tensor
        def _(pe):
            def transposes(t):
                for x, ps, ev, tr in ((q_t, tq, evq, trq), (k_t, tk, evk, trk)):
                    if t >= 1:
                        pe.wait_ge(ev, t)
                    for h in range(RH):
                        last = nc.tensor.transpose(ps[:, h, :], x[:, t, h * RD:(h + 1) * RD], c.ident[:])
                    last.then_inc(tr, 1)

            for t in range(NT):
                transposes(t)
            for n in range(NT - 1):
                for d in range(2):
                    t = ORDER[d][n]
                    pe.wait_ge(vz_done, 2 * n + d + 1)
                    if n >= 1:
                        pe.wait_ge(st_done, 2 * (n - 1) + d + 1)
                    for h in range(RH):
                        last = nc.tensor.matmul(up[d][:, h, :], k_t[:, t, h * RD:(h + 1) * RD], vz[d][:, h, :],
                                                start=True, stop=True)
                    last.then_inc(u_done, 1)
            pe.wait_ge(evq, NT)
            pe.wait_ge(evk, NT)
            pe.wait_ge(st_done, 2 * (NT - 1))

            def scores(t):
                if t >= 2:
                    pe.wait_ge(sc_ev, t - 1)
                for h in range(RH):
                    last = nc.tensor.matmul(sp_[t % 2][:, h, :], kT[:, h, t * P:(t + 1) * P],
                                            qT[:, h, t * P:(t + 1) * P], start=True, stop=True)
                last.then_inc(sc, 1)

            scores(0)
            for t in range(NT):
                if t + 1 < NT:
                    scores(t + 1)
                pe.wait_ge(sc_ev, t + 1)
                pe.wait_ge(qx_done, 2 * t + 2)
                if t >= 2:
                    pe.wait_ge(o_ev, t - 1)
                for h in range(RH):
                    parts = [(sT[t % 2][:, h, :], v_t[:, t, h * RD:(h + 1) * RD])]
                    parts += [(qx[t % 2][d][:, h, :], st[:, d, t, h, :]) for d in range(2) if t != ORDER[d][0]]
                    for n, (lhs, rhs) in enumerate(parts):
                        last = nc.tensor.matmul(op[t % 2][:, h, :], lhs, rhs, start=(n == 0), stop=(n == len(parts) - 1))
                last.then_inc(o_done, 1)

        @block.scalar
        def _(act):
            for t in range(NT):
                act.wait_ge(trq, t + 1)
                nc.scalar.copy(qT[:, :, t * P:(t + 1) * P], tq[:]).then_inc(evq, 1)
                act.wait_ge(trk, t + 1)
                nc.scalar.copy(kT[:, :, t * P:(t + 1) * P], tk[:]).then_inc(evk, 1)
            nc.scalar.activation(rows[:, 3], rows[:, 3], ACT.Silu).then_inc(tail, 1)
            for t in range(NT):
                act.wait_ge(o_done, t + 1)
                nc.scalar.copy(rows[:, 0, t, :].rearrange("p (h e) -> p h e", h=RH), op[t % 2][:]).then_inc(o_ev, 1)

        @block.vector
        def _(dve):
            link = Chain(dve, chain)
            V = nc.vector

            def sum_squares(t):
                dve.wait_ge(squared, t + 1)
                V.tensor_reduce(ms[:, t * RH:(t + 1) * RH], rows[:, 1, t].rearrange("p (h e) -> p h e", e=RD),
                                AX, ALU.add).then_inc(tail, 1)

            for n in range(NT - 1):
                for d in range(2):
                    t, nxt = ORDER[d][n], ORDER[d][n + 1]
                    dve.wait_ge(u_done, 2 * n + d + 1)
                    if n == 0:
                        V.tensor_copy(st[:, d, nxt], up[d][:]).then_inc(st_done, 1)
                    else:
                        dve.wait_ge(st_done, 2 * n)
                        link(V.tensor_tensor(st[:, d, nxt], st[:, d, t],
                                             k.dec[:, d, :, None].to_broadcast([P, RH, RD]), ALU.mult))
                        V.tensor_tensor(st[:, d, nxt], st[:, d, nxt], up[d][:], ALU.add).then_inc(st_done, 1)
            dve.wait_ge(evq, NT)
            for t in range(NT):
                if t >= 2:
                    dve.wait_ge(o_done, t - 1)
                for d in range(2):
                    V.tensor_tensor(qx[t % 2][d][:], qT[:, :, t * P:(t + 1) * P], k.XI[:, d], ALU.mult).then_inc(qx_done, 1)
                dve.wait_ge(sc, t + 1)
                V.tensor_tensor(sT[t % 2][:], sp_[t % 2][:], k.DT[:], ALU.mult).then_inc(sc_ev, 1)
                if t >= 2:
                    sum_squares(t - 2)
            for t in range(NT - 2, NT):
                sum_squares(t)


def ab_output(nc, c, a, gate, rows, yT, w, w_ready, ms):
    with Scope(nc, "abo") as s:
        rT = rows[:, 2].rearrange("p t n -> p (t n)").rearrange("p (h n) -> p h n", h=RH)
        sg = rows[:, 3]
        tmp = [s.sb(f"tmp{i}", [P, 512]) for i in range(2)]
        root, rstd, tm = (s.sb(n, [P, NT * RH]) for n in ("root", "rstd", "tm"))
        tp = [s.ps(f"tp{i}", [P, RH, P]) for i in range(2)]
        ps = [s.ps(f"ps{i}", [P, 512]) for i in range(4)]
        chain, root_done, r_done, tr, tr_ev, mm, x_done = (
            s.sem(n) for n in ("chain", "root_done", "r_done", "tr", "tr_ev", "mm", "x_done"))
        logits = tp[0][:].rearrange("p h n -> p (h n)")[:, 0:NT * ROUTES].rearrange("p (t n) -> p t n", t=NT)
        norm = NormModulate(nc, c, a, s, 0, 1, 0, lambda eng, t: eng.wait_ge(x_done, 2 * t + 2), c.h_rows,
                            logits=logits)
        block = s.block()
        ret = rows[:, 0]

        @block.sync
        def _(sp):
            norm.load(sp)
            norm.load_router(sp)
            norm.store(sp)

        @block.scalar
        def _(act):
            act.wait_ge(norm.eps_set, 1)
            nc.scalar.activation(root[:], ms[:], ACT.Sqrt, scale=1.0 / RD, bias=norm.eps[:]).then_inc(root_done, 1)
            for t in range(NT):
                act.wait_ge(tr, t + 1)
                nc.scalar.copy(rT[:, :, t * P:(t + 1) * P], tp[t % 2][:]).then_inc(tr_ev, 1)
            for t in range(NT):
                norm.square(act, t)
                if t >= 1:
                    norm.first_half(act, t - 1)
            norm.first_half(act, NT - 1)

        @block.vector
        def _(dve):
            link = Chain(dve, chain)
            V = nc.vector
            V.memset(norm.eps[:], EPS).then_inc(norm.eps_set, 1)
            dve.wait_ge(root_done, 1)
            rms_rows(V, link, rstd[:], root[:], ms[:], tm[:], RD)
            for t in range(NT):
                link(V.tensor_tensor(ret[:, t].rearrange("p (h e) -> p h e", e=RD),
                                     ret[:, t].rearrange("p (h e) -> p h e", e=RD),
                                     rstd[:, t * RH:(t + 1) * RH, None].to_broadcast([P, RH, RD]), ALU.mult))
                V.tensor_tensor(ret[:, t], ret[:, t], sg[:, t], ALU.mult).then_inc(r_done, 1)
            norm.prepare(dve, eps=False)
            for t in range(NT):
                if t >= 1:
                    norm.scale(dve, link, t - 1)
                add_gated(nc, dve, link, c, gate, t, 0, ps, tmp, mm, x_done)
                if t >= 1:
                    norm.second_half(dve, t - 1)
            norm.scale(dve, link, NT - 1)
            norm.second_half(dve, NT - 1)
            norm.logits_out(dve)

        @block.gpsimd
        def _(pool):
            for t in range(NT):
                norm.shift(pool, t)

        @block.tensor
        def _(pe):
            for t in range(NT):
                pe.wait_ge(r_done, t + 1)
                if t >= 2:
                    pe.wait_ge(tr_ev, t - 1)
                for h in range(RH):
                    last = nc.tensor.transpose(tp[t % 2][:, h, :], ret[:, t, h * RD:(h + 1) * RD], c.ident[:])
                last.then_inc(tr, 1)
            pe.wait_ge(w_ready, 16)
            for t in range(NT):
                pe.wait_ge(tr_ev, t + 1)
                for half in range(2):
                    n = 2 * t + half
                    if n >= 4:
                        pe.wait_ge(x_done, n - 3)
                    for j in range(KD):
                        lhs = rT[:, j, t * P:(t + 1) * P] if j < RH else yT[:, j - RH, t * P:(t + 1) * P]
                        last = nc.tensor.matmul(ps[n % 4][:], lhs, w[:, j, half * 512:(half + 1) * 512],
                                                start=(j == 0), stop=(j == KD - 1))
                    last.then_inc(mm, 1)
                if t >= 1:
                    norm.transpose(pe, t - 1)
                if t == 2:
                    pe.wait_ge(tr_ev, NT)
                if t >= 2:
                    norm.logits(pe, t - 2)
            norm.logits(pe, NT - 2)
            norm.transpose(pe, NT - 1)
            norm.logits(pe, NT - 1)


def add_gated(nc, dve, link, c, gate, t, t0, ps, tmp, mm, x_done):
    st = 1 if t0 + t < CT else 0
    for half in range(2):
        n = 2 * t + half
        cols = slice(half * 512, (half + 1) * 512)
        dve.wait_ge(mm, n + 1)
        link(nc.vector.tensor_tensor(tmp[n % 2][:], ps[n % len(ps)][:], gate[:, st, cols], ALU.mult))
        nc.vector.tensor_tensor(c.X[:, t0 + t, cols], c.X[:, t0 + t, cols], tmp[n % 2][:], ALU.add).then_inc(x_done, 1)


def load_gates(sp, c, gate, ready, layer, sub, streams):
    for st in range(streams):
        sp.dma_start(gate[:, st], c.mods[st, layer:layer + 1, (sub * 3 + 2) * DM:(sub * 3 + 3) * DM]
                     .to_broadcast([P, DM])).then_inc(ready, 16)


def ab_layer(nc, c, a, k):
    with Scope(nc, "ab") as s:
        rows = s.sb("rows", [P, 4, NT, QK])
        yT = s.sb("yT", [P, LT, TOK])
        with Scope(nc, "abh") as s2:
            u = s2.sb("u", [P, LT, U_LEN])
            ab_project(nc, c, a, k, c.hT, rows, u, yT)
        w = s.sb("w", [P, KD, DM])
        gate = s.sb("gate", [P, 2, DM])
        ms = s.sb("ms", [P, NT * RH])
        w_ready = s.sem("w_ready")
        gate_ready = s.sem("gate_ready")
        qT, kT = c.hT[:, 0:RH, :], c.hT[:, RH:2 * RH, :]
        retention(nc, c, a, k, rows, qT, kT, w, w_ready, gate, gate_ready, ms)
        ab_output(nc, c, a, gate, rows, yT, w, w_ready, ms)


def mla_latents(nc, c, a, hT, k):
    IN = QR + KVR + ROPE
    L = NT - CT
    with Scope(nc, "mlat") as s:
        w = k.w_in
        take = carve(k.QT[:].rearrange("p h n -> p (h n)"))
        p = take("p", [P, NT, IN])
        krT = k.KT[:, 0, :]
        junk = s.sb("junk", [P, QR])
        g = s.sb("g", [P, (QR + KVR) // P])
        ms = s.sb("ms", [P, 2, NT])
        root, rstd, tmp, width = (s.sb(n, [P, 2, NT]) for n in ("root", "rstd", "tmp", "width"))
        eps = s.sb("eps", [P, 1])
        cs = s.sb("cs", [P, 2, L, ROPE // 2])
        ta, tb = s.sb("ta", [P, L, ROPE // 2]), s.sb("tb", [P, L, ROPE // 2])
        ps = [s.ps(f"ps{i}", [P, 2, 512]) for i in range(2)]
        tq, tk, tr_ = (s.ps(n, [P, 4, P]) for n in ("tq", "tk", "tr"))
        g_ready, mm, ev, sq, root_done, chain, rows_done, qtr, ktr, rtr, q_ev, k_ev, r_ev, set_ = (
            s.sem(n) for n in ("g_ready", "mm", "ev", "sq", "root_done", "chain", "rows_done", "qtr",
                               "ktr", "rtr", "q_ev", "k_ev", "r_ev", "set"))
        block = s.block()

        @block.sync
        def _(sp):
            sp.dma_start(g[:, 0:QR // P], a["mla_q_norm_g"][0].rearrange("(c p) -> p c", p=P),
                         allow_slow_non_contiguous=True).then_inc(g_ready, 16)
            sp.dma_start(g[:, QR // P:], a["mla_kv_norm_g"][0].rearrange("(c p) -> p c", p=P),
                         allow_slow_non_contiguous=True).then_inc(g_ready, 16)
            sp.dma_start(cs[:], a["mla_cs"]).then_inc(g_ready, 16)
            sp.dma_start(k.wkv[:], a["mla_w_ukv"][0].rearrange("(k p) n -> p k n", p=P)).then_inc(k.heads_ready, 16)
            sp.dma_start(k.wq[:], a["mla_w_uq"][0].rearrange("(k p) n -> p k n", p=P)).then_inc(k.heads_ready, 16)

        @block.tensor
        def _(pe):
            pe.wait_ge(k.w_in_ready, 16)
            for t in range(NT):
                if t >= 2:
                    pe.wait_ge(ev, t - 1)
                for k_ in range(KD):
                    if t >= CT:
                        nc.tensor.matmul(ps[t % 2][:, 0, 0:QR], hT[:, k_, t * P:(t + 1) * P], w[:, k_, 0:QR],
                                         start=(k_ == 0), stop=(k_ == KD - 1))
                for k_ in range(KD):
                    last = nc.tensor.matmul(ps[t % 2][:, 1, 0:KVR + ROPE], hT[:, k_, t * P:(t + 1) * P], w[:, k_, QR:],
                                            start=(k_ == 0), stop=(k_ == KD - 1))
                last.then_inc(mm, 1)
            for t in range(NT):
                pe.wait_ge(rows_done, t + 1)
                if t > CT:
                    pe.wait_ge(q_ev, t - CT)
                if t >= CT:
                    for j in range(QR // P):
                        last = nc.tensor.transpose(tq[:, j, :], p[:, t, j * P:(j + 1) * P], c.ident[:])
                    last.then_inc(qtr, 1)
                if t >= 1:
                    pe.wait_ge(k_ev, t)
                for j in range(KVR // P):
                    last = nc.tensor.transpose(tk[:, j, :], p[:, t, QR + j * P:QR + (j + 1) * P], c.ident[:])
                last.then_inc(ktr, 1)
                if t >= 1:
                    pe.wait_ge(r_ev, t)
                nc.tensor.transpose(tr_[0:ROPE, 0, :], p[:, t, QR + KVR:], c.ident[:]).then_inc(rtr, 1)

        @block.scalar
        def _(act):
            act.wait_ge(set_, 1)
            n = 0
            for t in range(NT):
                act.wait_ge(ev, t + 1)
                for i, (o, m) in enumerate(((0, QR), (QR, KVR))):
                    if i == 0 and t < CT:
                        continue
                    n += 1
                    nc.scalar.activation(junk[:, 0:m], p[:, t, o:o + m], ACT.Square, accum_out=ms[:, i, t:t + 1]).then_inc(sq, 1)
                    act.wait_ge(sq, n)
            nc.scalar.activation(root[:, 0], ms[:, 0], ACT.Sqrt, scale=1.0 / QR, bias=eps[:]).then_inc(root_done, 1)
            nc.scalar.activation(root[:, 1], ms[:, 1], ACT.Sqrt, scale=1.0 / KVR, bias=eps[:]).then_inc(root_done, 1)

        @block.vector
        def _(dve):
            link = Chain(dve, chain)
            V = nc.vector
            link(V.memset(eps[:], EPS))
            link(V.memset(width[:, 0], 1.0 / QR))
            link(V.memset(width[:, 1], 1.0 / KVR))
            V.memset(ms[:], 1.0).then_inc(set_, 1)
            for t in range(NT):
                dve.wait_ge(mm, t + 1)
                if t >= CT:
                    link(V.tensor_copy(p[:, t, 0:QR], ps[t % 2][:, 0, 0:QR]))
                V.tensor_copy(p[:, t, QR:], ps[t % 2][:, 1, 0:KVR + ROPE]).then_inc(ev, 1)
            dve.wait_ge(g_ready, 48)
            x1, x2 = (p[:, CT:, QR + KVR + i * (ROPE // 2):QR + KVR + (i + 1) * (ROPE // 2)] for i in range(2))
            dve.wait_ge(ev, NT)
            link(V.tensor_tensor(ta[:], x1, cs[:, 1], ALU.mult))
            link(V.tensor_tensor(tb[:], x2, cs[:, 1], ALU.mult))
            link(V.tensor_tensor(x1, x1, cs[:, 0], ALU.mult))
            link(V.tensor_tensor(x2, x2, cs[:, 0], ALU.mult))
            link(V.tensor_tensor(x1, x1, tb[:], ALU.subtract))
            link(V.tensor_tensor(x2, x2, ta[:], ALU.add))
            dve.wait_ge(root_done, 2)
            link(V.reciprocal(rstd[:], root[:]))
            link(V.tensor_tensor(ms[:], ms[:], width[:], ALU.mult))
            link(V.tensor_scalar(ms[:], ms[:], EPS, None, ALU.add))
            link(V.tensor_tensor(tmp[:], rstd[:], rstd[:], ALU.mult))
            link(V.tensor_tensor(tmp[:], tmp[:], ms[:], ALU.mult))
            link(V.tensor_scalar(tmp[:], tmp[:], -0.5, 1.5, ALU.mult, ALU.add))
            link(V.tensor_tensor(rstd[:], rstd[:], tmp[:], ALU.mult))
            for t in range(NT):
                if t >= CT:
                    link(V.tensor_scalar(p[:, t, 0:QR], p[:, t, 0:QR], rstd[:, 0, t:t + 1], None, ALU.mult))
                V.tensor_scalar(p[:, t, QR:QR + KVR], p[:, t, QR:QR + KVR], rstd[:, 1, t:t + 1], None,
                                ALU.mult).then_inc(rows_done, 1)
            for t in range(NT):
                if t >= CT:
                    dve.wait_ge(qtr, t - CT + 1)
                    V.tensor_tensor(k.cqT[:, :, (t - CT) * P:(t - CT + 1) * P], tq[:, 0:QR // P, :],
                                    g[:, 0:QR // P, None].to_broadcast([P, QR // P, P]), ALU.mult).then_inc(q_ev, 1)
                dve.wait_ge(ktr, t + 1)
                V.tensor_tensor(k.ckT[:, :, t * P:(t + 1) * P], tk[:, 0:KVR // P, :],
                                g[:, QR // P:, None].to_broadcast([P, KVR // P, P]), ALU.mult).then_inc(k_ev, 1)
                dve.wait_ge(rtr, t + 1)
                V.tensor_copy(krT[NOPE:NOPE + ROPE, t * P:(t + 1) * P], tr_[0:ROPE, 0, :]).then_inc(r_ev, 1)


def mla_heads(nc, c, a, k):
    L = NT - CT
    QD = NOPE + ROPE
    HALF = TOK // 2
    with Scope(nc, "mhead") as s:
        wq, wkv = k.wq, k.wkv
        q = k.q
        cs = s.sb("cs", [P, 2, L, ROPE // 2])
        ta, tb = (s.sb(n, [P, AH, ROPE // 2]) for n in ("ta", "tb"))
        ps = [s.ps(f"ps{i}", [P, 512]) for i in range(8)]
        cs_ready, mm, chain, rot, kr_done = (s.sem(n) for n in ("cs_ready", "mm", "chain", "rot", "kr_done"))
        evs = [s.sem("ev_act"), s.sem("ev_dve")]
        block = s.block()
        groups = [("v", t, b) for t in range(NT) for b in range(2)]
        groups += [("q", t, b) for t in range(L) for b in range(3)]
        groups += [("k", h, b) for h in range(0, AH, 2) for b in range(2)]
        groups += [("t", h, 0) for h in range(AH)]
        Q_END = NT * 2 + L * 3

        def copy_out(eng_copy, eng_scale, i, kind, x, b):
            bank = ps[i % 8]
            if kind == "v":
                return [eng_copy(k.V[:, x, b * 512:(b + 1) * 512], bank[:])]
            if kind == "q":
                return [eng_copy(q[:, x, b * 512:(b + 1) * 512], bank[:])]
            if kind == "k":
                return [eng_copy(k.KT[0:NOPE, x + j, b * HALF:(b + 1) * HALF], bank[64 * j:64 * j + NOPE, 0:HALF])
                        for j in range(2)]
            return [eng_scale(k.QT[0:QD, x, :], bank[0:QD, :])]

        @block.sync
        def _(sp):
            sp.dma_start(cs[:], a["mla_cs"]).then_inc(cs_ready, 16)

        @block.gpsimd
        def _(pool):
            for h in range(1, AH):
                nc.gpsimd.tensor_copy(k.KT[NOPE:NOPE + ROPE, h, :], k.KT[NOPE:NOPE + ROPE, 0, :]).then_inc(kr_done, 1)
            pool.wait_ge(kr_done, AH - 1)

        @block.tensor
        def _(pe):
            pe.wait_ge(k.heads_ready, 32)
            wv = wkv[:].rearrange("p k (h two n) -> p k h two n", two=2, n=VD)
            for i, (kind, x, b) in enumerate(groups):
                bank = ps[i % 8]
                if i >= 8:
                    pe.wait_ge(evs[i % 2], (i - 8) // 2 + 1)
                if kind == "v":
                    for j in range(KVR // P):
                        last = nc.tensor.matmul(bank[:], k.ckT[:, j, x * P:(x + 1) * P], wv[:, j, b * 8:(b + 1) * 8, 1, :],
                                                start=(j == 0), stop=(j == KVR // P - 1))
                elif kind == "q":
                    for j in range(QR // P):
                        last = nc.tensor.matmul(bank[:], k.cqT[:, j, x * P:(x + 1) * P], wq[:, j, b * 512:(b + 1) * 512],
                                                start=(j == 0), stop=(j == QR // P - 1))
                elif kind == "k":
                    for j in range(KVR // P):
                        for e in range(2):
                            last = nc.tensor.matmul(bank[64 * e:64 * e + NOPE, 0:HALF], wv[:, j, x + e, 0, :],
                                                    k.ckT[:, j, b * HALF:(b + 1) * HALF],
                                                    start=(j == 0), stop=(j == KVR // P - 1))
                else:
                    pe.wait_ge(rot, L)
                    for t in range(L):
                        last = nc.tensor.transpose(bank[0:QD, t * P:(t + 1) * P], q[:, t, x * QD:(x + 1) * QD], c.ident[:])
                last.then_inc(mm, 1)

        @block.scalar
        def _(act):
            for i in range(0, len(groups), 2):
                act.wait_ge(mm, i + 1)
                copies = copy_out(nc.scalar.copy, lambda o, x: nc.scalar.mul(o, x, MLA_SCALE), i, *groups[i])
                copies[-1].then_inc(evs[0], 1)

        @block.vector
        def _(dve):
            link = Chain(dve, chain)
            V = nc.vector
            dve.wait_ge(cs_ready, 16)
            for i in range(1, len(groups), 2):
                dve.wait_ge(mm, i + 1)
                copies = copy_out(V.tensor_copy, lambda o, x: V.tensor_scalar(o, x, MLA_SCALE, None, ALU.mult),
                                  i, *groups[i])
                copies[-1].then_inc(evs[1], 1)
                if i + 1 == Q_END:
                    dve.wait_ge(evs[0], Q_END // 2)
                    dve.wait_ge(evs[1], Q_END // 2)
                    for t in range(L):
                        x = q[:, t, :].rearrange("p (h n) -> p h n", n=QD)
                        x1, x2 = x[:, :, NOPE:NOPE + ROPE // 2], x[:, :, NOPE + ROPE // 2:]
                        co, si = (cs[:, j, t, None, :].to_broadcast([P, AH, ROPE // 2]) for j in range(2))
                        link(V.tensor_tensor(ta[:], x1, si, ALU.mult))
                        link(V.tensor_tensor(tb[:], x2, si, ALU.mult))
                        link(V.tensor_tensor(x1, x1, co, ALU.mult))
                        link(V.tensor_tensor(x2, x2, co, ALU.mult))
                        link(V.tensor_tensor(x1, x1, tb[:], ALU.subtract))
                        V.tensor_tensor(x2, x2, ta[:], ALU.add).then_inc(rot, 1)
                        dve.wait_ge(rot, t + 1)


def attention(nc, c, a, k):
    L = NT - CT
    QD = NOPE + ROPE
    UNITS = [(h, t) for h in range(AH) for t in range(L)]
    N = len(UNITS)
    with Scope(nc, "att") as s:
        pr = [k.cqT[:].rearrange("p a b -> p (a b)")[:, i * TOK:(i + 1) * TOK] for i in range(2)]
        pT = [k.ckT[:, i, :].rearrange("p (n m) -> p n m", m=P) for i in range(2)]
        nmax = s.sb("nmax", [P, 2])
        tot = s.sb("tot", [P, 2])
        inv = s.sb("inv", [P, 2])
        sc = [s.ps(f"sc{i}", [P, 2, 512]) for i in range(2)]
        tp = [s.ps(f"tp{i}", [P, 3, P]) for i in range(2)]
        pv = [s.ps(f"pv{i}", [P, 512]) for i in range(2)]
        sc_done, mx, ex, tr, ev_a, ev_d, pv_done, inv_done, o_done = (
            s.sem(n) for n in ("sc_done", "mx", "ex", "tr", "ev_a", "ev_d", "pv_done", "inv_done", "o_done"))
        block = s.block()
        HALF = TOK // 2

        @block.sync
        def _(sp):
            sp.dma_start(k.wo[:], a["mla_w_out"][0].rearrange("(k p) n -> p k n", p=P)).then_inc(k.wo_ready, 16)
            load_gates(sp, c, k.gate, k.gate_ready, 1, 0, 1)
            sp.wait_ge(k.gate_ready, 16)

        @block.tensor
        def _(pe):
            def scores(n):
                h, t = UNITS[n]
                if n >= 2:
                    pe.wait_ge(ex, n - 1)
                for b in range(2):
                    last = nc.tensor.matmul(sc[n % 2][:, b, 0:HALF], k.QT[0:QD, h, t * P:(t + 1) * P],
                                            k.KT[0:QD, h, b * HALF:(b + 1) * HALF], start=True, stop=True)
                last.then_inc(sc_done, 1)

            def values(n):
                h, t = UNITS[n]
                if n >= 2:
                    pe.wait_ge(o_done, n - 1)
                for kt in range(NT):
                    if kt % 3 == 0:
                        pe.wait_ge((ev_a, ev_d)[kt // 3], n + 1)
                    last = nc.tensor.matmul(pv[n % 2][:, 0:VD], pT[n % 2][:, kt, :], k.V[:, kt, h * VD:(h + 1) * VD],
                                            start=(kt == 0), stop=(kt == NT - 1))
                last.then_inc(pv_done, 1)

            scores(0)
            for n in range(N):
                if n + 1 < N:
                    scores(n + 1)
                pe.wait_ge(ex, n + 1)
                for b, ev in ((0, ev_a), (1, ev_d)):
                    if n >= 1:
                        pe.wait_ge(ev, n)
                    for j in range(3):
                        kt = 3 * b + j
                        last = nc.tensor.transpose(tp[b][:, j, :], pr[n % 2][:, kt * P:(kt + 1) * P], c.ident[:])
                    last.then_inc(tr, 1)
                if n >= 1:
                    values(n - 1)
            values(N - 1)

        @block.scalar
        def _(act):
            for n in range(N):
                act.wait_ge(mx, n + 1)
                if n >= 2:
                    act.wait_ge(inv_done, n - 1)
                nc.scalar.activation(pr[n % 2].rearrange("p (b m) -> p b m", b=2), sc[n % 2][:, :, 0:HALF], ACT.Exp,
                                     bias=nmax[:, n % 2:n % 2 + 1], accum_out=tot[:, n % 2:n % 2 + 1]).then_inc(ex, 1)
                if n >= 2:
                    act.wait_ge(pv_done, n - 1)
                act.wait_ge(tr, 2 * n + 1)
                nc.scalar.copy(pT[n % 2][:, 0:3, :], tp[0][:]).then_inc(ev_a, 1)

        @block.vector
        def _(dve):
            def maximum(n):
                dve.wait_ge(sc_done, n + 1)
                if n >= 2:
                    dve.wait_ge(ex, n - 1)
                nc.vector.tensor_reduce(nmax[:, n % 2:n % 2 + 1], sc[n % 2][:, :, 0:HALF], mybir.AxisListType.XY,
                                        ALU.max, negate=True).then_inc(mx, 1)

            def output(n):
                h, t = UNITS[n]
                dve.wait_ge(inv_done, n + 1)
                dve.wait_ge(pv_done, n + 1)
                nc.vector.tensor_scalar(k.O[:, t, h * VD:(h + 1) * VD], pv[n % 2][:, 0:VD], inv[:, n % 2:n % 2 + 1],
                                        None, ALU.mult).then_inc(o_done, 1)

            maximum(0)
            for n in range(N):
                if n + 1 < N:
                    maximum(n + 1)
                if n >= 2:
                    dve.wait_ge(pv_done, n - 1)
                dve.wait_ge(tr, 2 * n + 2)
                nc.vector.tensor_copy(pT[n % 2][:, 3:6, :], tp[1][:]).then_inc(ev_d, 1)
                if n >= 1:
                    output(n - 1)
                if n >= 2:
                    dve.wait_ge(o_done, n - 1)
                nc.vector.reciprocal(inv[:, n % 2:n % 2 + 1], tot[:, n % 2:n % 2 + 1]).then_inc(inv_done, 1)
            output(N - 1)


def mla_output(nc, c, a, k):
    L = NT - CT
    with Scope(nc, "mlao") as s:
        w, O = k.wo, k.O
        oT = k.QT[:, 0:KD, :]
        tmp = [s.sb(f"tmp{i}", [P, 512]) for i in range(2)]
        tp = [s.ps(f"tp{i}", [P, 4, P]) for i in range(2)]
        ps = [s.ps(f"ps{i}", [P, 512]) for i in range(4)]
        tr, ev, mm, x_done, chain = (s.sem(n) for n in ("tr", "ev", "mm", "x_done", "chain"))
        logits = tp[0][:].rearrange("p h n -> p (h n)")[:, 0:L * ROUTES].rearrange("p (t n) -> p t n", t=L)
        norm = NormModulate(nc, c, a, s, 1, 1, CT, lambda eng, t: eng.wait_ge(x_done, 2 * t + 2), c.h_rows,
                            carve(k.KT[:].rearrange("p h n -> p (h n)")), lambda eng: eng.wait_ge(tr, 2 * L),
                            logits=logits)
        block = s.block()

        @block.sync
        def _(sp):
            norm.load(sp)
            norm.load_router(sp)
            norm.store(sp)

        @block.tensor
        def _(pe):
            for n in range(2 * L):
                t, half = divmod(n, 2)
                if n >= 2:
                    pe.wait_ge(ev, n - 1)
                for j in range(4):
                    m = 4 * half + j
                    last = nc.tensor.transpose(tp[n % 2][:, j, :], O[:, t, m * P:(m + 1) * P], c.ident[:])
                last.then_inc(tr, 1)
            pe.wait_ge(k.wo_ready, 16)
            for n in range(2 * L):
                t, half = divmod(n, 2)
                pe.wait_ge(ev, 2 * t + 2)
                if n >= 4:
                    pe.wait_ge(x_done, n - 3)
                for j in range(KD):
                    last = nc.tensor.matmul(ps[n % 4][:], oT[:, j, t * P:(t + 1) * P], w[:, j, half * 512:(half + 1) * 512],
                                            start=(j == 0), stop=(j == KD - 1))
                last.then_inc(mm, 1)
                if half and t >= 1:
                    norm.transpose(pe, t - 1)
                if half and t == 2:
                    pe.wait_ge(ev, 2 * L)
                if half and t >= 2:
                    norm.logits(pe, t - 2)
            norm.logits(pe, L - 2)
            norm.transpose(pe, L - 1)
            norm.logits(pe, L - 1)

        @block.scalar
        def _(act):
            for n in range(2 * L):
                t, half = divmod(n, 2)
                act.wait_ge(tr, n + 1)
                nc.scalar.copy(oT[:, 4 * half:4 * half + 4, t * P:(t + 1) * P], tp[n % 2][:]).then_inc(ev, 1)
            for t in range(L):
                norm.square(act, t)
                if t >= 1:
                    norm.first_half(act, t - 1)
            norm.first_half(act, L - 1)

        @block.vector
        def _(dve):
            link = Chain(dve, chain)
            norm.prepare(dve)
            for t in range(L):
                if t >= 1:
                    norm.scale(dve, link, t - 1)
                add_gated(nc, dve, link, c, k.gate, t, CT, ps, tmp, mm, x_done)
                if t >= 1:
                    norm.second_half(dve, t - 1)
            norm.scale(dve, link, L - 1)
            norm.second_half(dve, L - 1)
            norm.logits_out(dve)

        @block.gpsimd
        def _(pool):
            for t in range(L):
                norm.shift(pool, t)


def mla_buffers(s):
    k = Box()
    k.KT = s.sb("KT", [P, AH, TOK])
    k.cqT = s.sb("cqT", [P, QR // P, SEQ])
    k.ckT = s.sb("ckT", [P, KVR // P, TOK])
    k.V = s.sb("V", [P, NT, AH * VD])
    IN = QR + KVR + ROPE
    k.w_in = k.V[:].rearrange("p t n -> p (t n)")[:, 0:KD * IN].rearrange("p (k n) -> p k n", k=KD)
    k.w_in_ready = s.sem("w_in_ready")
    return k


def load_w_in(sp, a, k):
    sp.dma_start(k.w_in, a["mla_w_in"][0].rearrange("(k p) n -> p k n", p=P)).then_inc(k.w_in_ready, 16)


def mla_layer(nc, c, a, k):
    L = NT - CT
    with Scope(nc, "mlak") as s:
        k.gate = s.sb("gate", [P, 1, DM])
        k.gate_ready, k.heads_ready, k.wo_ready = (s.sem(n) for n in ("gate_ready", "heads_ready", "wo_ready"))
        k.q = c.hT[:].rearrange("p k n -> p (k n)").rearrange("p (t n) -> p t n", t=L)
        k.O = k.q[:, :, 0:AH * VD]
        k.QT = s.sb("QT", [P, AH, L * P])
        with Scope(nc, "mlaw") as s1:
            k.wq = s1.sb("wq", [P, QR // P, AH * (NOPE + ROPE)])
            k.wkv = s1.sb("wkv", [P, KVR // P, AH * (NOPE + VD)])
            mla_latents(nc, c, a, c.hT, k)
            mla_heads(nc, c, a, k)
        with Scope(nc, "mlawo") as s1:
            k.wo = s1.sb("wo", [P, KD, DM])
            attention(nc, c, a, k)
            mla_output(nc, c, a, k)


def routing(nc, c, a, layer, t0, r, prefetch):
    T = NT - t0
    OVB = T * 2 - 1
    STEPS = T - 1
    NB = E + OVB
    with Scope(nc, f"route{layer}") as s:
        take = carve(c.hT[:].rearrange("p k n -> p (k n)"))
        g4 = [take("g4", [P, T, G]) for i in range(2)]
        t1 = [take("t1", [P, T, 1]) for i in range(5)]
        e8 = [take("e8", [P, T, EPG]) for i in range(5)]
        sel = take("sel", [P, T, G, EPG])
        pick = take("pick", [P, 2, T * E])
        both = take("both", [P, T, E])
        pos, nb, hot, block_of = (take(n, [P, T, E]) for n in ("pos", "nb", "hot", "block_of"))
        chosen = take("chosen", [P, 2, T * E])
        row, blk = (take(n, [P, 2 * T]) for n in ("row", "blk"))
        cnt, blocks, ends, starts, ioE, onesE = (take(n, [P, E]) for n in ("cnt", "blocks", "ends", "starts", "ioE", "onesE"))
        oute = take("oute", [P, OVB, E])
        ove = take("ove", [P, OVB + 1])
        iog, ioe = take("iog", [P, G]), take("ioe", [P, EPG])
        iob, iop = take("iob", [P, NB]), take("iop", [P, P])
        tokid = take("tokid", [P, T])
        row_hot = take("row_hot", [P, 2 * T, P])
        blk_hot = take("blk_hot", [P, 2 * T, NB])
        pps = s.ps("pps", [P, T, E])
        cps = s.ps("cps", [P, T, E])
        lps = s.ps("lps", [P, NB])
        io_ready, m_done, pos_done, chain, hots_done, list_done = (
            s.sem(n) for n in ("io_ready", "m_done", "pos_done", "chain", "hots_done", "list_done"))
        block = s.block()

        @block.sync
        def _(sp):
            prefetch(sp)

        @block.gpsimd
        def _(pool):
            def index(out, pattern, base, mult=0):
                nc.gpsimd.iota(out, pattern=pattern, base=base, channel_multiplier=mult,
                               allow_small_or_imprecise_dtypes=True).then_inc(io_ready, 1)

            index(iog, [[-1, G]], G)
            index(ioe, [[-1, EPG]], EPG)
            index(ioE, [[1, E]], 0)
            index(iob, [[1, NB]], 0)
            index(iop, [[1, P]], 0)
            index(tokid, [[P, T]], t0 * P, 1)
            nc.gpsimd.memset(onesE, 1.0).then_inc(io_ready, 1)

        @block.tensor
        def _(pe):
            pe.wait_ge(m_done, 1)
            nc.tensor.matmul(pps[:], c.before[:], both, start=True, stop=(T == 1))
            for j in range(1, T):
                nc.tensor.matmul(pps[:, j:, :], c.ones[:], both[:, 0:T - j, :], start=False, stop=(j == T - 1))
            nc.tensor.matmul(cps[:], c.ones[:], both, start=True, stop=True).then_inc(pos_done, 1)
            pe.wait_ge(hots_done, 2)
            for n in range(2 * T):
                last = nc.tensor.matmul(lps[:], row_hot[:, n, :], blk_hot[:, n, :], start=(n == 0), stop=(n == 2 * T - 1))
            last.then_inc(list_done, 1)

        @block.vector
        def _(dve):
            link = Chain(dve, chain)
            V = nc.vector
            dve.wait_ge(io_ready, 7)
            gl, el = c.lg[:, 0:T, 0:G], c.lg[:, 0:T, G:]

            def first_hot(out, vals, top, order, tmp, best, n):
                link(V.tensor_reduce(top[:, :, 0], vals, AX, ALU.max))
                link(V.tensor_tensor(tmp, vals, top.to_broadcast([P, T, n]), ALU.is_equal))
                link(V.tensor_tensor(tmp, tmp, order[:, None, :].to_broadcast([P, T, n]), ALU.mult))
                link(V.tensor_reduce(best[:, :, 0], tmp, AX, ALU.max))
                link(V.tensor_tensor(out, tmp, best.to_broadcast([P, T, n]), ALU.is_equal))

            gtop, best, e1, e2, wt = t1
            first_hot(g4[0], gl, gtop, iog, g4[1], best, G)
            best_group = g4[0][:, :, :, None].to_broadcast([P, T, G, EPG])
            link(V.tensor_tensor(sel, el.rearrange("p t (g e) -> p t g e", g=G), best_group, ALU.mult))
            link(V.tensor_reduce(e8[0], sel.rearrange("p t g e -> p t e g"), AX, ALU.add))
            first_hot(e8[1], e8[0], e1, ioe, e8[2], best, EPG)
            link(V.scalar_tensor_tensor(out=e8[3], in0=e8[1], scalar=-1e30, in1=e8[0], op0=ALU.mult, op1=ALU.add))
            first_hot(e8[4], e8[3], e2, ioe, e8[2], best, EPG)
            for k, hot8 in ((0, e8[1]), (1, e8[4])):
                link(V.tensor_tensor(pick[:, k, :].rearrange("p (t g e) -> p t g e", t=T, g=G), best_group,
                                     hot8[:, :, None, :].to_broadcast([P, T, G, EPG]), ALU.mult))
            V.tensor_tensor(both.rearrange("p t e -> p (t e)"), pick[:, 0, :], pick[:, 1, :], ALU.add).then_inc(m_done, 1)
            link(V.tensor_tensor(r.gshift[:, 0:T, :], gl, gtop.to_broadcast([P, T, G]), ALU.subtract))
            link(V.tensor_tensor(r.eshift[:, 0:T], e2[:, :, 0], e1[:, :, 0], ALU.subtract))
            dve.wait_ge(pos_done, 1)
            link(V.tensor_reduce(cnt, cps[:].rearrange("p t e -> p e t"), AX, ALU.add))
            link(V.tensor_copy(pos, pps[:]))
            link(V.tensor_scalar(blocks, cnt, float(CAP), None, ALU.is_gt))
            for j in range(2, STEPS + 1):
                link(V.scalar_tensor_tensor(out=blocks, in0=cnt, scalar=float(CAP * j), in1=blocks,
                                            op0=ALU.is_gt, op1=ALU.add))
            link(V.tensor_tensor_scan(ends, onesE, blocks, 0.0, ALU.mult, ALU.add))
            link(V.tensor_tensor(starts, ends, blocks, ALU.subtract))
            link(V.tensor_scalar(nb, pos, float(CAP), None, ALU.is_ge))
            for j in range(2, STEPS + 1):
                link(V.scalar_tensor_tensor(out=nb, in0=pos, scalar=float(CAP * j), in1=nb,
                                            op0=ALU.is_ge, op1=ALU.add))
            link(V.tensor_scalar(hot, nb, 0.0, None, ALU.is_gt))
            link(V.scalar_tensor_tensor(out=starts, in0=starts, scalar=float(E - 1), in1=ioE,
                                        op0=ALU.add, op1=ALU.subtract))
            link(V.tensor_tensor(block_of, hot, starts[:, None, :].to_broadcast([P, T, E]), ALU.mult))
            link(V.tensor_tensor(block_of, block_of, ioE[:, None, :].to_broadcast([P, T, E]), ALU.add))
            link(V.tensor_tensor(block_of, block_of, nb, ALU.add))
            link(V.scalar_tensor_tensor(out=pos, in0=nb, scalar=-float(CAP), in1=pos, op0=ALU.mult, op1=ALU.add))
            for of, into in ((pos, row), (block_of, blk)):
                flat = of.rearrange("p t e -> p (t e)")
                link(V.tensor_tensor(chosen, pick, flat[:, None, :].to_broadcast([P, 2, T * E]), ALU.mult))
                link(V.tensor_reduce(into, chosen.rearrange("p k (t e) -> p (k t) e", e=E), AX, ALU.add))
            V.tensor_tensor(row_hot, iop[:, None, :].to_broadcast([P, 2 * T, P]),
                            row[:, :, None].to_broadcast([P, 2 * T, P]), ALU.is_equal).then_inc(hots_done, 1)
            link(V.tensor_tensor(blk_hot, iob[:, None, :].to_broadcast([P, 2 * T, NB]),
                                 blk[:, :, None].to_broadcast([P, 2 * T, NB]), ALU.is_equal))
            for k in range(2):
                half = blk_hot[:, k * T:(k + 1) * T, :]
                ins = V.tensor_tensor(half, half, tokid[:, :, None].to_broadcast([P, T, NB]), ALU.mult)
                ins.then_inc(hots_done, 1) if k else link(ins)
            link(V.scalar_tensor_tensor(out=r.slot[:, 0:2 * T], in0=blk, scalar=float(CAP), in1=row,
                                        op0=ALU.mult, op1=ALU.add))
            link(V.tensor_tensor(oute, ends[:, None, :].to_broadcast([P, OVB, E]),
                                 iob[:, 0:OVB, None].to_broadcast([P, OVB, E]), ALU.is_le))
            link(V.tensor_reduce(ove[:, 0:OVB], oute, AX, ALU.add))
            link(V.tensor_scalar(ove[:, 0:OVB], ove[:, 0:OVB], float(E - 1), None, ALU.min))
            link(V.tensor_copy(ove[:, OVB:OVB + 1], ends[:, E - 1:E]))
            link(V.tensor_copy(r.more[:, 0:OVB + 1], ove))
            link(V.tensor_copy(r.cnt[:], cnt))
            dve.wait_ge(list_done, 1)
            link(V.tensor_copy(r.tok[:, 0:NB], lps[:]))


def expert_weights(s, slots):
    w = Box()
    w.g = [s.sb(f"wg{i}", [P, KD, HID]) for i in range(slots)]
    w.u = [s.sb(f"wu{i}", [P, KD, HID]) for i in range(slots)]
    w.d = [s.sb(f"wd{i}", [P, HT_N, DM]) for i in range(slots)]
    w.gu_ready = [s.sem(f"gu_ready{i}") for i in range(slots)]
    w.d_ready = [s.sem(f"d_ready{i}") for i in range(slots)]
    return w


def load_gate_up(sp, a, layer, w, e, q):
    for buf, name in ((w.g, "moe_w_gate"), (w.u, "moe_w_up")):
        src = a[name][layer].rearrange("e (k p) n -> e p k n", p=P)[bass.ds(e, 1)]
        sp.dma_start(buf[q][:], src.rearrange("o p k n -> (o p) k n")).then_inc(w.gu_ready[q], 16)


def load_down(sp, a, layer, w, e, q):
    src = a["moe_w_down"][layer].rearrange("e (k p) n -> e p k n", p=P)[bass.ds(e, 1)]
    sp.dma_start(w.d[q][:], src.rearrange("o p k n -> (o p) k n")).then_inc(w.d_ready[q], 16)


def experts(nc, c, a, layer, t0, r, w):
    with Scope(nc, f"exp{layer}") as s:
        S = len(w.g)
        LOOPS = (E - 1) // S
        H = P // 2
        idx = [s.sb(f"idx{i}", [P, 1], I32) for i in range(S)]
        y = [s.sb(f"y{i}", [P, DM]) for i in range(S)]
        spare = s.sb("spare", [1, 1])
        take = carve(c.hT[:].rearrange("p k n -> p (k n)"))
        xg = [take("xg", [P, DM]) for _ in range(S)]
        xT = take("xT", [P, KD, P])
        sg = take("sg", [P, HID])
        h = take("h", [P, HID])
        hT = take("hT", [P, HT_N, P])
        xps = [s.ps(f"xps{i}", [P, 4, P]) for i in range(2)]
        gps, ups = s.ps("gps", [P, HID]), s.ps("ups", [P, HID])
        hps = s.ps("hps", [P, HT_N, P])
        yps = [s.ps(f"yps{i}", [P, 512]) for i in range(2)]
        x_ready = [s.sem(f"x_ready{i}") for i in range(S)]
        y_free = [s.sem(f"y_free{i}") for i in range(S)]
        (gu_used, d_used, idx_done, xg_set, xg_free, xt_act, xt_dve, xtr, sg_done, h_done, htr, ht_done,
         y_act, y_dve) = (s.sem(n) for n in (
             "gu_used", "d_used", "idx_done", "xg_set", "xg_free", "xt_act", "xt_dve", "xtr", "sg_done",
             "h_done", "htr", "ht_done", "y_act", "y_dve"))
        block = s.block()
        ys = c.ys.rearrange("(b p) n -> b p n", p=P)

        def turns(eng, turn):
            with eng.Fori(0, LOOPS) as i:
                for q in range(S):
                    turn(i * S + q, q, i)
            for n in range(LOOPS * S, E):
                turn(n, n % S, n // S)

        def by_rows(eng, n, work):
            rows = eng.value_load(r.cnt[0:1, bass.ds(n, 1)], min_val=0, max_val=TOK)
            with eng.If(rows > H):
                work(P)
            with eng.Else():
                work(H)

        @block.sync
        def _(sp):
            sp.wait_ge(x_ready[0], 16)
            load_gate_up(sp, a, layer, w, S - 1, S - 1)
            load_down(sp, a, layer, w, S - 1, S - 1)

            def turn(n, q, i):
                sp.wait_ge(gu_used, n + 1)
                load_gate_up(sp, a, layer, w, n + S, q)
                sp.wait_ge(d_used, n + 1)
                load_down(sp, a, layer, w, n + S, q)

            with sp.Fori(0, E // S - 1) as i:
                for q in range(S):
                    turn(i * S + q, q, i)
            for n in range((E // S - 1) * S, E - S):
                turn(n, n % S, n // S)

        @block.gpsimd
        def _(pool):
            nc.gpsimd.memset(spare[:], 0.0)
            for x in xg:
                nc.gpsimd.memset(x, 0.0).then_inc(xg_set, 1)
            pool.wait_ge(xg_set, S)

            def turn(n, q, i):
                pool.wait_ge(xg_free, n + 1)
                nc.gpsimd.tensor_copy(idx[q][:], r.tok[:, bass.ds(n, 1)]).then_inc(idx_done, 1)
                pool.wait_ge(idx_done, n + 1)
                nc.gpsimd.tensor_tensor(spare[:], spare[:], spare[:], ALU.add)

                def gather(rows):
                    nc.gpsimd.indirect_dma_start(xg[q][0:rows, :], None, c.h_rows[:, :],
                                                 bass.IndirectOffsetOnAxis(idx[q][0:rows, :], 0)).then_inc(x_ready[q], 16)

                by_rows(pool, n, gather)

            turns(pool, turn)

        @block.tensor
        def _(pe):
            pe.sem_inc(xg_free, S)

            def x_transposes(n, q, i):
                pe.wait_ge(x_ready[q], i * 16 + 16)
                pe.wait_ge(xt_act, n + 1)
                pe.wait_ge(xt_dve, n + 1)
                for k in range(KD):
                    last = nc.tensor.transpose(xps[k // 4][:, k % 4, :], xg[q][:, k * P:(k + 1) * P], c.ident[:])
                last.then_inc(xtr, 1)

            def turn(n, q, i, more=True):
                x = xT

                def up(rows):
                    pe.wait_ge(w.gu_ready[q], i * 32 + 32)
                    pe.wait_ge(xt_act, n + 2)
                    pe.wait_ge(xt_dve, n + 2)
                    pe.wait_ge(h_done, n + 1)
                    at = 0 if rows == P else H
                    for k in range(KD):
                        nc.tensor.matmul(gps[0:rows, :], x[:, k, 0:rows], w.g[q][:, k, :], start=(k == 0), stop=(k == KD - 1))
                        last = nc.tensor.matmul(ups[at:at + rows, :], x[:, k, 0:rows], w.u[q][:, k, :],
                                                start=(k == 0), stop=(k == KD - 1))
                    last.then_inc(gu_used, 1)

                def down(rows):
                    at = 0 if rows == P else H
                    for k in range(HT_N):
                        last = nc.tensor.transpose(hps[:, k, 0:rows], h[at:at + rows, k * P:(k + 1) * P],
                                                   c.ident[at:at + rows, at:at + rows])
                    last.then_inc(htr, 1)
                    pe.wait_ge(w.d_ready[q], i * 16 + 16)
                    pe.wait_ge(ht_done, n + 2)
                    pe.wait_ge(y_act, n + 1)
                    pe.wait_ge(y_dve, n + 1)
                    for k in range(HT_N):
                        nc.tensor.matmul(yps[0][0:rows, :], hT[:, k, 0:rows], w.d[q][:, k, 0:512],
                                         start=(k == 0), stop=(k == HT_N - 1))
                        last = nc.tensor.matmul(yps[1][at:at + rows, :], hT[:, k, 0:rows], w.d[q][:, k, 512:1024],
                                                start=(k == 0), stop=(k == HT_N - 1))
                    last.then_inc(d_used, 1)

                rows = pe.value_load(r.cnt[0:1, bass.ds(n, 1)], min_val=0, max_val=TOK)
                with pe.If(rows > H):
                    up(P)
                with pe.Else():
                    up(H)
                if more:
                    x_transposes(n + 1, (q + 1) % S, i + (q + 1) // S)
                pe.wait_ge(h_done, n + 2)
                pe.wait_ge(ht_done, n + 1)
                with pe.If(rows > H):
                    down(P)
                with pe.Else():
                    down(H)

            x_transposes(0, 0, 0)
            with pe.Fori(0, LOOPS) as i:
                for q in range(S):
                    turn(i * S + q, q, i)
            for n in range(LOOPS * S, E):
                turn(n, n % S, n // S, more=n + 1 < E)

        @block.scalar
        def _(act):
            act.sem_inc(xt_act, 1)
            act.sem_inc(y_act, 1)
            for free in y_free:
                act.sem_inc(free, 16)

            def x_copy(n, q):
                act.wait_ge(xtr, n + 1)
                nc.scalar.copy(xT[:, 0:4, :], xps[0][:]).then_inc(xt_act, 1)

            def turn(n, q, i, more=True):
                rows = act.value_load(r.cnt[0:1, bass.ds(n, 1)], min_val=0, max_val=TOK)

                def silu(rows):
                    at = 0 if rows == P else H
                    act.wait_ge(gu_used, n + 1)
                    act.wait_ge(h_done, n + 1)
                    nc.scalar.activation(sg[at:at + rows, :], gps[0:rows, :], ACT.Silu).then_inc(sg_done, 1)

                def rows_out(rows):
                    act.wait_ge(d_used, n + 1)
                    act.wait_ge(y_free[q], i * 16 + 16)
                    nc.scalar.copy(y[q][0:rows, 0:512], yps[0][0:rows, :]).then_inc(y_act, 1)
                    act.wait_ge(y_act, n + 2)
                    act.wait_ge(y_dve, n + 2)
                    act.dma_start(ys[bass.ds(n, 1), 0:rows].rearrange("o p n -> (o p) n"), y[q][0:rows, :]).then_inc(y_free[q], 16)

                with act.If(rows > H):
                    silu(P)
                with act.Else():
                    silu(H)
                if more:
                    x_copy(n + 1, (q + 1) % S)
                with act.If(rows > H):
                    rows_out(P)
                with act.Else():
                    rows_out(H)

            x_copy(0, 0)
            with act.Fori(0, LOOPS) as i:
                for q in range(S):
                    turn(i * S + q, q, i)
            for n in range(LOOPS * S, E):
                turn(n, n % S, n // S, more=n + 1 < E)
            for q in range(S):
                act.wait_ge(y_free[q], 16 * (len(range(q, E, S)) + 1))

        @block.vector
        def _(dve):
            dve.sem_inc(xt_dve, 1)
            dve.sem_inc(h_done, 1)
            dve.sem_inc(ht_done, 1)
            dve.sem_inc(y_dve, 1)

            def x_copy(n, q):
                dve.wait_ge(xtr, n + 1)
                dve.sem_inc(xg_free, 1)
                nc.vector.tensor_copy(xT[:, 4:8, :], xps[1][:]).then_inc(xt_dve, 1)

            def turn(n, q, i, more=True):
                rows = dve.value_load(r.cnt[0:1, bass.ds(n, 1)], min_val=0, max_val=TOK)

                def hidden(rows):
                    at = 0 if rows == P else H
                    dve.wait_ge(gu_used, n + 1)
                    dve.wait_ge(sg_done, n + 1)
                    nc.vector.tensor_tensor(h[at:at + rows, :], sg[at:at + rows, :], ups[at:at + rows, :],
                                            ALU.mult).then_inc(h_done, 1)

                def rows_out(rows):
                    at = 0 if rows == P else H
                    dve.wait_ge(htr, n + 1)
                    nc.vector.tensor_copy(hT[:, :, 0:rows], hps[:, :, 0:rows]).then_inc(ht_done, 1)
                    dve.wait_ge(d_used, n + 1)
                    dve.wait_ge(y_free[q], i * 16 + 16)
                    nc.vector.tensor_copy(y[q][0:rows, 512:1024], yps[1][at:at + rows, :]).then_inc(y_dve, 1)

                with dve.If(rows > H):
                    hidden(P)
                with dve.Else():
                    hidden(H)
                if more:
                    x_copy(n + 1, (q + 1) % S)
                with dve.If(rows > H):
                    rows_out(P)
                with dve.Else():
                    rows_out(H)

            x_copy(0, 0)
            with dve.Fori(0, LOOPS) as i:
                for q in range(S):
                    turn(i * S + q, q, i)
            for n in range(LOOPS * S, E):
                turn(n, n % S, n // S, more=n + 1 < E)


def further_blocks(nc, c, a, layer, t0, r):
    T = NT - t0
    OVB = T * 2 - 1
    with Scope(nc, f"more{layer}") as s:
        wg, wu = s.sb("wg", [P, KD, HID]), s.sb("wu", [P, KD, HID])
        wd = s.sb("wd", [P, HT_N, DM])
        idx = s.sb("idx", [P, 1], I32)
        spare = s.sb("spare", [1, 1])
        xg = s.sb("xg", [P, DM])
        xT = s.sb("xT", [P, KD, P])
        sg, h = s.sb("sg", [P, HID]), s.sb("h", [P, HID])
        hT = s.sb("hT", [P, HT_N, P])
        y = s.sb("y", [P, DM])
        xps = s.ps("xps", [P, KD, P])
        gps, ups = s.ps("gps", [P, HID]), s.ps("ups", [P, HID])
        hps = s.ps("hps", [P, HT_N, P])
        yps = s.ps("yps", [P, DM])
        w_ready, idx_done, x_ready, xtr, xt, gu, sg_done, h_done, htr, ht, down, y_done, stored = (
            s.sem(n) for n in ("w_ready", "idx_done", "x_ready", "xtr", "xt", "gu", "sg_done", "h_done",
                               "htr", "ht", "down", "y_done", "stored"))
        block = s.block()
        wg_e = a["moe_w_gate"][layer].rearrange("e (k p) n -> e p k n", p=P)
        wu_e = a["moe_w_up"][layer].rearrange("e (k p) n -> e p k n", p=P)
        wd_e = a["moe_w_down"][layer].rearrange("e (k p) n -> e p k n", p=P)
        ys = c.ys.rearrange("(b p) n -> b p n", p=P)

        def asked(eng):
            return eng.value_load(r.more[0:1, OVB:OVB + 1], min_val=0, max_val=OVB)

        @block.sync
        def _(sp):
            num = asked(sp)
            with sp.If(num > 0):
                with sp.Fori(0, OVB) as b:
                    with sp.If(b < num):
                        e = sp.value_load(r.more[0:1, bass.ds(b, 1)], min_val=0, max_val=E - 1)
                        sp.dma_start(wg[:], wg_e[bass.ds(e, 1)].rearrange("o p k n -> (o p) k n")).then_inc(w_ready, 16)
                        sp.dma_start(wu[:], wu_e[bass.ds(e, 1)].rearrange("o p k n -> (o p) k n")).then_inc(w_ready, 16)
                        sp.dma_start(wd[:], wd_e[bass.ds(e, 1)].rearrange("o p k n -> (o p) k n")).then_inc(w_ready, 16)
                        sp.wait_ge(y_done, b + 1)
                        sp.dma_start(ys[bass.ds(b + E, 1)].rearrange("o p n -> (o p) n"), y[:]).then_inc(stored, 16)

        @block.gpsimd
        def _(pool):
            num = asked(pool)
            nc.gpsimd.memset(spare[:], 0.0)
            with pool.If(num > 0):
                with pool.Fori(0, OVB) as b:
                    with pool.If(b < num):
                        nc.gpsimd.tensor_copy(idx[:], r.tok[:, bass.ds(b + E, 1)]).then_inc(idx_done, 1)
                        pool.wait_ge(idx_done, b + 1)
                        nc.gpsimd.tensor_tensor(spare[:], spare[:], spare[:], ALU.add)
                        nc.gpsimd.indirect_dma_start(xg[:], None, c.h_rows[:, :],
                                                     bass.IndirectOffsetOnAxis(idx[:], 0)).then_inc(x_ready, 16)
                        pool.wait_ge(stored, b * 16 + 16)

        @block.tensor
        def _(pe):
            num = asked(pe)
            with pe.If(num > 0):
                with pe.Fori(0, OVB) as b:
                    with pe.If(b < num):
                        pe.wait_ge(x_ready, b * 16 + 16)
                        for k in range(KD):
                            last = nc.tensor.transpose(xps[:, k, :], xg[:, k * P:(k + 1) * P], c.ident[:])
                        last.then_inc(xtr, 1)
                        pe.wait_ge(w_ready, b * 48 + 48)
                        pe.wait_ge(xt, b + 1)
                        for k in range(KD):
                            nc.tensor.matmul(gps[:], xT[:, k, :], wg[:, k, :], start=(k == 0), stop=(k == KD - 1))
                        for k in range(KD):
                            last = nc.tensor.matmul(ups[:], xT[:, k, :], wu[:, k, :], start=(k == 0), stop=(k == KD - 1))
                        last.then_inc(gu, 1)
                        pe.wait_ge(h_done, b + 1)
                        for k in range(HT_N):
                            last = nc.tensor.transpose(hps[:, k, :], h[:, k * P:(k + 1) * P], c.ident[:])
                        last.then_inc(htr, 1)
                        pe.wait_ge(ht, b + 1)
                        for half in range(2):
                            for k in range(HT_N):
                                last = nc.tensor.matmul(yps[:, half * 512:(half + 1) * 512], hT[:, k, :],
                                                        wd[:, k, half * 512:(half + 1) * 512],
                                                        start=(k == 0), stop=(k == HT_N - 1))
                        last.then_inc(down, 1)

        @block.scalar
        def _(act):
            num = asked(act)
            with act.If(num > 0):
                with act.Fori(0, OVB) as b:
                    with act.If(b < num):
                        act.wait_ge(gu, b + 1)
                        nc.scalar.activation(sg[:], gps[:], ACT.Silu).then_inc(sg_done, 1)

        @block.vector
        def _(dve):
            num = asked(dve)
            with dve.If(num > 0):
                with dve.Fori(0, OVB) as b:
                    with dve.If(b < num):
                        dve.wait_ge(xtr, b + 1)
                        nc.vector.tensor_copy(xT[:], xps[:]).then_inc(xt, 1)
                        dve.wait_ge(sg_done, b + 1)
                        nc.vector.tensor_tensor(h[:], sg[:], ups[:], ALU.mult).then_inc(h_done, 1)
                        dve.wait_ge(htr, b + 1)
                        nc.vector.tensor_copy(hT[:], hps[:]).then_inc(ht, 1)
                        dve.wait_ge(down, b + 1)
                        nc.vector.tensor_copy(y[:], yps[:]).then_inc(y_done, 1)


def combine(nc, c, a, layer, t0, r, prefetch=None):
    T = NT - t0
    with Scope(nc, f"comb{layer}") as s:
        YB = 3
        y = [[s.sb(f"y{b}{k}", [P, DM]) for k in range(2)] for b in range(YB)]
        got = [s.sem(f"got{b}") for b in range(YB)]
        weighed, x_done, chain = s.sem("weighed"), s.sem("x_done"), s.sem("chain")
        gate = s.sb("gate", [P, 1 if t0 else 2, DM])
        gate_ready = s.sem("gate_ready")
        gs, ex = s.sb("gs", [P, T]), s.sb("ex", [P, T])
        exp_done, w_done = s.sem("exp_done"), s.sem("w_done")
        tile_done = lambda eng, t: eng.wait_ge(x_done, t + 1)
        if layer + 1 < DEPTH:
            norm = NormModulate(nc, c, a, s, layer + 1, 0, t0, tile_done, pairs=2)
        else:
            norm = FinalNorm(nc, c, a, s, t0, tile_done)
        block = s.block()

        @block.sync
        def _(sp):
            load_gates(sp, c, gate, gate_ready, layer, 1, 1 if t0 else 2)
            sp.wait_ge(got[0], 32)
            norm.load(sp)
            if prefetch:
                prefetch(sp)
            norm.store(sp)

        @block.gpsimd
        def _(pool):
            for t in range(T + 1):
                if t < T:
                    if t >= YB:
                        pool.wait_ge(x_done, t - YB + 1)
                    for k in range(2):
                        nc.gpsimd.indirect_dma_start(y[t % YB][k][:], None, c.ys[:, :],
                                                     bass.IndirectOffsetOnAxis(r.slot[:, k * T + t:k * T + t + 1], 0)
                                                     ).then_inc(got[t % YB], 16)
                if t >= 3:
                    norm.shift(pool, t - 3)
            for t in range(T - 2, T):
                norm.shift(pool, t)

        @block.scalar
        def _(act):
            nc.scalar.activation(r.gshift[:, 0:T, :], r.gshift[:, 0:T, :], ACT.Exp).then_inc(exp_done, 1)
            nc.scalar.activation(ex[:], r.eshift[:, 0:T], ACT.Exp).then_inc(exp_done, 1)
            act.wait_ge(w_done, 1)
            for t in range(T + 2):
                if t < T:
                    act.wait_ge(got[t % YB], 32 * (t // YB + 1))
                    nc.scalar.mul(y[t % YB][0][:], y[t % YB][0][:], r.w[:, 0, t:t + 1]).then_inc(weighed, 1)
                if 1 <= t <= T:
                    norm.square(act, t - 1)
                if t >= 2:
                    norm.first_half(act, t - 2)
                    norm.second_half(act, t - 2, nc.scalar.copy)

        @block.vector
        def _(dve):
            link = Chain(dve, chain)
            V = nc.vector
            dve.wait_ge(exp_done, 2)
            link(V.tensor_reduce(gs[:], r.gshift[:, 0:T, :], AX, ALU.add))
            link(V.scalar_tensor_tensor(out=gs[:], in0=ex[:], scalar=1.0, in1=gs[:], op0=ALU.add, op1=ALU.mult))
            link(V.reciprocal(r.w[:, 0, 0:T], gs[:]))
            V.tensor_tensor(r.w[:, 1, 0:T], r.w[:, 0, 0:T], ex[:], ALU.mult).then_inc(w_done, 1)
            dve.wait_ge(w_done, 1)
            dve.wait_ge(gate_ready, 16 if t0 else 32)
            for t in range(T + 2):
                if t < T:
                    st = 1 if t0 + t < CT else 0
                    y0, y1 = y[t % YB]
                    dve.wait_ge(weighed, t + 1)
                    link(V.scalar_tensor_tensor(out=y0[:], in0=y1[:], scalar=r.w[:, 1, t:t + 1], in1=y0[:],
                                                op0=ALU.mult, op1=ALU.add))
                    link(V.tensor_tensor(y0[:], y0[:], gate[:, st, :], ALU.mult))
                    V.tensor_tensor(c.X[:, t0 + t, :], c.X[:, t0 + t, :], y0[:], ALU.add).then_inc(x_done, 1)
                if t == 1:
                    norm.prepare(dve)
                if 1 <= t <= T:
                    norm.scale(dve, link, t - 1)

        @block.tensor
        def _(pe):
            for t in range(T):
                norm.transpose(pe, t)


def routed(s):
    r = Box()
    r.slot = s.sb("slot", [P, 2 * NT], I32)
    r.tok = s.sb("tok", [P, E + 2 * NT], I32)
    r.more = s.sb("more", [P, 2 * NT], I32)
    r.cnt = s.sb("cnt", [P, E], I32)
    r.gshift = s.sb("gshift", [P, NT, G])
    r.eshift = s.sb("eshift", [P, NT])
    r.w = s.sb("w", [P, 2, NT])
    return r


def moe_rows(nc, c, a, layer, t0, r):
    with Scope(nc, f"moew{layer}") as s:
        w = expert_weights(s, 3)

        def first(sp):
            for e in range(len(w.g) - 1):
                load_gate_up(sp, a, layer, w, e, e)
                load_down(sp, a, layer, w, e, e)

        routing(nc, c, a, layer, t0, r, first)
        experts(nc, c, a, layer, t0, r, w)
    further_blocks(nc, c, a, layer, t0, r)


class Box:
    pass


class FinalNorm(RowNorm):

    def __init__(self, nc, c, a, s, t0, x_ready):
        super().__init__(nc, c, a, s, t0, x_ready, s.sb)
        self.o = s.sb("o", [P, self.T, DM])
        self.o_done, self.stored = s.sem("o_done"), s.sem("stored")

    def load(self, sp):
        sp.dma_start(self.g[:], self.a["final_norm_g"].rearrange("(o n) -> o n", o=1)
                     .to_broadcast([P, DM])).then_inc(self.g_ready, 16)

    def store(self, sp):
        for t in range(self.T):
            sp.wait_ge(self.o_done, t + 1)
            sp.dma_start(self.c.out[0, t * P:(t + 1) * P, :], self.o[:, t, :]).then_inc(self.stored, 16)
        sp.wait_ge(self.stored, 16 * self.T)

    def prepare(self, dve):
        self.nc.vector.memset(self.eps[:], EPS).then_inc(self.eps_set, 1)
        dve.wait_ge(self.g_ready, 16)

    def scale(self, dve, link, t):
        self.inverse(dve, link, t)
        self.nc.vector.scalar_tensor_tensor(out=self.o[:, t, :], in0=self.c.X[:, self.t0 + t, :],
                                            scalar=self.rstd[:, t:t + 1], in1=self.g[:],
                                            op0=ALU.mult, op1=ALU.mult).then_inc(self.o_done, 1)

    def shift(self, pool, t):
        pass

    transpose = first_half = shift

    def second_half(self, eng, t, copy):
        pass


def backbone(nc, a, out):
    c = Box()
    c.out = out
    c.mods = nc.dram_tensor("mods", (2, DEPTH, 6 * DM), F32, kind="Internal").ap()
    c.h_rows = nc.dram_tensor("h_rows", (TOK, DM), F32, kind="Internal").ap()
    slots = (E + 2 * NT - 1) * P
    c.ys = nc.dram_tensor("ys", (slots, DM), F32, kind="Internal").ap()
    with Scope(nc, "all") as s:
        c.X = s.sb("X", [P, NT, DM])
        c.hT = s.sb("hT", [P, KD, TOK])
        c.lg = s.sb("lg", [P, NT, ROUTES])
        c.ident, c.ones, c.before = (s.sb(n, [P, P]) for n in ("ident", "ones", "before"))
        c.x_ready = s.sem("x_ready")
        constants(nc, c)
        with Scope(nc, "tables") as s1:
            k = Box()
            k.sp = s1.sb("sp", [P, 2 * RH + 2 * LT])
            k.lg = s1.sb("lg", [P, 2 * RH])
            k.zeta, k.dec = s1.sb("zeta", [P, 2, RH]), s1.sb("dec", [P, 2, RH])
            k.XI = s1.sb("XI", [P, 2, RH, P])
            k.DT = s1.sb("DT", [P, RH, P])
            adaln(nc, c, a, k)
            ab_layer(nc, c, a, k)
        r = routed(s)
        moe_rows(nc, c, a, 0, 0, r)
        with Scope(nc, "mla") as s1:
            k = mla_buffers(s1)
            combine(nc, c, a, 0, 0, r, lambda sp: load_w_in(sp, a, k))
            mla_layer(nc, c, a, k)
        moe_rows(nc, c, a, 1, CT, r)
        combine(nc, c, a, 1, CT, r)


_INS = ['x', 'c', 'ctx', 'c_ctx', 'ada_w', 'ada_b', 'norm_g', 'ab_w_in', 'ab_w_out', 'ret_decay_logit',
        'lru_conv_w', 'lru_conv_b', 'lru_gate_w', 'lru_gate_b', 'lru_lambda', 'mla_w_in', 'mla_q_norm_g',
        'mla_kv_norm_g', 'mla_w_uq', 'mla_w_ukv', 'mla_w_out', 'moe_group_w', 'moe_group_b', 'moe_expert_w',
        'moe_expert_b', 'moe_w_gate', 'moe_w_up', 'moe_w_down', 'final_norm_g']


def rope_tables():
    t = np.arange(SEQ, dtype=np.float32)
    inv1 = np.float32(ROPE_BASE) ** (-np.arange(0, RD, 2, dtype=np.float32) / np.float32(RD))
    ang1 = t[:, None] * inv1[None, :]
    ax = ROPE // 2
    inv2 = np.float32(ROPE_BASE) ** (-np.arange(0, ax, 2, dtype=np.float32) / np.float32(ax))
    r_pos = np.repeat(np.arange(SEQ // GRID_W, dtype=np.float32), GRID_W)
    c_pos = np.tile(np.arange(GRID_W, dtype=np.float32), SEQ // GRID_W)
    ang2 = np.concatenate([r_pos[:, None] * inv2[None, :], c_pos[:, None] * inv2[None, :]], axis=-1)

    def laid(ang):
        both = np.stack([np.cos(ang), np.sin(ang)]).astype(np.float32)
        return np.ascontiguousarray(both.reshape(2, SEQ // P, P, -1).transpose(2, 0, 1, 3))

    return {"ret_cs": laid(ang1), "mla_cs": laid(ang2)}


def kernel(**inputs):
    import concourse.bacc as bacc
    from concourse.bass_utils import run_bass_kernel_spmd as run

    nc = bacc.Bacc("TRN2", target_bir_lowering=False, num_devices=1)
    arrays, args = {}, {}
    for name in _INS:
        v = np.ascontiguousarray(inputs[name])
        arrays[f"in_{name}"] = v
        args[name] = nc.dram_tensor(f"in_{name}", v.shape, mybir.dt.from_np(v.dtype), kind="ExternalInput").ap()
    for name, v in rope_tables().items():
        arrays[f"in_{name}"] = v
        args[name] = nc.dram_tensor(f"in_{name}", v.shape, F32, kind="ExternalInput").ap()
    out = nc.dram_tensor("out", (1, SEQ, DM), F32, kind="ExternalOutput").ap()
    backbone(nc, args, out)
    return run(nc, [arrays], core_ids=[0]).results[0]["out"]
```
